# Optimizing a Trainium2 kernel written in Bass

```python
import math
import jax
import jax.numpy as jnp
from jax import lax
import numpy as np

D_MODEL = 1024
BATCH = 1
SEQ = 256
DEPTH = 2

A_HEADS = 4
A_DIM = 64
B_GROUPS = 4
B_GROUP_DIM = 128
B_CHUNK = 128
C_HEADS = 4
C_DIM = 128
C_IDX_HEADS = 8
C_IDX_DIM = 64
C_TOPK_MAX = 256
MEM_LEN = 256
M_HEADS = 4
M_DIM = 128
P_HEADS = 8
P_QDIM = 256
P_NKEYS = 128
P_EXPERTS = P_NKEYS * P_NKEYS
P_TOPK = 16
P_CHUNK = 128
REL_BUCKETS = 32
REL_MAX_DIST = 128
N_BIAS_HEADS = A_HEADS + C_HEADS
Q_BLOCK = 128
N_BRANCH = 3
EPS = 1e-6
BRANCH_W = 512

SPLITS = (
    A_HEADS * 2 * A_DIM,
    A_HEADS * 2 * A_DIM,
    A_HEADS * 2 * A_DIM,
    B_GROUPS * B_GROUP_DIM,
    B_GROUPS * B_GROUP_DIM,
    C_HEADS * C_DIM,
    C_DIM,
    C_DIM,
    C_IDX_HEADS * C_IDX_DIM,
    C_IDX_DIM,
    C_IDX_HEADS,
    N_BRANCH * D_MODEL,
)
D_IN = sum(SPLITS)
SPLIT_POINTS = tuple(int(v) for v in np.cumsum(SPLITS)[:-1])

kernel_name = "hybrid_diffattn_gmlp_dsa_peer"

def rmsnorm(x, g):
    xf = x.astype(jnp.float32)
    y = xf * lax.rsqrt(jnp.mean(xf * xf, axis=-1, keepdims=True) + EPS)
    return (y * g.astype(jnp.float32)).astype(x.dtype)

def t5_bucket(dist):
    n = jnp.maximum(dist, 0)
    max_exact = REL_BUCKETS // 2
    nf = jnp.maximum(n, 1).astype(jnp.float32)
    large = max_exact + (jnp.log(nf / max_exact) / math.log(REL_MAX_DIST / max_exact)
                         * (REL_BUCKETS - max_exact)).astype(jnp.int32)
    large = jnp.minimum(large, REL_BUCKETS - 1)
    return jnp.where(n < max_exact, n, large)

def diff_attention(qa, ka, va, lam, rel_bias):
    bsz, seq = qa.shape[0], qa.shape[1]
    nb = seq // Q_BLOCK
    scale = A_DIM ** -0.5
    q_blocks = qa.reshape(bsz, nb, Q_BLOCK, A_HEADS, 2, A_DIM).swapaxes(0, 1)
    starts = jnp.arange(nb, dtype=jnp.int32) * Q_BLOCK
    k_pos = jnp.arange(seq, dtype=jnp.int32)

    def block(args):
        qb, start = args
        q_pos = start + jnp.arange(Q_BLOCK, dtype=jnp.int32)
        dist = q_pos[:, None] - k_pos[None, :]
        bias = rel_bias[t5_bucket(dist)][..., :A_HEADS]
        logits = jnp.einsum('bqhmd,bkhmd->bhmqk', qb, ka).astype(jnp.float32) * scale
        logits = logits + jnp.transpose(bias, (2, 0, 1))[None, :, None].astype(jnp.float32)
        logits = jnp.where(dist >= 0, logits, -jnp.inf)
        p = jax.nn.softmax(logits, axis=-1)
        p_diff = (p[:, :, 0] - lam * p[:, :, 1]).astype(va.dtype)
        return jnp.einsum('bhqk,bkhd->bqhd', p_diff, va)

    out = lax.map(block, (q_blocks, starts))
    return out.swapaxes(0, 1).reshape(bsz, seq, A_HEADS, 2 * A_DIM)

def spatial_gating(zu, zv, v_gain, w_s, b_s):
    bsz, seq = zu.shape[0], zu.shape[1]
    nc = seq // B_CHUNK
    u = jax.nn.gelu(zu, approximate=False)
    v = jax.nn.gelu(zv, approximate=False).reshape(bsz, seq, B_GROUPS, B_GROUP_DIM)
    v = rmsnorm(v, v_gain.reshape(B_GROUPS, B_GROUP_DIM))
    v = v.reshape(bsz, nc, B_CHUNK, B_GROUPS, B_GROUP_DIM)
    w = w_s * jnp.tril(jnp.ones((B_CHUNK, B_CHUNK), dtype=w_s.dtype))
    sv = jnp.einsum('gts,bcsgd->bctgd', w, v) + b_s.T[:, :, None]
    return u * sv.reshape(bsz, seq, B_GROUPS * B_GROUP_DIM)

def dsa_attention(cq, ck, cv, iq, ik, iw, rel_bias, k_sel):
    bsz, seq = cq.shape[0], cq.shape[1]
    nb = seq // Q_BLOCK
    scale = C_DIM ** -0.5
    to_blocks = lambda a: a.reshape((bsz, nb, Q_BLOCK) + a.shape[2:]).swapaxes(0, 1)
    starts = jnp.arange(nb, dtype=jnp.int32) * Q_BLOCK
    k_pos = jnp.arange(seq, dtype=jnp.int32)
    gather = jax.vmap(lambda a, i: a[i])

    def block(args):
        qb, iqb, iwb, start = args
        q_pos = start + jnp.arange(Q_BLOCK, dtype=jnp.int32)
        dist = q_pos[:, None] - k_pos[None, :]
        score = jnp.einsum('bqhk,bqh->bqk',
                           jax.nn.relu(jnp.einsum('bqhd,bkd->bqhk', iqb, ik)),
                           iwb).astype(jnp.float32)
        score = jnp.where(dist >= 0, score, -jnp.inf)
        _, sel = lax.top_k(score, k_sel)
        k_g = gather(ck, sel)
        v_g = gather(cv, sel)
        dsel = q_pos[None, :, None] - sel
        bias = rel_bias[t5_bucket(dsel)][..., A_HEADS:]
        logits = jnp.einsum('bqhd,bqkd->bqhk', qb, k_g).astype(jnp.float32) * scale
        logits = logits + jnp.swapaxes(bias, -1, -2).astype(jnp.float32)
        logits = jnp.where(dsel[:, :, None, :] >= 0, logits, -jnp.inf)
        p = jax.nn.softmax(logits, axis=-1).astype(cv.dtype)
        return jnp.einsum('bqhk,bqkd->bqhd', p, v_g)

    out = lax.map(block, (to_blocks(cq), to_blocks(iq), to_blocks(iw), starts))
    return out.swapaxes(0, 1).reshape(bsz, seq, C_HEADS * C_DIM)

def mixer_block(xn, rel_bias, w_in, a_q_gain, a_k_gain, a_lq1, a_lk1, a_lq2, a_lk2,
                a_subln_gain, lam_init, b_v_gain, b_w_s, b_b_s, c_q_gain, c_k_gain,
                w_br_a, w_br_b, w_br_c, w_out):
    bsz, seq, _ = xn.shape
    h = xn @ w_in
    (qa, ka, va, zu, zv, cq, ck, cv, iq, ik, iw, gts) = jnp.split(h, SPLIT_POINTS, axis=-1)
    qa = rmsnorm(qa.reshape(bsz, seq, A_HEADS, 2, A_DIM), a_q_gain)
    ka = rmsnorm(ka.reshape(bsz, seq, A_HEADS, 2, A_DIM), a_k_gain)
    va = va.reshape(bsz, seq, A_HEADS, 2 * A_DIM)
    lam = (jnp.exp(jnp.sum(a_lq1.astype(jnp.float32) * a_lk1.astype(jnp.float32)))
           - jnp.exp(jnp.sum(a_lq2.astype(jnp.float32) * a_lk2.astype(jnp.float32))) + lam_init)
    ya = diff_attention(qa, ka, va, lam, rel_bias)
    ya = (rmsnorm(ya, a_subln_gain) * (1.0 - lam_init)).reshape(bsz, seq, BRANCH_W)
    yb = spatial_gating(zu, zv, b_v_gain, b_w_s, b_b_s)
    k_sel = min(C_TOPK_MAX, seq // 4)
    cq = rmsnorm(cq.reshape(bsz, seq, C_HEADS, C_DIM), c_q_gain)
    ck = rmsnorm(ck, c_k_gain)
    iq = iq.reshape(bsz, seq, C_IDX_HEADS, C_IDX_DIM)
    yc = dsa_attention(cq, ck, cv, iq, ik, iw, rel_bias, k_sel)
    g = jax.nn.sigmoid(gts).reshape(bsz, seq, N_BRANCH, D_MODEL)
    merged = (g[:, :, 0] * (ya @ w_br_a) + g[:, :, 1] * (yb @ w_br_b)
              + g[:, :, 2] * (yc @ w_br_c))
    return merged @ w_out

def memory_xattn(xn, memn, wq, wkv, q_gain, k_gain, wo):
    bsz, seq, _ = xn.shape
    mlen = memn.shape[1]
    q = rmsnorm((xn @ wq).reshape(bsz, seq, M_HEADS, M_DIM), q_gain)
    k, v = jnp.split(memn @ wkv, 2, axis=-1)
    k = rmsnorm(k.reshape(bsz, mlen, M_HEADS, M_DIM), k_gain)
    v = v.reshape(bsz, mlen, M_HEADS, M_DIM)
    logits = jnp.einsum('bqhd,bkhd->bhqk', q, k).astype(jnp.float32) * (M_DIM ** -0.5)
    p = jax.nn.softmax(logits, axis=-1).astype(v.dtype)
    o = jnp.einsum('bhqk,bkhd->bqhd', p, v).reshape(bsz, seq, M_HEADS * M_DIM)
    return o @ wo

def peer(xn, wq, sk1, sk2, u_tab, v_tab):
    bsz, seq, dm = xn.shape
    q = (xn @ wq).reshape(bsz, seq, P_HEADS, 2, P_QDIM // 2)
    s1 = jnp.einsum('bshd,nd->bshn', q[..., 0, :], sk1).astype(jnp.float32)
    s2 = jnp.einsum('bshd,nd->bshn', q[..., 1, :], sk2).astype(jnp.float32)
    v1, i1 = lax.top_k(s1, P_TOPK)
    v2, i2 = lax.top_k(s2, P_TOPK)
    cand = (v1[..., :, None] + v2[..., None, :]).reshape(bsz, seq, P_HEADS, P_TOPK * P_TOPK)
    cs, ci = lax.top_k(cand, P_TOPK)
    e1 = jnp.take_along_axis(i1, ci // P_TOPK, axis=-1)
    e2 = jnp.take_along_axis(i2, ci % P_TOPK, axis=-1)
    expert = e1 * P_NKEYS + e2
    gate = jax.nn.softmax(cs, axis=-1).astype(xn.dtype)
    n_chunk = (bsz * seq) // P_CHUNK
    xc = xn.reshape(n_chunk, P_CHUNK, dm)
    ec = expert.reshape(n_chunk, P_CHUNK, P_HEADS, P_TOPK)
    gc = gate.reshape(n_chunk, P_CHUNK, P_HEADS, P_TOPK)

    def chunk(args):
        xt, et, gt = args
        act = jax.nn.gelu(jnp.einsum('td,thkd->thk', xt, u_tab[et]), approximate=False)
        return jnp.einsum('thk,thkd->td', gt * act, v_tab[et])

    return lax.map(chunk, (xc, ec, gc)).reshape(bsz, seq, dm)

def setup_inputs(seed: int = 0) -> dict:
    key = jax.random.key(seed)
    ks = iter(jax.random.split(key, 48))
    L, D = DEPTH, D_MODEL
    nrm = lambda shape, s: jax.random.normal(next(ks), shape, jnp.float32) * s
    gain = lambda shape: 1.0 + 0.05 * jax.random.normal(next(ks), shape, jnp.float32)
    return {
        "x": nrm((BATCH, SEQ, D), 1.0),
        "mem": nrm((BATCH, MEM_LEN, D), 1.0),
        "rel_bias": nrm((REL_BUCKETS, N_BIAS_HEADS), 0.5),
        "norm_mix": gain((L, D)),
        "w_in": nrm((L, D, D_IN), D ** -0.5),
        "a_q_gain": gain((L, A_DIM)),
        "a_k_gain": gain((L, A_DIM)),
        "a_lq1": nrm((L, A_DIM), 0.1),
        "a_lk1": nrm((L, A_DIM), 0.1),
        "a_lq2": nrm((L, A_DIM), 0.1),
        "a_lk2": nrm((L, A_DIM), 0.1),
        "a_subln_gain": gain((L, 2 * A_DIM)),
        "b_v_gain": gain((L, B_GROUPS * B_GROUP_DIM)),
        "b_w_s": nrm((L, B_GROUPS, B_CHUNK, B_CHUNK), 0.5 * B_CHUNK ** -0.5),
        "b_b_s": 1.0 + nrm((L, B_GROUPS, B_CHUNK), 0.1),
        "c_q_gain": gain((L, C_DIM)),
        "c_k_gain": gain((L, C_DIM)),
        "w_br_a": nrm((L, BRANCH_W, D), BRANCH_W ** -0.5),
        "w_br_b": nrm((L, BRANCH_W, D), BRANCH_W ** -0.5),
        "w_br_c": nrm((L, BRANCH_W, D), BRANCH_W ** -0.5),
        "w_mix_out": nrm((L, D, D), D ** -0.5),
        "norm_mem": gain((L, D)),
        "norm_memsrc": gain((L, D)),
        "m_wq": nrm((L, D, M_HEADS * M_DIM), D ** -0.5),
        "m_wkv": nrm((L, D, 2 * M_HEADS * M_DIM), D ** -0.5),
        "m_q_gain": gain((L, M_DIM)),
        "m_k_gain": gain((L, M_DIM)),
        "m_wo": nrm((L, M_HEADS * M_DIM, D), (M_HEADS * M_DIM) ** -0.5),
        "norm_peer": gain((L, D)),
        "p_wq": nrm((L, D, P_HEADS * P_QDIM), D ** -0.5),
        "p_subkey1": nrm((L, P_NKEYS, P_QDIM // 2), (P_QDIM // 2) ** -0.5),
        "p_subkey2": nrm((L, P_NKEYS, P_QDIM // 2), (P_QDIM // 2) ** -0.5),
        "p_u": nrm((L, P_EXPERTS, D), D ** -0.5),
        "p_v": nrm((L, P_EXPERTS, D), P_HEADS ** -0.5),
    }

def reference(x, mem, rel_bias, norm_mix, w_in, a_q_gain, a_k_gain, a_lq1, a_lk1, a_lq2,
              a_lk2, a_subln_gain, b_v_gain, b_w_s, b_b_s, c_q_gain, c_k_gain, w_br_a,
              w_br_b, w_br_c, w_mix_out, norm_mem, norm_memsrc, m_wq, m_wkv, m_q_gain,
              m_k_gain, m_wo, norm_peer, p_wq, p_subkey1, p_subkey2, p_u, p_v):
    for l in range(DEPTH):
        lam_init = 0.8 - 0.6 * math.exp(-0.3 * l)
        x = x + mixer_block(rmsnorm(x, norm_mix[l]), rel_bias, w_in[l], a_q_gain[l],
                            a_k_gain[l], a_lq1[l], a_lk1[l], a_lq2[l], a_lk2[l],
                            a_subln_gain[l], lam_init, b_v_gain[l], b_w_s[l], b_b_s[l],
                            c_q_gain[l], c_k_gain[l], w_br_a[l], w_br_b[l], w_br_c[l],
                            w_mix_out[l])
        x = x + memory_xattn(rmsnorm(x, norm_mem[l]), rmsnorm(mem, norm_memsrc[l]), m_wq[l],
                             m_wkv[l], m_q_gain[l], m_k_gain[l], m_wo[l])
        x = x + peer(rmsnorm(x, norm_peer[l]), p_wq[l], p_subkey1[l], p_subkey2[l],
                     p_u[l], p_v[l])
    return x


_drawn_inputs = setup_inputs


def setup_inputs(seed=0):
    import zlib

    import numpy as np

    out = dict(_drawn_inputs(seed))
    spreads = {}
    factors = {}
    for name, (base, spread) in spreads.items():
        noise = np.random.default_rng([zlib.crc32(name.encode()), seed]).standard_normal(out[name].shape)
        drawn = base * np.exp(spread * noise) if base else spread * noise
        out[name] = jnp.asarray(drawn.astype(out[name].dtype))
    for name, factor in factors.items():
        out[name] = (out[name] * factor).astype(out[name].dtype)
    return out
```

```python
import math
from contextlib import ExitStack

import concourse.bass as bass
from concourse import mybir

F32 = mybir.dt.float32
U32 = mybir.dt.uint32
BF16 = mybir.dt.bfloat16
ACT = mybir.ActivationFunctionType
ALU = mybir.AluOpType
AX = mybir.AxisListType.X

P = 128
D = 1024
SEQ = 256
NT = SEQ // P
DEPTH = 2
KC = D // P
AH, AD = 4, 64
CH, CD = 4, 128
IH, ID = 8, 64
MH, MD = 4, 128
BG = 4
TOPK_C = 64
PH, PK, NKEY = 8, 16, 128
BUCKETS, MAXDIST = 32, 128
NHB = AH + CH
EPS = 1e-6
MASK = -1e30
TAKEN = -3e38
RING = 8
STRIP = 3 * P

PARTS = [("g_mix", 8), ("g_mem", 8), ("g_src", 8), ("g_peer", 8), ("aq", 1), ("ak", 1), ("cq", 1),
         ("ck", 1), ("mq", 1), ("mk", 1), ("asub", 1), ("bv", 4), ("ws", BG * P), ("bs", BG * P),
         ("lam", 4 * AD), ("sk", 2 * NKEY)]
PAR = {}
NPAR = 0
for _n, _w in PARTS:
    PAR[_n] = (NPAR, NPAR + _w)
    NPAR += _w

STREAM = [("cs", 4), ("iq", 4), ("ik", 1), ("cq", 4), ("qa", 4), ("ka", 4), ("va", 4), ("zv", 4),
          ("zu", 4), ("gts", 24), ("mk", 4), ("mv", 4), ("br", 12), ("mix_out", 8), ("mq", 4),
          ("mo", 4), ("pq", 16), ("uv", 256)]
NBLK = sum(n for _, n in STREAM)

JOBS = (["nx0", "nx1", "nx2", "nx3", "cs0", "cs1", "iq0", "iq1", "ik", "cq0", "cq1",
         "is00", "is01", "is10", "is11", "is12", "is13", "qa0", "qa1", "ka0", "ka1", "ckT", "cqT0",
         "cqT1", "va0", "va1", "zv0", "zv1", "qT0", "qT1", "kT0", "kT1", "zu0", "zu1"]
        + [f"gt{i}" for i in range(12)] + [f"al{h}{m}" for h in range(AH) for m in range(2)]
        + [f"mx{i}" for i in range(4)] + ["mk0", "mk1", "mv0", "mv1", "sv0", "sv1", "cl0", "cl1",
                                          "cl2"]
        + [f"pT{i}" for i in range(AH)] + ["ay0", "ay1", "ct0", "ct1", "ct2", "cy0", "cy1",
                                           "mkT0", "mkT1", "yT0", "yT1"]
        + [f"m{b}{i}" for i in range(4) for b in "abc"]
        + [f"o{i}" for i in range(4)] + [f"ny{i}" for i in range(4)]
        + ["mq0", "mq1", "mqT0", "mqT1", "ml00", "ml01", "ml10", "ml11", "mp00", "mp01", "mp10",
           "mp11", "mo0", "mo1"]
        + [f"w{i}" for i in range(4)] + [f"nz{i}" for i in range(4)]
        + [f"pq{i}" for i in range(8)] + [f"ps{t}{i}" for t in range(NT) for i in range(4)]
        + ["eT", "gT"])
BANK = {j: n % 8 for n, j in enumerate(JOBS)}
USE = {j: n // 8 + 1 for n, j in enumerate(JOBS)}
USES = [sum(1 for j in JOBS if BANK[j] == b) for b in range(8)]

SQUARES = ["cq", "qa", "ka", "v", "ya", "mk", "mq"]
ROOTS = dict(x=(0, 2, D), m=(2, 2, D), ck=(4, 2, CD), cq=(6, 8, CD), qa=(14, 16, AD),
             ka=(30, 16, AD), v=(46, 8, P), mk=(54, 8, MD), ya=(62, 8, P), y=(70, 2, D),
             mq=(72, 8, MD), z=(80, 2, D))
SQUARES = ["cq", "qa", "ka", "v", "mk", "ya", "mq"]
NSQ = len(SQUARES) * NT

PER_LAYER = dict(
    params=16, bias=32, mem_in=16, sumsq=8, rms_in=len(ROOTS), rms_rt=len(ROOTS), rows=8,
    csq=2, relu_used=6, masked=2, wmask=1, pen=2, sq=NSQ, sq_used=NSQ, vn=2,
    lam_s=1, lam_e=1, a_max=8, a_exp=8, pd=8, yb=4, c_max=2, c_exp=2, c_p=2, merged=4, m_max=2,
    m_p=2, r_sub=2, r_exp=2, route=2, x_peer=1)


def build(nc, x_d, mem_d, relb_d, onehot_d, par_d, w_d, out_d, strip_d):
    ctx = ExitStack()
    with ctx:
        def sb(name, shape, dt=F32):
            return ctx.enter_context(nc.sbuf_tensor(name, shape, dt))

        def sem(name):
            return ctx.enter_context(nc.semaphore(name))

        X = sb("X", [P, NT, D])
        xnT = sb("xnT", [P, KC, SEQ])
        ring = [sb(f"ring{i}", [P, 1024]) for i in range(RING)]
        stat = sb("stat", [P, 82])
        ident = sb("ident", [P, P])
        iota = sb("iota", [P, P])
        credit = sb("credit", [P, 5])
        top8 = sb("top8", [P, 8])
        iota16 = sb("iota16", [P, PK])
        zeros = sb("zeros", [P, 512], BF16)
        ms = sb("ms", [P, NT, D])[:, :, :]
        mkT = sb("mkT", [P, 4, SEQ])[:, :, :]
        loops = sb("loops", [P, 4 * 4 * P + 4 * SEQ + 3 * SEQ])
        loop_buf = lambda at, *d: loops[:, at:at + math.prod(d)]
        oh1 = [loop_buf(i * 512, 512).rearrange("p (q n) -> p q n", q=4) for i in (0, 1)]
        oh2 = [loop_buf(i * 512, 512).rearrange("p (q n) -> p q n", q=4) for i in (2, 3)]
        act_t = [loop_buf(2048 + i * SEQ, SEQ) for i in (0, 1)]
        hid_t = [loop_buf(2048 + i * SEQ, SEQ) for i in (2, 3)]
        e1T, e2T, gateT = [loop_buf(3072 + i * SEQ, SEQ) for i in range(3)]
        arena = sb("arena", [P, SEQ * NKEY])
        G = arena[:, :].rearrange("p (t n) -> p t n", n=NKEY)
        def rooms(whole, at, *shapes):
            out = []
            for shape in shapes:
                n = math.prod(shape)
                assert at + n <= whole.shape[1], (at, n)
                a = whole[:, at:at + n]
                at += n
                names = "abcd"[:len(shape)]
                if len(shape) > 1:
                    a = a.rearrange(f"p ({' '.join(names)}) -> p {' '.join(names)}",
                                    **{c: k for c, k in zip(names, shape)})
                out.append(a)
            return out

        wide = (4, SEQ)
        rows4 = (NT, 512)
        va, vg, c_log1, c_log0 = rooms(loops, 0, rows4, rows4, (4, SEQ), (4, P))
        c_log = [c_log0, c_log1]
        at = 0
        layout = {}

        def put(name, *shapes):
            nonlocal at
            layout[name] = at
            out = rooms(arena, at, *shapes)
            at += sum(math.prod(k) for k in shapes)
            return out

        par, = put("par", (NPAR,))
        bias = put("bias", (NHB, P), (NHB, SEQ))
        xn, = put("xn", (NT, D))
        msT, = rooms(arena, layout["xn"], (KC, SEQ))
        cqn, qan, kan = put("heads", rows4, rows4, rows4)
        mkn, = rooms(arena, layout["heads"], rows4)
        a_pT = rooms(arena, layout["heads"] + 1024, *[(3, P)] * AH)
        merged, mtmp = rooms(arena, layout["heads"], (KC, SEQ), (2, SEQ))
        sq = put("sq", *[(512,)] * 4)
        ckn, cv, iw = put("small", (NT, P), (NT, P), (NT, IH))
        iqT, = put("iqT", wide)
        ybT, = rooms(arena, layout["iqT"], wide)
        ikT, = put("ikT", (SEQ,))
        relu = put("relu", (512,), (512,))
        ycT, = rooms(arena, layout["relu"], wide)
        score, pen = put("score", (NT, SEQ), (NT, SEQ))
        qaT, = put("qaT", wide)
        yaT, = rooms(arena, layout["qaT"], wide)
        kaT, = put("kaT", wide)
        ya, = rooms(arena, layout["kaT"], rows4)
        cqT, ckT = put("cqT", wide, (SEQ,))
        uT, gates = put("gates", wide, (24, SEQ))
        mqn, mqT, moT, m_e0, m_e1, m_pT = rooms(
            arena, layout["gates"], rows4, wide, wide, wide, wide, (2, 4, SEQ))
        m_e = [m_e0, m_e1]
        a_log = put("a_log", (2, SEQ), (2, SEQ))
        c_pT = rooms(arena, layout["a_log"], *[(4, P)] * 3)
        put("rest of c_pT", (512,))
        a_pd = put("a_pd", *[(NT, SEQ)] * AH)
        mv, = put("mv", rows4)
        lamt, lam = put("lam", (2, AD), (4,))
        a_mx, a_sum = put("a_stats", (8, 2), (8, 2))
        c_mx, c_sum, m_mx, m_sum = put("stats", *[(NT, 4)] * 4)
        at = NPAR
        pqT, ps0, ps1 = put("ps", (16, SEQ), (16, P), (16, P))
        ps = [ps0, ps1]
        v16, i16f, cand = put("top", (NT, 16, PK), (NT, 16, PK), (NT, PH, 256))
        cs, gate, halff, eq = put("gate", (NT, PH, PK), (NT, P), (NT, P), (PH * PK, PK))
        etok, rstat = put("etok", (2, NT, P), (NT, 3, PH))
        i16, ci, half = [x.bitcast(U32) for x in put("int", (NT, 16, PK), (NT, PH, PK), (NT, P))]

        bank = [ctx.enter_context(nc.psum_tensor(f"bank{i}", [P, 512], F32)) for i in range(8)]
        bank_full = [sem(f"bank_full{i}") for i in range(8)]
        bank_free = [sem(f"bank_free{i}") for i in range(8)]
        landed = [sem(f"landed{i}") for i in range(RING)]
        S = {n: sem(n) for n in PER_LAYER}
        blocks_used = sem("blocks_used")
        consts, x_in, strip_in = sem("consts"), sem("x_in"), sem("strip_in")
        strip_sb_ready, strip_out, strip_mm = sem("strip_sb"), sem("strip_out"), sem("strip_mm")
        dve_step, act_step, out_done = sem("dve_step"), sem("act_step"), sem("out_done")
        oh_ready, g_full, g_free = sem("oh_ready"), sem("g_full"), sem("g_free")
        a_full, a_done, h_ready = sem("a_full"), sem("a_done"), sem("h_ready")
        y_full = sem("y_full")

        def p_(name, lo=0, hi=None):
            a, b = PAR[name]
            return par[:, a + lo:(b if hi is None else a + hi)]

        def pb(job):
            return bank[BANK[job]]

        def pb2(job):
            return bank[BANK[job]][:, :].rearrange("p (a b) -> p a b", a=2)

        def pb4(job):
            return bank[BANK[job]][:, :].rearrange("p (a b) -> p a b", a=4)

        def index_head(per, i, j):
            return 2 * per * (i // 2) + i % 2 + 2 * j

        def flat(ap):
            return ap.rearrange("p a b -> p (a b)")

        first, at_block = {}, 0
        for n, c in STREAM:
            first[n] = at_block
            at_block += c

        made = {}

        class Side:

            def __init__(self, eng, step):
                self.eng, self.step, self.n, self.last, self.l = eng, step, {}, None, 0

            def sig(self, ins, s=None, by=1):
                s = self.step if s is None else s
                ins.then_inc(s, by)
                self.n[s.name] = self.n.get(s.name, 0) + by
                self.last = s, self.n[s.name]

            def settle(self):
                self.eng.wait_ge(*self.last)

            def give(self, l, ins, name):
                self.sig(ins, S[name])
                made[(l, name)] = made.get((l, name), 0) + 1

            def need(self, l, name, k):
                assert 0 < k <= PER_LAYER[name], (name, k)
                self.eng.wait_ge(S[name], l * PER_LAYER[name] + k)

            def full(self, l, job):
                self.eng.wait_ge(bank_full[BANK[job]], l * USES[BANK[job]] + USE[job])

            def free(self, ins, job):
                b = BANK[job]
                ins.then_inc(bank_free[b], 1)
                self.last = bank_free[b], self.l * USES[b] + USE[job]

            def took(self, l, job):
                self.eng.wait_ge(bank_free[BANK[job]], l * USES[BANK[job]] + USE[job])

        block = ctx.enter_context(nc.Block())
        NUV = 256
        PAIRS_A_TURN = RING // 2

        @block.sync
        def _(sp):
            sp.dma_start(X[:, :, :], x_d.rearrange("(t p) d -> p t d", p=P)).then_inc(x_in, 16)
            for l in range(DEPTH):
                base, uv = l * NBLK, l * NBLK + first["uv"]
                for n in range(base, uv + 1):
                    if n >= RING:
                        sp.wait_ge(blocks_used, n - RING + 1)
                    sp.dma_start(ring[n % RING][:, :], w_d[n]).then_inc(landed[n % RING], 16)
                with sp.Fori(0, (NUV - RING) // RING) as i:
                    for j in range(RING):
                        n = uv + 1 + j
                        sp.wait_ge(blocks_used, i * RING + (n - RING + 1))
                        sp.dma_start(ring[n % RING][:, :],
                                     w_d[bass.ds(i * RING + n, 1), :, :].rearrange("o p n -> (o p) n")
                                     ).then_inc(landed[n % RING], 16)
                for n in range(uv + 1 + NUV - RING, uv + NUV):
                    sp.wait_ge(blocks_used, n - RING + 1)
                    sp.dma_start(ring[n % RING][:, :], w_d[n]).then_inc(landed[n % RING], 16)
            sp.wait_ge(S["x_peer"], DEPTH)
            sp.dma_start(out_d.rearrange("(t p) d -> p t d", p=P), X[:, :, :]).then_inc(out_done, 16)
            sp.wait_ge(out_done, 16)

        relb = sb("relb", [64, NHB])
        onehot = xn.rearrange("p t d -> p (t d)")[0:64, 0:STRIP]
        strip_sb = xn.rearrange("p t d -> p (t d)")[0:NHB, STRIP:2 * STRIP]

        @block.gpsimd
        def _(pool):
            nc.gpsimd.memset(relb[:, :], 1.0).then_inc(consts, 1)
            pool.wait_ge(consts, 1)
            pool.dma_start(relb[0:BUCKETS, :], relb_d).then_inc(strip_in, 16)
            pool.dma_start(onehot, onehot_d).then_inc(strip_in, 16)
            nc.gpsimd.memset(ident[:, :], 0.0).then_inc(consts, 1)
            pool.wait_ge(consts, 2)
            nc.gpsimd.affine_select(out=ident[:, :], in_=ident[:, :], compare_op=ALU.not_equal,
                                    fill=1.0, base=0, pattern=[[-1, P]],
                                    channel_multiplier=1).then_inc(consts, 1)
            nc.gpsimd.iota(iota[:, :], pattern=[[1, P]], base=0, channel_multiplier=0,
                           allow_small_or_imprecise_dtypes=True).then_inc(consts, 1)
            nc.gpsimd.iota(iota16[:, :], pattern=[[1, PK]], base=0, channel_multiplier=0,
                           allow_small_or_imprecise_dtypes=True).then_inc(consts, 1)
            nc.gpsimd.memset(zeros[:, :], 0.0).then_inc(consts, 1)
            for n, s in enumerate((g_full, g_free, h_ready, a_done, y_full)):
                nc.gpsimd.memset(credit[:, n:n + 1], 0.0).then_inc(s, 2)
            pool.wait_ge(strip_sb_ready, 1)
            pool.dma_start(strip_d, strip_sb.unsqueeze(1).broadcast_to([NHB, P, STRIP])
                           ).then_inc(strip_out, 16)
            pool.wait_ge(strip_out, 16)
            for l in range(DEPTH):
                if l:
                    pool.wait_ge(h_ready, l * NKEY + 2)
                    pool.wait_ge(S["x_peer"], l)
                pool.dma_start(par, par_d[l]).then_inc(S["params"], 16)
                for t in range(NT):
                    k = P * (t + 1)
                    src = bass.AP(strip_d.tensor, strip_d.offset + 255 - P * t,
                                  [[STRIP - 1, P], [P * STRIP, NHB], [1, k]])
                    pool.dma_start(bias[t], src).then_inc(S["bias"], 16)
                pool.wait_ge(S["params"], 16 * (l + 1))
                ws = p_("ws").rearrange("p (g t) -> p g t", g=BG)
                nc.gpsimd.affine_select(out=ws, in_=ws, compare_op=ALU.is_ge, fill=0.0, base=0,
                                        pattern=[[0, BG], [1, P]],
                                        channel_multiplier=-1).then_inc(S["wmask"], 1)
                pool.dma_start(ms, mem_d.rearrange("(t p) d -> p t d", p=P)).then_inc(S["mem_in"], 16)
                for t in range(NT):
                    pool.wait_ge(S["relu_used"], 6 * l + (2, 6)[t])
                    k = P * (t + 1)
                    nc.gpsimd.affine_select(out=score[:, t, 0:k], in_=score[:, t, 0:k],
                                            compare_op=ALU.is_ge, fill=MASK, base=P * t,
                                            pattern=[[-1, k]],
                                            channel_multiplier=1).then_inc(S["masked"], 1)

        def stats(name):
            a, w, _ = ROOTS[name]
            return stat[:, a:a + w]

        RORD = {n: i + 1 for i, n in enumerate(["x", "m", "ck", "cq", "qa", "ka", "v", "mk", "ya",
                                                "y", "mq", "z"])}
        SQO = {n: NT * i for i, n in enumerate(SQUARES)}
        ROWS = {"x": 0, "m": 2, "y": 4, "z": 6}
        HN = {"cq": 0, "qa": 2, "ka": 4, "mk": 6, "mq": 8}
        assert sorted(RORD) == sorted(ROOTS)

        @block.scalar
        def _(act):
            A = Side(act, act_step)
            a_ = nc.scalar.activation

            def row_sumsq(l, src, name):
                for t in range(NT):
                    A.give(l, a_(xn[:, t, :], src[:, t, :], ACT.Square,
                                 accum_out=stats(name)[:, t:t + 1]), "sumsq")

            def root(l, name):
                A.need(l, "rms_in", RORD[name])
                A.give(l, a_(stats(name), stats(name), ACT.Sqrt), "rms_rt")

            def square(l, name, job=None):
                for t in range(NT):
                    n = l * NSQ + SQO[name] + t
                    if n >= 4:
                        act.wait_ge(S["sq_used"], n - 3)
                    if job:
                        A.full(l, f"{job}{t}")
                    A.give(l, a_(sq[n % 4], pb(f"{job}{t}")[:, :] if job else vg[:, t, :],
                                 ACT.Square), "sq")

            def copy_out(l, job, dst, src, func=ACT.Copy):
                A.full(l, job)
                A.free(a_(dst, src, func), job)

            def gain_out(l, job, dst, gain, i):
                A.full(l, job)
                A.sig(a_(dst[:, 2 * i, :], pb2(job)[:, 0, :], ACT.Copy,
                         scale=p_(gain, 2 * i, 2 * i + 1)))
                A.free(a_(dst[:, 2 * i + 1, :], pb2(job)[:, 1, :], ACT.Copy,
                          scale=p_(gain, 2 * i + 1, 2 * i + 2)), job)

            act.wait_ge(x_in, 16)
            act.wait_ge(strip_out, 16)
            for l in range(DEPTH):
                A.l = l
                if l:
                    act.wait_ge(S["x_peer"], l)
                row_sumsq(l, X, "x")
                root(l, "x")
                act.wait_ge(S["params"], 16 * (l + 1))
                A.need(l, "rows", ROWS["x"] + NT)
                for i in (0, 2):
                    gain_out(l, f"nx{i}", xnT, "g_mix", i)
                act.wait_ge(S["mem_in"], 16 * (l + 1))
                for i in range(NT):
                    A.full(l, "nx3")
                row_sumsq(l, ms, "m")
                root(l, "m")
                for t in range(NT):
                    A.full(l, f"cs{t}")
                    A.give(l, a_(sq[t][:, 0:P], pb(f"cs{t}")[:, 0:P], ACT.Square,
                                 accum_out=stats("ck")[:, t:t + 1]), "csq")
                root(l, "ck")
                for i in range(2):
                    copy_out(l, f"iq{i}", iqT[:, 2 * i:2 * i + 2, :], pb2(f"iq{i}"))
                copy_out(l, "ik", ikT, pb("ik")[:, 0:SEQ])
                for n, job in enumerate(["is00", "is01", "is10", "is11", "is12", "is13"]):
                    if l * 6 + n >= 2:
                        act.wait_ge(S["relu_used"], l * 6 + n - 1)
                    copy_out(l, job, relu[n % 2], pb(job)[:, :], ACT.Relu)
                square(l, "cq", "cq")
                root(l, "cq")
                square(l, "qa", "qa")
                root(l, "qa")
                square(l, "ka", "ka")
                root(l, "ka")
                for t in range(NT):
                    copy_out(l, f"va{t}", va[:, t, :], pb(f"va{t}")[:, :])
                for t in range(NT):
                    copy_out(l, f"zv{t}", vg[:, t, :], pb(f"zv{t}")[:, :], ACT.Gelu)
                A.settle()
                square(l, "v")
                root(l, "v")
                for i in range(2):
                    copy_out(l, f"zu{i}", uT[:, 2 * i:2 * i + 2, :], pb2(f"zu{i}"), ACT.Gelu)
                for i in range(12):
                    copy_out(l, f"gt{i}", gates[:, 2 * i:2 * i + 2, :], pb2(f"gt{i}"), ACT.Sigmoid)
                A.need(l, "lam_s", 1)
                A.give(l, a_(lam[:, 0:2], lam[:, 0:2], ACT.Exp), "lam_e")

                def a_exp(u):
                    k = P * (u % 2 + 1)
                    A.need(l, "a_max", u + 1)
                    for m in range(2):
                        e = a_(a_log[u % 2][:, m, 0:k], a_log[u % 2][:, m, 0:k], ACT.Exp,
                               bias=a_mx[:, u, m:m + 1], accum_out=a_sum[:, u, m:m + 1])
                        if m:
                            A.give(l, e, "a_exp")
                        else:
                            A.sig(e)

                for u in range(4):
                    a_exp(u)
                for i in range(4):
                    gain_out(l, f"mx{i}", msT, "g_src", i)
                for u in range(4, 8):
                    a_exp(u)
                square(l, "mk", "mk")
                root(l, "mk")
                for t in range(NT):
                    copy_out(l, f"mv{t}", mv[:, t, :], pb(f"mv{t}")[:, :])
                for t in range(NT):
                    A.need(l, "c_max", t + 1)
                    A.give(l, a_(c_log[t], c_log[t], ACT.Exp), "c_exp")
                for h in range(AH):
                    copy_out(l, f"pT{h}", a_pT[h],
                             pb(f"pT{h}")[:, 0:3 * P].rearrange("p (a b) -> p a b", a=3))
                square(l, "ya", "ay")
                root(l, "ya")
                for i in range(3):
                    copy_out(l, f"ct{i}", c_pT[i], pb4(f"ct{i}"))
                for t in range(NT):
                    copy_out(l, f"cy{t}", ycT[:, :, t * P:(t + 1) * P], pb4(f"cy{t}"))
                A.took(l, "o3")
                row_sumsq(l, X, "y")
                root(l, "y")
                A.need(l, "rows", ROWS["y"] + NT)
                for i in (0, 2):
                    gain_out(l, f"ny{i}", xnT, "g_mem", i)
                square(l, "mq", "mq")
                root(l, "mq")
                for t in range(NT):
                    A.need(l, "m_max", t + 1)
                    for h in range(MH):
                        job = f"ml{t}{h // 2}"
                        e = a_(m_e[t][:, h, :], pb2(job)[:, h % 2, :], ACT.Exp, scale=MD ** -0.5,
                               bias=m_mx[:, t, h:h + 1], accum_out=m_sum[:, t, h:h + 1])
                        if h % 2:
                            A.free(e, job)
                        else:
                            A.sig(e)
                for t in range(NT):
                    for k in range(NT):
                        copy_out(l, f"mp{t}{k}", m_pT[:, k, :, t * P:(t + 1) * P], pb4(f"mp{t}{k}"))
                for i in range(2):
                    copy_out(l, f"mo{i}", moT[:, 2 * i:2 * i + 2, :], pb2(f"mo{i}"))
                A.took(l, "w3")
                row_sumsq(l, X, "z")
                root(l, "z")
                A.need(l, "rows", ROWS["z"] + NT)
                for i in (0, 2):
                    gain_out(l, f"nz{i}", xnT, "g_peer", i)
                for i in range(8):
                    copy_out(l, f"pq{i}", pqT[:, 2 * i:2 * i + 2, :], pb2(f"pq{i}"))
                for t in range(NT):
                    for i in range(4):
                        copy_out(l, f"ps{t}{i}", ps[t][:, 4 * i:4 * i + 4, :], pb4(f"ps{t}{i}"))
                for t in range(NT):
                    A.need(l, "r_sub", t + 1)
                    A.give(l, a_(cs[:, t], cs[:, t], ACT.Exp), "r_exp")
                A.took(l, "gT")
                A.took(l, "eT")
                with act.Fori(0, SEQ // 16) as i:
                    for s in range(4):
                        act.wait_ge(g_full, i * 4 + (l * 64 + s + 3))
                        nc.scalar.copy(G[:, bass.ds(i * 16 + 4 * s, 4), :],
                                       bank[6 + s % 2][:, :].rearrange("p (t n) -> p t n", t=4)
                                       ).then_inc(g_free, 1)
                def gelu(i, j):
                    act.wait_ge(a_full, i * 4 + (l * NKEY + j + 1))
                    act.wait_ge(h_ready, i * 4 + (l * NKEY + j + 1))
                    a_(act_t[j % 2][:, :], bank[4 + j % 2][:, 0:SEQ], ACT.Gelu).then_inc(a_done, 1)
                with act.Fori(0, NKEY // 4) as i:
                    for j in range(4):
                        gelu(i, j)

        @block.vector
        def _(dve):
            V = Side(dve, dve_step)
            v = nc.vector

            def inverse_rms(l, name, ready):
                _, _, n = ROOTS[name]
                ready()
                V.give(l, v.tensor_scalar(stats(name), stats(name), 1.0 / n, EPS, ALU.mult,
                                          ALU.add), "rms_in")
                V.need(l, "rms_rt", RORD[name])
                V.sig(v.reciprocal(stats(name), stats(name)))
                V.settle()

            def norm_rows(l, src, dst, name):
                inverse_rms(l, name, lambda: V.need(l, "sumsq", ROWS[name] + NT))
                for t in range(NT):
                    V.give(l, v.tensor_scalar(dst[:, t, :], src[:, t, :],
                                              stats(name)[:, t:t + 1], None, ALU.mult), "rows")

            def sum_squares(l, name, w):
                for t in range(NT):
                    n = SQO[name] + t
                    V.need(l, "sq", n + 1)
                    g = 512 // w
                    V.give(l, v.tensor_reduce(
                        out=stats(name)[:, t * g:(t + 1) * g],
                        in_=sq[(l * NSQ + n) % 4].rearrange("p (g w) -> p g w", w=w),
                        axis=AX, op=ALU.add), "sq_used")

            def norm_heads(l, name, job, dst, w):
                sum_squares(l, name, w)
                inverse_rms(l, name, V.settle)
                g = 512 // w
                for t in range(NT):
                    r = stats(name)[:, t * g:(t + 1) * g]
                    V.free(v.tensor_tensor(
                        dst[:, t, :].rearrange("p (g w) -> p g w", w=w),
                        pb(f"{job}{t}")[:, :].rearrange("p (g w) -> p g w", w=w),
                        r.unsqueeze(2).broadcast_to([P, g, w]), ALU.mult), f"{job}{t}")

            def gain_out(l, job, dst, gain, i):
                V.full(l, job)
                for j in range(2):
                    o = v.tensor_scalar(dst[:, 2 * i + j, :], pb2(job)[:, j, :],
                                        p_(gain, 2 * i + j, 2 * i + j + 1), None, ALU.mult)
                    if j:
                        V.free(o, job)
                    else:
                        V.sig(o)

            def gain_all(l, job, dst, src, gain, more=None):
                V.full(l, job)
                V.free(v.tensor_scalar(dst, src, p_(gain), more, ALU.mult,
                                       ALU.mult if more is not None else ALU.bypass), job)

            def add_to_x(l, jobs):
                for n, job in enumerate(jobs):
                    t, h = n // 2, n % 2
                    xs = X[:, t, h * 512:(h + 1) * 512]
                    V.full(l, job)
                    V.free(v.tensor_tensor(xs, pb(job)[:, :], xs, ALU.add), job)

            dve.wait_ge(strip_mm, 1)
            v.tensor_copy(strip_sb, bank[0][0:NHB, 0:STRIP]).then_inc(strip_sb_ready, 1)
            dve.wait_ge(x_in, 16)
            dve.wait_ge(strip_out, 16)
            for l in range(DEPTH):
                V.l = l
                lam_init = 0.8 - 0.6 * math.exp(-0.3 * l)
                norm_rows(l, X, xn, "x")
                dve.wait_ge(S["params"], 16 * (l + 1))
                for i in (1, 3):
                    gain_out(l, f"nx{i}", xnT, "g_mix", i)
                for m in range(2):
                    V.sig(v.tensor_tensor(lamt[:, m, :], p_("lam", 2 * m * AD, (2 * m + 1) * AD),
                                          p_("lam", (2 * m + 1) * AD, (2 * m + 2) * AD), ALU.mult))
                V.settle()
                V.give(l, v.tensor_reduce(out=lam[:, 0:2], in_=lamt, axis=AX, op=ALU.add), "lam_s")
                norm_rows(l, ms, ms, "m")
                inverse_rms(l, "ck", lambda: V.need(l, "csq", NT))
                for t in range(NT):
                    job = f"cs{t}"
                    V.sig(v.tensor_scalar(ckn[:, t, :], pb(job)[:, 0:P], stats("ck")[:, t:t + 1],
                                          None, ALU.mult))
                    V.sig(v.tensor_copy(cv[:, t, :], pb(job)[:, P:2 * P]))
                    V.free(v.tensor_copy(iw[:, t, :], pb(job)[:, 2 * P:2 * P + IH]), job)
                V.sig(v.memset(score[:, :, :], 0.0))
                V.settle()
                n = 0
                for t in range(NT):
                    k = P * (t + 1)
                    per = 512 // k
                    for i in range(IH // per):
                        V.took(l, f"is{t}{i}")
                        for j in range(per):
                            h = index_head(per, i, j)
                            o = v.scalar_tensor_tensor(
                                out=score[:, t, 0:k], in0=relu[n % 2][:, j * k:(j + 1) * k],
                                scalar=iw[:, t, h:h + 1], in1=score[:, t, 0:k],
                                op0=ALU.mult, op1=ALU.add)
                            if j == per - 1:
                                V.give(l, o, "relu_used")
                            else:
                                V.sig(o)
                            V.settle()
                        n += 1
                norm_heads(l, "cq", "cq", cqn, CD)
                norm_heads(l, "qa", "qa", qan, AD)
                norm_heads(l, "ka", "ka", kan, AD)
                gain_all(l, "ckT", ckT, pb("ckT")[:, 0:SEQ], "ck")
                for i in range(2):
                    gain_all(l, f"cqT{i}", cqT[:, 2 * i:2 * i + 2, :], pb2(f"cqT{i}"), "cq")
                sum_squares(l, "v", P)
                inverse_rms(l, "v", V.settle)
                for t in range(NT):
                    x3 = vg[:, t, :].rearrange("p (g w) -> p g w", w=P)
                    V.give(l, v.tensor_tensor(x3, x3, stats("v")[:, 4 * t:4 * t + 4].unsqueeze(2)
                                              .broadcast_to([P, 4, P]), ALU.mult), "vn")
                for i in range(2):
                    gain_all(l, f"qT{i}", qaT[:, 2 * i:2 * i + 2, :], pb2(f"qT{i}"), "aq")
                for i in range(2):
                    gain_all(l, f"kT{i}", kaT[:, 2 * i:2 * i + 2, :], pb2(f"kT{i}"), "ak")
                for t in range(NT):
                    k = P * (t + 1)
                    V.need(l, "masked", t + 1)
                    for r in range(TOPK_C // 8):
                        V.sig(v.max(out=top8[:, :], in_=score[:, t, 0:k]))
                        V.settle()
                        V.sig(v.match_replace(out=score[:, t, 0:k], in_to_replace=top8[:, :],
                                              in_values=score[:, t, 0:k], imm_value=TAKEN))
                        V.settle()
                    V.give(l, v.tensor_scalar(pen[:, t, 0:k], score[:, t, 0:k], TAKEN / 2, MASK,
                                              ALU.is_gt, ALU.mult), "pen")
                dve.wait_ge(S["bias"], 32 * (l + 1))
                V.need(l, "lam_e", 1)
                V.sig(v.tensor_tensor(lam[:, 2:3], lam[:, 1:2], lam[:, 0:1], ALU.subtract))
                V.settle()
                V.sig(v.tensor_scalar(lam[:, 2:3], lam[:, 2:3], -lam_init, None, ALU.add))
                V.settle()

                def a_start(u):
                    h, t = divmod(u, 2)
                    k = P * (t + 1)
                    for m in range(2):
                        job = f"al{h}{m}"
                        V.full(l, job)
                        o = v.scalar_tensor_tensor(
                            out=a_log[u % 2][:, m, 0:k], in0=pb(job)[:, t * P:t * P + k],
                            scalar=AD ** -0.5, in1=bias[t][:, h, :], op0=ALU.mult, op1=ALU.add)
                        if t:
                            V.free(o, job)
                        else:
                            V.sig(o)
                    V.settle()
                    V.sig(v.tensor_reduce(out=a_mx[:, u, :], in_=a_log[u % 2][:, :, 0:k], axis=AX,
                                          op=ALU.max))
                    V.settle()
                    V.give(l, v.tensor_scalar(a_mx[:, u, :], a_mx[:, u, :], -1.0, None, ALU.mult),
                           "a_max")

                def a_end(u):
                    h, t = divmod(u, 2)
                    k = P * (t + 1)
                    V.need(l, "a_exp", u + 1)
                    V.sig(v.reciprocal(a_sum[:, u, :], a_sum[:, u, :]))
                    V.settle()
                    V.sig(v.tensor_tensor(a_sum[:, u, 1:2], a_sum[:, u, 1:2], lam[:, 2:3],
                                          ALU.mult))
                    V.settle()
                    V.sig(v.tensor_scalar(a_log[u % 2][:, 1, 0:k], a_log[u % 2][:, 1, 0:k],
                                          a_sum[:, u, 1:2], None, ALU.mult))
                    V.settle()
                    V.give(l, v.scalar_tensor_tensor(
                        out=a_pd[h][:, t, 0:k], in0=a_log[u % 2][:, 0, 0:k],
                        scalar=a_sum[:, u, 0:1], in1=a_log[u % 2][:, 1, 0:k],
                        op0=ALU.mult, op1=ALU.add), "pd")
                    V.settle()

                a_start(0)
                for u in range(8):
                    if u < 7:
                        a_start(u + 1)
                    a_end(u)
                norm_heads(l, "mk", "mk", mkn, MD)
                for i in range(2):
                    V.full(l, f"sv{i}")
                    V.took(l, f"zu{i}")
                    for j in range(2):
                        g = 2 * i + j
                        o = v.scalar_tensor_tensor(
                            out=ybT[:, g, :].rearrange("p (c t) -> p c t", c=2),
                            in0=pb2(f"sv{i}")[:, j, :].rearrange("p (c t) -> p c t", c=2),
                            scalar=p_("bv", g, g + 1),
                            in1=p_("bs", g * P, (g + 1) * P).unsqueeze(1).broadcast_to([P, 2, P]),
                            op0=ALU.mult, op1=ALU.add)
                        if j:
                            V.free(o, f"sv{i}")
                        else:
                            V.sig(o)
                    V.settle()
                    for j in range(2):
                        g = 2 * i + j
                        V.give(l, v.tensor_tensor(ybT[:, g, :], ybT[:, g, :], uT[:, g, :],
                                                  ALU.mult), "yb")
                for t in range(NT):
                    k = P * (t + 1)
                    for n, job in enumerate(["cl0"] if t == 0 else ["cl1", "cl2"]):
                        hs = slice(0, 4) if t == 0 else slice(2 * n, 2 * n + 2)
                        V.full(l, job)
                        V.free(v.scalar_tensor_tensor(
                            out=c_log[t][:, hs, :],
                            in0=pb(job)[:, :].rearrange("p (h k) -> p h k", k=k),
                            scalar=CD ** -0.5, in1=bias[t][:, AH:, :][:, hs, :],
                            op0=ALU.mult, op1=ALU.add), job)
                    V.settle()
                    V.sig(v.tensor_tensor(c_log[t], c_log[t], pen[:, t, 0:k].unsqueeze(1)
                                          .broadcast_to([P, 4, k]), ALU.add))
                    V.settle()
                    V.sig(v.tensor_reduce(out=c_mx[:, t, :], in_=c_log[t], axis=AX, op=ALU.max))
                    V.settle()
                    V.give(l, v.tensor_tensor(c_log[t], c_log[t], c_mx[:, t, :].unsqueeze(2)
                                              .broadcast_to([P, 4, k]), ALU.subtract), "c_max")
                for t in range(NT):
                    k = P * (t + 1)
                    V.need(l, "c_exp", t + 1)
                    V.sig(v.tensor_reduce(out=c_sum[:, t, :], in_=c_log[t], axis=AX, op=ALU.add))
                    V.settle()
                    V.sig(v.reciprocal(c_sum[:, t, :], c_sum[:, t, :]))
                    V.settle()
                    V.give(l, v.tensor_tensor(c_log[t], c_log[t], c_sum[:, t, :].unsqueeze(2)
                                              .broadcast_to([P, 4, k]), ALU.mult), "c_p")
                norm_heads(l, "ya", "ay", ya, P)
                for i in range(2):
                    gain_all(l, f"mkT{i}", mkT[:, 2 * i:2 * i + 2, :], pb2(f"mkT{i}"), "mk")
                for i in range(2):
                    gain_all(l, f"yT{i}", yaT[:, 2 * i:2 * i + 2, :], pb2(f"yT{i}"), "asub",
                             1.0 - lam_init)
                V.took(l, "gt11")
                for i in range(4):
                    acc = merged[:, 2 * i:2 * i + 2, :]
                    for b, c in enumerate("abc"):
                        job = f"m{c}{i}"
                        V.full(l, job)
                        g = gates[:, b * KC + 2 * i:b * KC + 2 * i + 2, :]
                        V.free(v.tensor_tensor(acc if b == 0 else mtmp, pb2(job), g, ALU.mult), job)
                        V.settle()
                        if b == 1:
                            V.sig(v.tensor_tensor(acc, acc, mtmp, ALU.add))
                            V.settle()
                        if b == 2:
                            V.give(l, v.tensor_tensor(acc, acc, mtmp, ALU.add), "merged")
                add_to_x(l, [f"o{i}" for i in range(4)])
                norm_rows(l, X, xn, "y")
                for i in (1, 3):
                    gain_out(l, f"ny{i}", xnT, "g_mem", i)
                norm_heads(l, "mq", "mq", mqn, MD)
                for i in range(2):
                    gain_all(l, f"mqT{i}", mqT[:, 2 * i:2 * i + 2, :], pb2(f"mqT{i}"), "mq")
                for t in range(NT):
                    for i in range(2):
                        V.full(l, f"ml{t}{i}")
                        V.sig(v.tensor_reduce(out=m_mx[:, t, 2 * i:2 * i + 2], in_=pb2(f"ml{t}{i}"),
                                              axis=AX, op=ALU.max))
                    V.settle()
                    V.give(l, v.tensor_scalar(m_mx[:, t, :], m_mx[:, t, :], -MD ** -0.5, None,
                                              ALU.mult), "m_max")
                for t in range(NT):
                    V.took(l, f"ml{t}0")
                    V.took(l, f"ml{t}1")
                    V.sig(v.reciprocal(m_sum[:, t, :], m_sum[:, t, :]))
                    V.settle()
                    V.give(l, v.tensor_tensor(m_e[t], m_e[t], m_sum[:, t, :].unsqueeze(2)
                                              .broadcast_to([P, 4, SEQ]), ALU.mult), "m_p")
                add_to_x(l, [f"w{i}" for i in range(4)])
                norm_rows(l, X, xn, "z")
                for i in (1, 3):
                    gain_out(l, f"nz{i}", xnT, "g_peer", i)
                for t in range(NT):
                    for i in range(4):
                        V.took(l, f"ps{t}{i}")

                    def sixteen(src, vals, idx):
                        V.sig(v.max(out=vals[:, 0:8], in_=src))
                        V.settle()
                        V.sig(v.max_index(out=idx[:, 0:8], in_max=vals[:, 0:8], in_values=src))
                        V.sig(v.match_replace(out=src, in_to_replace=vals[:, 0:8], in_values=src,
                                              imm_value=TAKEN))
                        V.settle()
                        V.sig(v.max(out=vals[:, 8:16], in_=src))
                        V.settle()
                        V.sig(v.max_index(out=idx[:, 8:16], in_max=vals[:, 8:16], in_values=src))

                    for c in range(16):
                        sixteen(ps[t][:, c, :], v16[:, t, c, :], i16[:, t, c, :])
                    V.settle()
                    V.sig(v.tensor_copy(i16f[:, t], i16[:, t]))
                    vv = v16[:, t].rearrange("p (h two) k -> p h two k", two=2)
                    V.sig(v.tensor_tensor(
                        cand[:, t].rearrange("p h (i j) -> p h i j", i=PK),
                        vv[:, :, 0, :].unsqueeze(3).broadcast_to([P, PH, PK, PK]),
                        vv[:, :, 1, :].unsqueeze(2).broadcast_to([P, PH, PK, PK]), ALU.add))
                    V.settle()
                    for h in range(PH):
                        sixteen(cand[:, t, h, :], cs[:, t, h, :], ci[:, t, h, :])
                    V.settle()
                    V.sig(v.tensor_copy(rstat[:, t, 0, :], cs[:, t, :, 0]))
                    V.settle()
                    V.give(l, v.tensor_tensor(cs[:, t], cs[:, t], rstat[:, t, 0, :].unsqueeze(2)
                                              .broadcast_to([P, PH, PK]), ALU.subtract), "r_sub")
                    ii = i16f[:, t].rearrange("p (h two) k -> p h two k", two=2)
                    cit = ci[:, t].rearrange("p h k -> p (h k)")
                    for part in range(2):
                        if part == 0:
                            V.sig(v.tensor_scalar(half[:, t, :], cit, 4, None,
                                                  ALU.logical_shift_right))
                        else:
                            V.sig(v.tensor_scalar(half[:, t, :], cit, 15, None, ALU.bitwise_and))
                        V.settle()
                        V.sig(v.tensor_copy(halff[:, t, :], half[:, t, :]))
                        V.settle()
                        V.sig(v.tensor_tensor(
                            eq, halff[:, t, :].unsqueeze(2).broadcast_to([P, P, PK]),
                            iota16[:, :].unsqueeze(1).broadcast_to([P, P, PK]), ALU.is_equal))
                        V.settle()
                        eq4 = eq.rearrange("p (h k) i -> p h k i", h=PH)
                        V.sig(v.tensor_tensor(eq4, eq4, ii[:, :, part, :].unsqueeze(2)
                                              .broadcast_to([P, PH, PK, PK]), ALU.mult))
                        V.settle()
                        V.sig(v.tensor_reduce(out=etok[:, part, t, :], in_=eq, axis=AX, op=ALU.add))
                        V.settle()
                    V.need(l, "r_exp", t + 1)
                    V.sig(v.tensor_reduce(out=rstat[:, t, 1, :], in_=cs[:, t], axis=AX, op=ALU.add))
                    V.settle()
                    V.sig(v.reciprocal(rstat[:, t, 1, :], rstat[:, t, 1, :]))
                    V.settle()
                    V.give(l, v.tensor_tensor(
                        gate[:, t, :].rearrange("p (h k) -> p h k", h=PH), cs[:, t],
                        rstat[:, t, 1, :].unsqueeze(2).broadcast_to([P, PH, PK]), ALU.mult),
                        "route")
                V.full(l, "eT")
                V.sig(v.tensor_copy(e1T[:, :], pb2("eT")[:, 0, :]))
                V.free(v.tensor_copy(e2T[:, :], pb2("eT")[:, 1, :]), "eT")
                V.full(l, "gT")
                V.free(v.tensor_copy(gateT[:, :], pb("gT")[:, 0:SEQ]), "gT")
                V.settle()
                with dve.Fori(0, SEQ // 16) as i:
                    for s in range(4):
                        dve.wait_ge(g_full, i * 4 + (l * 64 + s + 1))
                        for q in range(4):
                            tok = bass.ds(i * 16 + (4 * s + q), 1)
                            v.tensor_scalar(oh1[s % 2][:, q, :], iota[:, :], e1T[:, tok], None,
                                            ALU.is_equal)
                            o = v.tensor_scalar(oh2[s % 2][:, q, :], iota[:, :], e2T[:, tok],
                                                gateT[:, tok], ALU.is_equal, ALU.mult)
                        o.then_inc(oh_ready, 1)
                dve.wait_ge(g_free, (l + 1) * 64 + 2)

                with dve.Fori(0, NKEY // 4) as i:
                    for j in range(4):
                        dve.wait_ge(a_done, i * 4 + (l * NKEY + j + 3))
                        dve.wait_ge(y_full, i * 4 + (l * NKEY + j + 1))
                        v.tensor_tensor(hid_t[j % 2][:, :], act_t[j % 2][:, :],
                                        G[:, :, bass.ds(i * 4 + j, 1)].rearrange("p t o -> p (t o)"),
                                        ALU.mult).then_inc(h_ready, 1)
                dve.wait_ge(y_full, (l + 1) * NKEY + 2)
                for n in range(4):
                    t, h = n // 2, n % 2
                    xs = X[:, t, h * 512:(h + 1) * 512]
                    o = v.tensor_tensor(xs, bank[n][:, :], xs, ALU.add)
                    if n == 3:
                        V.give(l, o, "x_peer")
                    else:
                        V.sig(o)
                V.settle()

        @block.tensor
        def _(pe):
            T = Side(pe, None)
            mm_, tr_ = nc.tensor.matmul, nc.tensor.transpose
            owed = [0]
            blk = [0]

            def mm(out, lhsT, rhs, start, stop, sem=None):
                o = mm_(out, lhsT, rhs, start=start, stop=stop)
                if sem is not None:
                    o.then_inc(sem, 1)
                elif owed[0]:
                    o.then_inc(blocks_used, owed[0])
                    owed[0] = 0
                return o

            def begin(l, job):
                n = l * USES[BANK[job]] + USE[job] - 1
                if n:
                    pe.wait_ge(bank_free[BANK[job]], n)

            def fullsem(job):
                return bank_full[BANK[job]]

            def next_block():
                n = blk[0]
                blk[0] += 1
                pe.wait_ge(landed[n % RING], 16 * (n // RING + 1))
                return ring[n % RING]

            def transposes(l, job, pairs):
                begin(l, job)
                for n, src in enumerate(pairs):
                    o = tr_(pb(job)[:, n * P:(n + 1) * P], src, ident[:, :])
                o.then_inc(fullsem(job), 1)

            def rows_T(l, pre, src):
                for i in range(4):
                    transposes(l, f"{pre}{i}", [src[:, t, c * P:(c + 1) * P]
                                                for c in (2 * i, 2 * i + 1) for t in range(NT)])

            def heads_T(l, pre, src):
                for i in range(2):
                    transposes(l, f"{pre}{i}", [src[:, t, c * P:(c + 1) * P]
                                                for c in (2 * i, 2 * i + 1) for t in range(NT)])

            def token_major(l, job, srcT, w=512):
                for t in range(NT):
                    begin(l, f"{job}{t}")
                for b in range(4):
                    wt = next_block()[:, :].rearrange("p (k n) -> p k n", k=2)
                    for t in range(NT):
                        for kk in range(2):
                            k = 2 * b + kk
                            end = k == KC - 1
                            mm(pb(f"{job}{t}")[:, 0:w], srcT[:, k, t * P:(t + 1) * P],
                               wt[:, kk, 0:w], k == 0, end, fullsem(f"{job}{t}") if end else None)
                    owed[0] += 1

            def transposed(l, job, srcT, n=2):
                begin(l, job)
                for c in range(n):
                    wt = next_block()
                    for k in range(KC):
                        last = c == n - 1 and k == KC - 1
                        mm(pb2(job)[:, c, :], wt[:, k * P:(k + 1) * P], srcT[:, k, :],
                           k == 0, k == KC - 1, fullsem(job) if last else None)
                    owed[0] += 1

            def half_rows(l, jobs, srcT, kc, per):
                for job in jobs:
                    begin(l, job)
                for k in range(kc):
                    wt = next_block()
                    for n, job in enumerate(jobs):
                        t, h = n // 2, n % 2
                        end = k == kc - 1
                        mm(pb(job)[:, :], srcT[:, k, t * P:(t + 1) * P],
                           wt[:, h * 512:(h + 1) * 512], k == 0, end, fullsem(job) if end else None)
                    owed[0] += 1

            pe.wait_ge(consts, 6)
            pe.wait_ge(strip_in, 32)
            mm_(bank[0][0:NHB, 0:STRIP], relb[:, :], onehot, start=True,
                stop=True).then_inc(strip_mm, 1)
            pe.wait_ge(strip_sb_ready, 1)
            for l in range(DEPTH):
                T.need(l, "rows", ROWS["x"] + NT)
                rows_T(l, "nx", xn)
                for i in range(4):
                    T.took(l, f"nx{i}")
                token_major(l, "cs", xnT, 2 * P + IH)
                for i in range(2):
                    transposed(l, f"iq{i}", xnT)
                transposed(l, "ik", xnT, 1)
                token_major(l, "cq", xnT)
                T.took(l, "iq0")
                T.took(l, "iq1")
                T.took(l, "ik")
                for t in range(NT):
                    k = P * (t + 1)
                    per = 512 // k
                    for i in range(IH // per):
                        job = f"is{t}{i}"
                        begin(l, job)
                        for j in range(per):
                            h = index_head(per, i, j)
                            r = slice(64 * (h % 2), 64 * (h % 2) + 64)
                            mm(pb(job)[:, j * k:(j + 1) * k], iqT[r, h // 2, t * P:(t + 1) * P],
                               ikT[r, 0:k], True, True, fullsem(job) if j == per - 1 else None)
                token_major(l, "qa", xnT)
                token_major(l, "ka", xnT)
                T.took(l, "cs0")
                T.took(l, "cs1")
                transposes(l, "ckT", [ckn[:, t, :] for t in range(NT)])
                T.took(l, "cq1")
                T.took(l, "cq0")
                heads_T(l, "cqT", cqn)
                token_major(l, "va", xnT)
                token_major(l, "zv", xnT)
                for t in range(NT):
                    T.took(l, f"qa{t}")
                    T.took(l, f"ka{t}")
                heads_T(l, "qT", qan)
                heads_T(l, "kT", kan)
                for i in range(2):
                    transposed(l, f"zu{i}", xnT)
                for i in range(12):
                    transposed(l, f"gt{i}", xnT)
                for i in range(2):
                    T.took(l, f"qT{i}")
                    T.took(l, f"kT{i}")
                for h in range(AH):
                    for m in range(2):
                        job = f"al{h}{m}"
                        begin(l, job)
                        r = slice(64 * m, 64 * m + 64)
                        for t in range(NT):
                            k = P * (t + 1)
                            mm(pb(job)[:, t * P:t * P + k], qaT[r, h, t * P:(t + 1) * P],
                               kaT[r, h, 0:k], True, True, fullsem(job) if t else None)
                T.need(l, "rows", ROWS["m"] + NT)
                rows_T(l, "mx", ms)
                for i in range(4):
                    T.took(l, f"mx{i}")
                token_major(l, "mk", msT)
                token_major(l, "mv", msT)
                T.need(l, "vn", NT)
                T.need(l, "wmask", 1)
                for i in range(2):
                    job = f"sv{i}"
                    begin(l, job)
                    for j in range(2):
                        for c in range(NT):
                            g = 2 * i + j
                            mm(pb2(job)[:, j, c * P:(c + 1) * P], vg[:, c, g * P:(g + 1) * P],
                               p_("ws", g * P, (g + 1) * P), True, True,
                               fullsem(job) if j and c else None)
                T.took(l, "ckT")
                T.took(l, "cqT0")
                T.took(l, "cqT1")
                for job, t, hs in (("cl0", 0, range(4)), ("cl1", 1, range(2)),
                                   ("cl2", 1, range(2, 4))):
                    k = P * (t + 1)
                    begin(l, job)
                    for n, h in enumerate(hs):
                        mm(pb(job)[:, n * k:(n + 1) * k], cqT[:, h, t * P:(t + 1) * P],
                           ckT[:, 0:k], True, True, fullsem(job) if h == hs[-1] else None)
                for h in range(AH):
                    T.need(l, "pd", 2 * h + 2)
                    transposes(l, f"pT{h}", [a_pd[h][:, 0, 0:P], a_pd[h][:, 1, 0:P],
                                             a_pd[h][:, 1, P:2 * P]])
                T.took(l, "va0")
                T.took(l, "va1")
                for t in range(NT):
                    begin(l, f"ay{t}")
                for h in range(AH):
                    T.took(l, f"pT{h}")
                    vh = va[:, :, h * P:(h + 1) * P]
                    end = h == AH - 1
                    mm(pb("ay0")[:, h * P:(h + 1) * P], a_pT[h][:, 0, :], vh[:, 0, :], True, True,
                       fullsem("ay0") if end else None)
                    mm(pb("ay1")[:, h * P:(h + 1) * P], a_pT[h][:, 1, :], vh[:, 0, :], True, False)
                    mm(pb("ay1")[:, h * P:(h + 1) * P], a_pT[h][:, 2, :], vh[:, 1, :], False, True,
                       fullsem("ay1") if end else None)
                T.need(l, "c_p", 1)
                transposes(l, "ct0", [c_log[0][:, h, :] for h in range(CH)])
                T.need(l, "c_p", 2)
                for c in range(NT):
                    transposes(l, f"ct{c + 1}", [c_log[1][:, h, c * P:(c + 1) * P]
                                                 for h in range(CH)])
                begin(l, "cy0")
                T.took(l, "ct0")
                mm(pb("cy0")[:, :], cv[:, 0, :], flat(c_pT[0]), True, True, fullsem("cy0"))
                begin(l, "cy1")
                for c in range(NT):
                    T.took(l, f"ct{c + 1}")
                    mm(pb("cy1")[:, :], cv[:, c, :], flat(c_pT[c + 1]), c == 0, c == 1,
                       fullsem("cy1") if c else None)
                T.took(l, "mk0")
                T.took(l, "mk1")
                heads_T(l, "mkT", mkn)
                T.took(l, "ay0")
                T.took(l, "ay1")
                heads_T(l, "yT", ya)
                T.took(l, "yT0")
                T.took(l, "yT1")
                T.need(l, "yb", 4)
                T.took(l, "cy0")
                T.took(l, "cy1")
                for i in range(4):
                    for b, src in (("a", yaT), ("b", ybT), ("c", ycT)):
                        job = f"m{b}{i}"
                        begin(l, job)
                        wt = next_block()[:, :].rearrange("p (c k n) -> p c k n", c=2, k=4)
                        for c in range(2):
                            for k in range(4):
                                mm(pb2(job)[:, c, :], wt[:, c, k, :], src[:, k, :], k == 0, k == 3,
                                   fullsem(job) if c and k == 3 else None)
                        owed[0] += 1
                for i in range(4):
                    T.need(l, "merged", i + 1)
                half_rows(l, [f"o{i}" for i in range(4)], merged, KC, 1)
                T.need(l, "rows", ROWS["y"] + NT)
                rows_T(l, "ny", xn)
                for i in range(4):
                    T.took(l, f"ny{i}")
                token_major(l, "mq", xnT)
                T.took(l, "mq0")
                T.took(l, "mq1")
                heads_T(l, "mqT", mqn)
                for i in range(2):
                    T.took(l, f"mqT{i}")
                    T.took(l, f"mkT{i}")
                for t in range(NT):
                    for i in range(2):
                        job = f"ml{t}{i}"
                        begin(l, job)
                        for j in range(2):
                            h = 2 * i + j
                            mm(pb2(job)[:, j, :], mqT[:, h, t * P:(t + 1) * P], mkT[:, h, :],
                               True, True, fullsem(job) if j else None)
                for t in range(NT):
                    T.need(l, "m_p", t + 1)
                    for k in range(NT):
                        transposes(l, f"mp{t}{k}", [m_e[t][:, h, k * P:(k + 1) * P]
                                                    for h in range(MH)])
                for t in range(NT):
                    T.took(l, f"mv{t}")
                    for k in range(NT):
                        T.took(l, f"mp{t}{k}")
                for i in range(2):
                    begin(l, f"mo{i}")
                    for j in range(2):
                        h = 2 * i + j
                        for k in range(NT):
                            mm(pb2(f"mo{i}")[:, j, :], mv[:, k, h * P:(h + 1) * P], m_pT[:, k, h, :],
                               k == 0, k == 1, fullsem(f"mo{i}") if j and k else None)
                T.took(l, "mo0")
                T.took(l, "mo1")
                half_rows(l, [f"w{i}" for i in range(4)], moT, 4, 1)
                T.need(l, "rows", ROWS["z"] + NT)
                rows_T(l, "nz", xn)
                for i in range(4):
                    T.took(l, f"nz{i}")
                for i in range(8):
                    transposed(l, f"pq{i}", xnT)
                for i in range(8):
                    T.took(l, f"pq{i}")
                for t in range(NT):
                    for i in range(4):
                        job = f"ps{t}{i}"
                        begin(l, job)
                        for j in range(4):
                            c = 4 * i + j
                            mm(pb4(job)[:, j, :], pqT[:, c, t * P:(t + 1) * P],
                               p_("sk", (c % 2) * NKEY, (c % 2 + 1) * NKEY), True, True,
                               fullsem(job) if j == 3 else None)
                T.need(l, "route", NT)
                transposes(l, "eT", [etok[:, part, t, :] for part in range(2) for t in range(NT)])
                transposes(l, "gT", [gate[:, t, :] for t in range(NT)])
                for b in range(8):
                    pe.wait_ge(bank_free[b], (l + 1) * USES[b])
                with pe.Fori(0, SEQ // 16) as i:
                    for s in range(4):
                        pe.wait_ge(oh_ready, i * 4 + (l * 64 + s + 1))
                        pe.wait_ge(g_free, i * 4 + (l * 64 + s + 1))
                        for q in range(4):
                            o = mm_(bank[6 + s % 2][:, q * P:(q + 1) * P], oh1[s % 2][:, q, :],
                                    oh2[s % 2][:, q, :], start=True, stop=True)
                        o.then_inc(g_full, 1)
                uv = l * NBLK + first["uv"]
                assert blk[0] == uv
                for n in range(4):
                    o = mm_(bank[n][:, :], zeros[:, 0:P], zeros[:, :], start=True, stop=False)
                    if n == 0 and owed[0]:
                        o.then_inc(blocks_used, owed[0])
                        owed[0] = 0

                def up(n, wait_landed, c, a_wait, give):
                    wait_landed()
                    a_wait()
                    for k in range(KC):
                        o = mm_(bank[4 + c % 2][:, 0:SEQ], ring[n % RING][:, k * P:(k + 1) * P],
                                xnT[:, k, :], start=k == 0, stop=k == KC - 1)
                        if k == 0 and give:
                            o.then_inc(blocks_used, 1)
                    o.then_inc(a_full, 1)

                def down(n, wait_landed, c, h_wait, stop=False):
                    wait_landed()
                    h_wait()
                    for m in range(4):
                        t, h = m // 2, m % 2
                        o = mm_(bank[m][:, :], hid_t[c % 2][:, t * P:(t + 1) * P],
                                ring[n % RING][:, h * 512:(h + 1) * 512], start=False, stop=stop)
                        if m == 0:
                            o.then_inc(blocks_used, 1)
                    o.then_inc(y_full, 1)

                up(uv, lambda: pe.wait_ge(landed[uv % RING], 16 * (uv // RING + 1)), 0,
                   lambda: pe.wait_ge(a_done, l * NKEY + 1), False)
                NPAIR = NKEY - 1
                TURNS = NPAIR // PAIRS_A_TURN
                rest = list(range(TURNS * PAIRS_A_TURN, NPAIR))

                def pair(i, j):
                    c = j
                    n = uv + 1 + 2 * j
                    up(n, lambda: pe.wait_ge(landed[n % RING], i * 16 + 16 * (n // RING + 1)),
                       c + 1, lambda: pe.wait_ge(a_done, i * PAIRS_A_TURN + (l * NKEY + c + 2)),
                       True)
                    down(n + 1, lambda: pe.wait_ge(landed[(n + 1) % RING],
                                                   i * 16 + 16 * ((n + 1) // RING + 1)),
                         c, lambda: pe.wait_ge(h_ready, i * PAIRS_A_TURN + (l * NKEY + c + 3)))

                with pe.Fori(0, TURNS) as i:
                    for j in range(PAIRS_A_TURN):
                        pair(i, j)
                for j in rest:
                    pair(0, j)
                n = uv + NUV - 1
                down(n, lambda: pe.wait_ge(landed[n % RING], 16 * (n // RING + 1)), NKEY - 1,
                     lambda: pe.wait_ge(h_ready, (l + 1) * NKEY + 2), stop=True)
                blk[0] = uv + NUV
                owed[0] = 1
        for (l, name), n in made.items():
            assert n == PER_LAYER[name], (l, name, n)


def strip_selector():
    import numpy as np
    n = 255 - np.arange(STRIP)
    exact = BUCKETS // 2
    nf = np.maximum(n, 1).astype(np.float32)
    large = exact + (np.log(nf / exact) / math.log(MAXDIST / exact) * (BUCKETS - exact)).astype(np.int32)
    b = np.where(n < exact, np.maximum(n, 0), np.minimum(large, BUCKETS - 1))
    out = np.zeros((64, STRIP), np.float32)
    out[b, np.arange(STRIP)] = 1.0
    out[BUCKETS, n < 0] = MASK
    return out


def kernel(**inputs):
    import numpy as np
    import concourse.bacc as bacc
    from concourse.bass_utils import run_bass_kernel_spmd

    a = {k: np.asarray(v) for k, v in inputs.items()}

    def token_major(w):
        return w.reshape(4, 2, P, 512).transpose(0, 2, 1, 3).reshape(4, P, 1024)

    def columns(w):
        n = w.shape[1] // P
        return w.reshape(KC, P, n, P).transpose(2, 1, 0, 3).reshape(n, P, 1024)

    def rows(w):
        return w.reshape(-1, P, 1024)

    def branch(w):
        return w.reshape(4, P, 4, 2, P).transpose(2, 1, 3, 0, 4).reshape(4, P, 1024)

    def cols(w):
        return w.reshape(-1, P).T

    blocks = np.empty((DEPTH * NBLK, P, 1024), np.float32)
    par = np.empty((DEPTH, P, NPAR), np.float32)
    widths = [512] * 6 + [CD, CD, IH * ID, ID, IH, 3 * D]
    for l in range(DEPTH):
        qa, ka, va, zu, zv, cq, ck, cv, iq, ik, iw, gts = np.split(
            a["w_in"][l], np.cumsum(widths)[:-1], axis=1)
        u = a["p_u"][l].reshape(NKEY, NKEY, KC, P).transpose(1, 3, 2, 0).reshape(NKEY, P, 1024)
        v = a["p_v"][l].reshape(NKEY, NKEY, D).transpose(1, 0, 2)
        kv = a["m_wkv"][l]
        small = np.concatenate([ck, cv, iw, np.zeros((D, 512 - 2 * CD - IH), np.float32)], 1)
        br = [branch(a[f"w_br_{c}"][l]) for c in "abc"]
        parts = dict(
            cs=token_major(small), iq=columns(iq), ik=columns(np.concatenate([ik, ik], 1)),
            cq=token_major(cq), qa=token_major(qa), ka=token_major(ka), va=token_major(va),
            zv=token_major(zv), zu=columns(zu), gts=columns(gts),
            mk=token_major(kv[:, :512]), mv=token_major(kv[:, 512:]),
            br=np.stack(br, 1).reshape(12, P, 1024), mix_out=rows(a["w_mix_out"][l]),
            mq=token_major(a["m_wq"][l]), mo=rows(a["m_wo"][l]), pq=columns(a["p_wq"][l]))
        at = l * NBLK
        for name, n in STREAM[:-1]:
            assert parts[name].shape[0] == n
            blocks[at:at + n] = parts[name]
            at += n
        blocks[at] = u[0]
        blocks[at + 1:at + 2 * NKEY - 1:2] = u[1:]
        blocks[at + 2:at + 2 * NKEY - 1:2] = v[:-1]
        blocks[at + 2 * NKEY - 1] = v[-1]
        everywhere = lambda w: np.broadcast_to(w.reshape(1, -1), (P, w.size))
        small = dict(
            g_mix=cols(a["norm_mix"][l]), g_mem=cols(a["norm_mem"][l]),
            g_src=cols(a["norm_memsrc"][l]), g_peer=cols(a["norm_peer"][l]),
            aq=cols(np.tile(a["a_q_gain"][l], 2)), ak=cols(np.tile(a["a_k_gain"][l], 2)),
            cq=cols(a["c_q_gain"][l]), ck=cols(a["c_k_gain"][l]), mq=cols(a["m_q_gain"][l]),
            mk=cols(a["m_k_gain"][l]), asub=cols(a["a_subln_gain"][l]), bv=cols(a["b_v_gain"][l]),
            ws=a["b_w_s"][l].transpose(2, 0, 1).reshape(P, BG * P),
            bs=everywhere(a["b_b_s"][l]),
            lam=everywhere(np.concatenate([a[k][l] for k in ("a_lq1", "a_lk1", "a_lq2", "a_lk2")])),
            sk=np.concatenate([a["p_subkey1"][l].T, a["p_subkey2"][l].T], 1))
        for name, (lo, hi) in PAR.items():
            par[l, :, lo:hi] = small[name]

    nc = bacc.Bacc("TRN2", target_bir_lowering=False, num_devices=1)
    arrays = dict(x=a["x"].reshape(SEQ, D), mem=a["mem"].reshape(SEQ, D), rel_bias=a["rel_bias"],
                  selector=strip_selector(), par=par, blocks=blocks)
    args = [nc.dram_tensor(n, w.shape, F32, kind="ExternalInput").ap() for n, w in arrays.items()]
    out = nc.dram_tensor("out", (SEQ, D), F32, kind="ExternalOutput").ap()
    strip = nc.dram_tensor("strip", (NHB, P, STRIP), F32).ap()
    build(nc, *args, out, strip)
    r = run_bass_kernel_spmd(nc, [{n: np.ascontiguousarray(w) for n, w in arrays.items()}],
                             core_ids=[0])
    return np.asarray(r.results[0]["out"]).reshape(1, SEQ, D)
```

```python
import math
from contextlib import ExitStack

import concourse.bass as bass
from concourse import mybir

F32 = mybir.dt.float32
F32R = mybir.dt.float32r
U32 = mybir.dt.uint32
BF16 = mybir.dt.bfloat16
ACT = mybir.ActivationFunctionType
ALU = mybir.AluOpType
AX = mybir.AxisListType.X

P = 128
D = 1024
SEQ = 256
NT = SEQ // P
DEPTH = 2
KC = D // P
AH, AD = 4, 64
CH, CD = 4, 128
IH, ID = 8, 64
MH, MD = 4, 128
BG = 4
TOPK_C = 64
PH, PK, NKEY = 8, 16, 128
BUCKETS, MAXDIST = 32, 128
NHB = AH + CH
EPS = 1e-6
MASK = -1e30
TAKEN = -3e38
RAW = 3
SPLIT = 3
AHEAD = 2
TURN = 6
R1, R2 = 42, 48
SET = 4
SOME = 64
HALF = NKEY // 2
STRIP = 3 * P

PARTS = [("g_mix", 8), ("g_mem", 8), ("g_src", 8), ("g_peer", 8), ("aq", 1), ("ak", 1), ("cq", 1),
         ("ck", 1), ("mq", 1), ("mk", 1), ("asub", 1), ("bv", 4), ("ws", BG * P), ("bs", BG * P),
         ("lam", 4 * AD), ("sk", 2 * NKEY)]
PAR = {}
NPAR = 0
for _n, _w in PARTS:
    PAR[_n] = (NPAR, NPAR + _w)
    NPAR += _w

STREAM = [("cs", 4, 1), ("iq", 4, 1), ("ik", 1, 1), ("cq", 4, 1), ("mk", 4, 0), ("mv", 4, 0),
          ("qa", 4, 1), ("ka", 4, 1), ("va", 4, 1), ("zv", 4, 1), ("zu", 4, 1), ("gts", 24, 1),
          ("br", 12, 0), ("mix_out", 8, 0), ("mq", 4, 1), ("mo", 4, 0), ("pq", 16, 1),
          ("uv", 2 * NKEY, 1)]
BLOCKS = [(_n, _i, _s) for _n, _c, _s in STREAM for _i in range(_c)]
NBLK = len(BLOCKS)
NSPLIT = sum(b[2] for b in BLOCKS)
NWHOLE = NBLK - NSPLIT
FIRST = {b[0]: i for i, b in reversed(list(enumerate(BLOCKS)))}


def split_no(n):
    l, k = divmod(n, NBLK)
    return l * NSPLIT + sum(b[2] for b in BLOCKS[:k])


JOBS = (["nx0", "nx1", "nx2", "nx3", "cs0", "cs1", "iq0", "iq1", "ik", "cq0", "cq1",
         "mx0", "mx1", "mx2", "mx3", "is00", "is01", "is10", "is11", "is12", "is13",
         "mk0", "mk1", "mv0", "mv1", "qa0", "qa1", "ka0", "ka1", "ckT", "cqT0",
         "cqT1", "va0", "va1", "zv0", "zv1", "mkT0", "mkT1", "qT0", "qT1", "kT0", "kT1", "zu0",
         "zu1"]
        + [f"gt{i}" for i in range(12)] + [f"al{h}{m}" for h in range(AH) for m in range(2)]
        + ["sv0", "sv1", "cl0", "cl1", "cl2"]
        + [f"pT{i}" for i in range(AH)] + ["ay0", "ay1", "ct0", "ct1", "ct2", "cy0", "cy1",
                                           "yT0", "yT1"]
        + [f"m{b}{i}" for i in range(4) for b in "abc"]
        + [f"o{i}" for i in range(4)] + [f"ny{i}" for i in range(4)]
        + ["mq0", "mq1", "mqT0", "mqT1", "ml00", "ml01", "ml10", "ml11", "mp00", "mp01", "mp10",
           "mp11", "mo0", "mo1"]
        + [f"w{i}" for i in range(4)] + [f"nz{i}" for i in range(4)]
        + [f"pq{i}" for i in range(8)] + [f"ps{t}{i}" for t in range(NT) for i in range(4)])
BANK = {j: n % 8 for n, j in enumerate(JOBS)}
BEFORE_LOOPS = [sum(1 for j in JOBS if BANK[j] == b) for b in range(8)]
JOBS += ["eT", "gT"]
BANK["eT"], BANK["gT"] = 0, 1
USE = {j: sum(1 for i in JOBS[:n + 1] if BANK[i] == BANK[j]) for n, j in enumerate(JOBS)}
USES = [sum(1 for j in JOBS if BANK[j] == b) for b in range(8)]

ROOTS = dict(x=(0, 2, D), m=(2, 2, D), ck=(4, 2, CD), cq=(6, 8, CD), qa=(14, 16, AD),
             ka=(30, 16, AD), v=(46, 8, P), mk=(54, 8, MD), ya=(62, 8, P), y=(70, 2, D),
             mq=(72, 8, MD), z=(80, 2, D))
SQUARES = ["cq", "mk", "qa", "ka", "v", "ya", "mq"]
NSQ = len(SQUARES) * NT

PER_LAYER = dict(
    params=16, bias=32, mem_in=16, score0=3, xhi=24, sumsq=8, rms_in=len(ROOTS), rms_rt=len(ROOTS), rows=8,
    csq=2, relu_used=6, wmask=1, pen=2, sq=NSQ, sq_used=NSQ, vn=2,
    lam_s=1, lam_e=1, a_max=8, a_exp=8, pd=8, yb=4, c_max=2, c_exp=2, c_p=2, merged=4, m_max=2,
    m_p=2, r_sub=2, r_exp=2, route=2, x_peer=1)


def build(nc, x_d, mem_d, relb_d, onehot_d, par_d, w_d, out_d, strip_d):
    ctx = ExitStack()
    with ctx:
        def sb(name, shape, dt=F32):
            return ctx.enter_context(nc.sbuf_tensor(name, shape, dt))

        def sem(name):
            return ctx.enter_context(nc.semaphore(name))

        X = sb("X", [P, NT, D])
        xh, xl = sb("xh", [P, KC, SEQ], F32R), sb("xl", [P, KC, SEQ], F32R)
        raw = [sb(f"raw{i}", [P, 1024]) for i in range(RAW)]
        wh = [sb(f"wh{i}", [P, 1024], F32R) for i in range(SPLIT)]
        wl = [sb(f"wl{i}", [P, 1024], F32R) for i in range(SPLIT)]
        stat = sb("stat", [P, 82])
        ident = sb("ident", [P, P])
        iota = sb("iota", [P, NKEY, SET], BF16)
        credit = sb("credit", [P, 5])
        top8 = sb("top8", [P, 8])
        iota16 = sb("iota16", [P, PK])
        loops = sb("loops", [P, 3 * 1024])
        loop_buf = lambda at, *d: loops[:, at:at + math.prod(d)]
        half_words = lambda at, *d: loops[:, at:at + math.prod(d) // 2].bitcast(BF16)
        oh1 = [half_words(i * 256, NKEY, SET).rearrange("p (n q) -> p n q", q=SET)
               for i in (0, 1)]
        chosen = [half_words(512 + i * 128, HALF, SET).rearrange("p (n q) -> p n q", q=SET)
                  for i in (0, 1)]
        oh2 = [half_words(768 + i * 384, 3, HALF, SET).rearrange(
            "p (g n q) -> p g n q", g=3, q=SET) for i in (0, 1)]
        choices = half_words(1536, 5, SEQ).rearrange("p (a t) -> p a t", a=5)
        hid = [loop_buf(2176 + i * SEQ, SEQ) for i in (0, 1)]
        iota_f = loop_buf(0, NKEY, SET).rearrange("p (n q) -> p n q", q=SET)
        some = sb("some", [P, 5, SOME], BF16)
        hh = [sb(f"hh{i}", [P, SEQ], F32R) for i in (0, 1)]
        hl = [sb(f"hl{i}", [P, SEQ], F32R) for i in (0, 1)]
        arena = sb("arena", [P, 2 * SEQ * HALF])
        part = [arena[:, i * SEQ * HALF:(i + 1) * SEQ * HALF] for i in range(2)]
        G = [a.rearrange("p (t n) -> p t n", n=HALF) for a in part]
        gelus = [part[1 - i].rearrange("p (n t) -> p n t", t=SEQ) for i in range(2)]
        def rooms(whole, at, *shapes):
            out = []
            for shape in shapes:
                n = math.prod(shape)
                assert at + n <= whole.shape[1], (at, n)
                a = whole[:, at:at + n]
                at += n
                names = "abcd"[:len(shape)]
                if len(shape) > 1:
                    a = a.rearrange(f"p ({' '.join(names)}) -> p {' '.join(names)}",
                                    **{c: k for c, k in zip(names, shape)})
                out.append(a)
            return out

        wide = (4, SEQ)
        rows4 = (NT, 512)
        va, vg, c_log1 = rooms(loops, 0, rows4, rows4, (4, SEQ))
        at = 0
        layout = {}

        def put(name, *shapes):
            nonlocal at
            layout[name] = at
            out = rooms(arena, at, *shapes)
            at += sum(math.prod(k) for k in shapes)
            return out

        par, = put("par", (NPAR,))
        bias = put("bias", (NHB, P), (NHB, SEQ))
        xn, = put("xn", (NT, D))
        cqn, qan, kan = put("heads", rows4, rows4, rows4)
        a_pT = rooms(arena, layout["heads"] + 1024, *[(3, P)] * AH)
        merged, mtmp = rooms(arena, layout["heads"], (KC, SEQ), (2, SEQ))
        sq = put("sq", *[(512,)] * 2)
        ckn, cv, iw = put("small", (NT, P), (NT, P), (NT, IH))
        iqT, = put("iqT", wide)
        ybT, = rooms(arena, layout["iqT"], wide)
        ikT, = put("ikT", (SEQ,))
        score, pen = put("score", (NT, SEQ), (NT, SEQ))
        qaT, = put("qaT", wide)
        yaT, = rooms(arena, layout["qaT"], wide)
        kaT, = put("kaT", wide)
        ya, = rooms(arena, layout["kaT"], rows4)
        cqT, ckT = put("cqT", wide, (SEQ,))
        uT, gates = put("gates", wide, (24, SEQ))
        ms, msT, _, mkn = rooms(
            arena, layout["gates"], (NT, D), (KC, SEQ), (1024,), rows4)
        mqn, mqT, moT, m_e0, m_e1, m_pT = rooms(
            arena, layout["gates"], rows4, wide, wide, wide, wide, (2, 4, SEQ))
        m_e = [m_e0, m_e1]
        a_log = put("a_log", (2, SEQ), (2, SEQ))
        c_pT = rooms(arena, layout["a_log"], *[(4, P)] * 3)
        put("rest of c_pT", (512,))
        relu = put("relu", (512,), (512,), (1024,))[:2]
        a_pd = rooms(arena, layout["relu"], *[(NT, SEQ)] * AH)
        ycT, = rooms(arena, layout["relu"], wide)
        mkT, = put("mkT", wide)
        c_log = [put("c_log0", (4, P))[0], c_log1]
        mv, = put("mv", rows4)
        lamt, lam = put("lam", (2, AD), (4,))
        a_mx, a_sum = put("a_stats", (8, 2), (8, 2))
        c_mx, c_sum, m_mx, m_sum = put("stats", *[(NT, 4)] * 4)
        at = NPAR
        pqT, ps0, ps1 = put("ps", (16, SEQ), (16, P), (16, P))
        cand, eq = rooms(arena, layout["ps"], (PH, 256), (PH * PK, PK))
        ps = [ps0, ps1]
        v16, i16f = put("top", (NT, 16, PK), (NT, 16, PK))
        cs, gate, half_f = put("gate", (NT, PH, PK), (NT, P), (NT, P))
        etok, rstat = put("etok", (2, NT, P), (NT, 3, PH))
        i16, ci, half_u = [x.bitcast(U32) for x in put("int", (NT, 16, PK), (NT, PH, PK), (NT, P))]
        assert at <= SEQ * HALF

        bank = [ctx.enter_context(nc.psum_tensor(f"bank{i}", [P, 512], F32)) for i in range(8)]
        bank_full = [sem(f"bank_full{i}") for i in range(8)]
        bank_free = [sem(f"bank_free{i}") for i in range(8)]
        landed = [sem(f"landed{i}") for i in range(RAW)]
        S = {n: sem(n) for n in PER_LAYER}
        whole_used = sem("whole_used")
        split_used = sem("split_used")
        hi_done, lo_done = sem("hi_done"), sem("lo_done")
        iota_ready = sem("iota_ready")
        consts, x_in, strip_in = sem("consts"), sem("x_in"), sem("strip_in")
        strip_sb_ready, strip_out, strip_mm = sem("strip_sb"), sem("strip_out"), sem("strip_mm")
        dve_step, act_step, out_done = sem("dve_step"), sem("act_step"), sem("out_done")
        chosen_done = sem("chosen_done")
        oh_ready, g_full, g_free = sem("oh_ready"), sem("g_full"), sem("g_free")
        a_full, a_done, h_ready = sem("a_full"), sem("a_done"), sem("h_ready")
        y_full, toks, hid_m, hid_h = sem("y_full"), sem("toks"), sem("hid_m"), sem("hid_h")

        def p_(name, lo=0, hi=None):
            a, b = PAR[name]
            return par[:, a + lo:(b if hi is None else a + hi)]

        def pb(job):
            return bank[BANK[job]]

        def pb2(job):
            return bank[BANK[job]][:, :].rearrange("p (a b) -> p a b", a=2)

        def pb4(job):
            return bank[BANK[job]][:, :].rearrange("p (a b) -> p a b", a=4)

        def index_head(per, i, j):
            return 2 * per * (i // 2) + i % 2 + 2 * j

        def flat(ap):
            return ap.rearrange("p a b -> p (a b)")

        def repeat(eng, n, turn, body):
            if n // turn:
                with eng.Fori(0, n // turn) as i:
                    for j in range(turn):
                        body(i, j)
            for j in range(n // turn * turn, n):
                body(0, j)

        made = {}

        def whereof(s):
            l, k = divmod(s, NSPLIT)
            return l * NBLK + [i for i, b in enumerate(BLOCKS) if b[2]][k]

        class Side:

            def __init__(self, eng, step):
                self.eng, self.step, self.n, self.last, self.l = eng, step, {}, None, 0

            def sig(self, ins, s=None, by=1):
                s = self.step if s is None else s
                ins.then_inc(s, by)
                self.n[s.name] = self.n.get(s.name, 0) + by
                self.last = s, self.n[s.name]

            def settle(self):
                self.eng.wait_ge(*self.last)

            def give(self, l, ins, name):
                self.sig(ins, S[name])
                made[(l, name)] = made.get((l, name), 0) + 1

            def need(self, l, name, k):
                assert 0 < k <= PER_LAYER[name], (name, k)
                self.eng.wait_ge(S[name], l * PER_LAYER[name] + k)

            def full(self, l, job):
                self.eng.wait_ge(bank_full[BANK[job]], l * USES[BANK[job]] + USE[job])

            def free(self, ins, job):
                b = BANK[job]
                ins.then_inc(bank_free[b], 1)
                self.last = bank_free[b], self.l * USES[b] + USE[job]

            def took(self, l, job):
                self.eng.wait_ge(bank_free[BANK[job]], l * USES[BANK[job]] + USE[job])

        block = ctx.enter_context(nc.Block())
        @block.sync
        def _(sp):
            def load(n):
                old = n - RAW
                if old >= 0 and BLOCKS[old % NBLK][2]:
                    sp.wait_ge(lo_done, split_no(old) + 1)
                elif old >= 0:
                    sp.wait_ge(whole_used, old - split_no(old) + 1)
                sp.dma_start(raw[n % RAW][:, :], w_d[n]).then_inc(landed[n % RAW], 16)

            sp.dma_start(X[:, :, :], x_d.rearrange("(t p) d -> p t d", p=P)).then_inc(x_in, 16)
            for l in range(DEPTH):
                base, loop_from = l * NBLK, l * NBLK + FIRST["uv"] + RAW
                for n in range(base, base + RAW):
                    load(n)
                if l:
                    sp.wait_ge(S["x_peer"], l)
                else:
                    sp.wait_ge(strip_out, 16)
                sp.dma_start(par, par_d[l]).then_inc(S["params"], 16)
                sp.dma_start(ms, mem_d.rearrange("(t p) d -> p t d", p=P)).then_inc(S["mem_in"], 16)
                for t in range(NT):
                    k = P * (t + 1)
                    src = bass.AP(strip_d.tensor, strip_d.offset + 255 - P * t,
                                  [[STRIP - 1, P], [P * STRIP, NHB], [1, k]])
                    sp.dma_start(bias[t], src).then_inc(S["bias"], 16)
                for n in range(base + RAW, loop_from):
                    load(n)

                def load_expert_block(i, j):
                    n = loop_from + j
                    sp.wait_ge(lo_done, i * TURN + (split_no(n - RAW) + 1))
                    src = w_d[bass.ds(i * TURN + n, 1), :, :].rearrange("o p n -> (o p) n")
                    sp.dma_start(raw[n % RAW][:, :], src).then_inc(landed[n % RAW], 16)

                repeat(sp, 2 * NKEY - RAW, TURN, load_expert_block)
            sp.wait_ge(S["x_peer"], DEPTH)
            sp.dma_start(out_d.rearrange("(t p) d -> p t d", p=P), X[:, :, :]).then_inc(out_done, 16)
            sp.wait_ge(out_done, 16)

        relb = sb("relb", [64, NHB])
        onehot = xn.rearrange("p t d -> p (t d)")[0:64, 0:STRIP]
        strip_sb = xn.rearrange("p t d -> p (t d)")[0:NHB, STRIP:2 * STRIP]

        @block.gpsimd
        def _(pool):
            nc.gpsimd.memset(relb[:, :], 1.0).then_inc(consts, 1)
            pool.wait_ge(consts, 1)
            pool.dma_start(relb[0:BUCKETS, :], relb_d).then_inc(strip_in, 16)
            pool.dma_start(onehot, onehot_d).then_inc(strip_in, 16)
            nc.gpsimd.memset(ident[:, :], 0.0).then_inc(consts, 1)
            pool.wait_ge(consts, 2)
            nc.gpsimd.affine_select(out=ident[:, :], in_=ident[:, :], compare_op=ALU.not_equal,
                                    fill=1.0, base=0, pattern=[[-1, P]],
                                    channel_multiplier=1).then_inc(consts, 1)
            nc.gpsimd.iota(iota_f, pattern=[[1, NKEY], [0, SET]], base=0, channel_multiplier=0,
                           allow_small_or_imprecise_dtypes=True).then_inc(consts, 1)
            nc.gpsimd.iota(iota16[:, :], pattern=[[1, PK]], base=0, channel_multiplier=0,
                           allow_small_or_imprecise_dtypes=True).then_inc(consts, 1)
            for n, s in enumerate((g_full, g_free, h_ready, a_done, y_full)):
                nc.gpsimd.memset(credit[:, n:n + 1], 0.0).then_inc(s, 2)
            pool.wait_ge(strip_sb_ready, 1)
            pool.dma_start(strip_d, strip_sb.unsqueeze(1).broadcast_to([NHB, P, STRIP])
                           ).then_inc(strip_out, 16)
            pool.wait_ge(strip_out, 16)

            def low(i, s):
                n = whereof(s)
                pool.wait_ge(hi_done, i * TURN + (s + 1))
                nc.gpsimd.tensor_tensor(wl[s % SPLIT][:, :], raw[n % RAW][:, :],
                                        wh[s % SPLIT][:, :].bitcast(F32),
                                        ALU.subtract).then_inc(lo_done, 1)

            for l in range(DEPTH):
                if l:
                    pool.wait_ge(S["x_peer"], l)
                nc.gpsimd.memset(score[:, :, :], 0.0).then_inc(S["score0"], 1)
                pool.wait_ge(S["score0"], 3 * l + 1)
                for t in range(NT):
                    k = P * (t + 1)
                    nc.gpsimd.affine_select(out=score[:, t, 0:k], in_=score[:, t, 0:k],
                                            compare_op=ALU.is_ge, fill=MASK, base=P * t,
                                            pattern=[[-1, k]],
                                            channel_multiplier=1).then_inc(S["score0"], 1)
                done = l * NSPLIT
                for s in range(done, done + 4):
                    low(0, s)
                pool.wait_ge(S["params"], 16 * (l + 1))
                ws = p_("ws").rearrange("p (g t) -> p g t", g=BG)
                nc.gpsimd.affine_select(out=ws, in_=ws, compare_op=ALU.is_ge, fill=0.0, base=0,
                                        pattern=[[0, BG], [1, P]],
                                        channel_multiplier=-1).then_inc(S["wmask"], 1)
                first = split_no(l * NBLK + FIRST["uv"])
                for s in range(done + 4, first):
                    low(0, s)
                repeat(pool, 2 * NKEY, TURN, lambda i, j: low(i, first + j))

        def stats(name):
            a, w, _ = ROOTS[name]
            return stat[:, a:a + w]

        RORD = {n: i + 1 for i, n in enumerate(["x", "m", "ck", "cq", "mk", "qa", "ka", "v", "ya",
                                                "y", "mq", "z"])}
        SQO = {n: NT * i for i, n in enumerate(SQUARES)}
        ROWS = {"x": 0, "m": 2, "y": 4, "z": 6}
        XHI = {"x": 0, "y": 8, "z": 16}
        assert sorted(RORD) == sorted(ROOTS)

        @block.scalar
        def _(act):
            A = Side(act, act_step)
            a_ = nc.scalar.activation

            def row_sumsq(l, src, name):
                for t in range(NT):
                    A.give(l, a_(xn[:, t, :], src[:, t, :], ACT.Square,
                                 accum_out=stats(name)[:, t:t + 1]), "sumsq")

            def root(l, name):
                A.need(l, "rms_in", RORD[name])
                A.give(l, a_(stats(name), stats(name), ACT.Sqrt), "rms_rt")

            def square(l, name, job=None):
                for t in range(NT):
                    n = l * NSQ + SQO[name] + t
                    if n >= 2:
                        act.wait_ge(S["sq_used"], n - 1)
                    if job:
                        A.full(l, f"{job}{t}")
                    A.give(l, a_(sq[n % 2], pb(f"{job}{t}")[:, :] if job else vg[:, t, :],
                                 ACT.Square), "sq")

            def copy_out(l, job, dst, src, func=ACT.Copy):
                A.full(l, job)
                A.free(a_(dst, src, func), job)

            def gain_out(l, job, dst, gain, i):
                A.full(l, job)
                A.sig(a_(dst[:, 2 * i, :], pb2(job)[:, 0, :], ACT.Copy,
                         scale=p_(gain, 2 * i, 2 * i + 1)))
                A.free(a_(dst[:, 2 * i + 1, :], pb2(job)[:, 1, :], ACT.Copy,
                          scale=p_(gain, 2 * i + 1, 2 * i + 2)), job)

            def high(i, s):
                n = whereof(s)
                if s >= SPLIT:
                    act.wait_ge(split_used, i * TURN + (s - SPLIT + 1))
                act.wait_ge(landed[n % RAW], i * (16 * TURN // RAW) + 16 * (n // RAW + 1))
                nc.scalar.copy(wh[s % SPLIT][:, :], raw[n % RAW][:, :]).then_inc(hi_done, 1)

            next_split = [0]

            def split_to(l, name, count, ahead=AHEAD):
                n = l * NBLK + FIRST[name] + count
                while ahead and BLOCKS[n % NBLK][2]:
                    n, ahead = n + 1, ahead - 1
                while next_split[0] < split_no(n):
                    high(0, next_split[0])
                    next_split[0] += 1

            def x_high(l, pre, gain):
                for i in range(4):
                    A.full(l, f"{pre}{i}")
                    for c in range(2):
                        k = 2 * i + c
                        A.give(l, a_(xh[:, k, :], pb2(f"{pre}{i}")[:, c, :], ACT.Copy,
                                     scale=p_(gain, k, k + 1)), "xhi")

            act.wait_ge(x_in, 16)
            act.wait_ge(strip_out, 16)
            for l in range(DEPTH):
                A.l = l
                split_to(l, "cs", SPLIT - 1, 0)
                if l:
                    act.wait_ge(S["x_peer"], l)
                row_sumsq(l, X, "x")
                root(l, "x")
                act.wait_ge(S["params"], 16 * (l + 1))
                x_high(l, "nx", "g_mix")
                act.wait_ge(S["mem_in"], 16 * (l + 1))
                row_sumsq(l, ms, "m")
                root(l, "m")
                split_to(l, "cs", 4)
                for t in range(NT):
                    A.full(l, f"cs{t}")
                    if l * NSQ + t >= 2:
                        act.wait_ge(S["sq_used"], l * NSQ + t - 1)
                    A.give(l, a_(sq[(l * NSQ + t) % 2][:, 0:P], pb(f"cs{t}")[:, 0:P], ACT.Square,
                                 accum_out=stats("ck")[:, t:t + 1]), "csq")
                root(l, "ck")
                for i in range(2):
                    split_to(l, "iq", 2 * i + 2)
                    copy_out(l, f"iq{i}", iqT[:, 2 * i:2 * i + 2, :], pb2(f"iq{i}"))
                split_to(l, "ik", 1)
                copy_out(l, "ik", ikT, pb("ik")[:, 0:SEQ])
                split_to(l, "cq", 4)
                for i in range(4):
                    gain_out(l, f"mx{i}", msT, "g_src", i)
                square(l, "cq", "cq")
                root(l, "cq")
                for n, job in enumerate(["is00", "is01", "is10", "is11", "is12", "is13"]):
                    if l * 6 + n >= 2:
                        act.wait_ge(S["relu_used"], l * 6 + n - 1)
                    copy_out(l, job, relu[n % 2], pb(job)[:, :], ACT.Relu)
                square(l, "mk", "mk")
                root(l, "mk")
                split_to(l, "qa", SPLIT - 1, 0)
                for t in range(NT):
                    copy_out(l, f"mv{t}", mv[:, t, :], pb(f"mv{t}")[:, :])
                split_to(l, "qa", 4)
                square(l, "qa", "qa")
                root(l, "qa")
                split_to(l, "ka", 4)
                square(l, "ka", "ka")
                root(l, "ka")
                split_to(l, "va", 4)
                for t in range(NT):
                    copy_out(l, f"va{t}", va[:, t, :], pb(f"va{t}")[:, :])
                split_to(l, "zv", 4)
                for t in range(NT):
                    copy_out(l, f"zv{t}", vg[:, t, :], pb(f"zv{t}")[:, :], ACT.Gelu)
                A.settle()
                square(l, "v")
                root(l, "v")
                for i in range(2):
                    split_to(l, "zu", 2 * i + 2)
                    copy_out(l, f"zu{i}", uT[:, 2 * i:2 * i + 2, :], pb2(f"zu{i}"), ACT.Gelu)
                for i in range(12):
                    split_to(l, "gts", 2 * i + 2)
                    copy_out(l, f"gt{i}", gates[:, 2 * i:2 * i + 2, :], pb2(f"gt{i}"), ACT.Sigmoid)
                A.need(l, "lam_s", 1)
                A.give(l, a_(lam[:, 0:2], lam[:, 0:2], ACT.Exp), "lam_e")
                for u in range(8):
                    k = P * (u % 2 + 1)
                    A.need(l, "a_max", u + 1)
                    for m in range(2):
                        e = a_(a_log[u % 2][:, m, 0:k], a_log[u % 2][:, m, 0:k], ACT.Exp,
                               bias=a_mx[:, u, m:m + 1], accum_out=a_sum[:, u, m:m + 1])
                        if m:
                            A.give(l, e, "a_exp")
                        else:
                            A.sig(e)
                for t in range(NT):
                    A.need(l, "c_max", t + 1)
                    A.give(l, a_(c_log[t], c_log[t], ACT.Exp), "c_exp")
                for h in range(AH):
                    copy_out(l, f"pT{h}", a_pT[h],
                             pb(f"pT{h}")[:, 0:3 * P].rearrange("p (a b) -> p a b", a=3))
                square(l, "ya", "ay")
                root(l, "ya")
                for i in range(3):
                    copy_out(l, f"ct{i}", c_pT[i], pb4(f"ct{i}"))
                for t in range(NT):
                    copy_out(l, f"cy{t}", ycT[:, :, t * P:(t + 1) * P], pb4(f"cy{t}"))
                split_to(l, "mq", 1, 0)
                A.took(l, "o3")
                row_sumsq(l, X, "y")
                root(l, "y")
                split_to(l, "mq", SPLIT, 0)
                x_high(l, "ny", "g_mem")
                split_to(l, "mq", 4)
                square(l, "mq", "mq")
                root(l, "mq")
                for t in range(NT):
                    A.need(l, "m_max", t + 1)
                    for h in range(MH):
                        job = f"ml{t}{h // 2}"
                        e = a_(m_e[t][:, h, :], pb2(job)[:, h % 2, :], ACT.Exp, scale=MD ** -0.5,
                               bias=m_mx[:, t, h:h + 1], accum_out=m_sum[:, t, h:h + 1])
                        if h % 2:
                            A.free(e, job)
                        else:
                            A.sig(e)
                for t in range(NT):
                    for k in range(NT):
                        copy_out(l, f"mp{t}{k}", m_pT[:, k, :, t * P:(t + 1) * P], pb4(f"mp{t}{k}"))
                for i in range(2):
                    copy_out(l, f"mo{i}", moT[:, 2 * i:2 * i + 2, :], pb2(f"mo{i}"))
                split_to(l, "pq", 1, 0)
                A.took(l, "w3")
                row_sumsq(l, X, "z")
                root(l, "z")
                split_to(l, "pq", SPLIT, 0)
                x_high(l, "nz", "g_peer")
                for i in range(8):
                    split_to(l, "pq", 2 * i + 2)
                    copy_out(l, f"pq{i}", pqT[:, 2 * i:2 * i + 2, :], pb2(f"pq{i}"))
                for t in range(NT):
                    for i in range(4):
                        copy_out(l, f"ps{t}{i}", ps[t][:, 4 * i:4 * i + 4, :], pb4(f"ps{t}{i}"))

                uv = split_no(l * NBLK + FIRST["uv"])
                assert next_split[0] == uv + AHEAD

                def high_ahead(i, k):
                    if uv + k + AHEAD < DEPTH * NSPLIT:
                        high(i, uv + k + AHEAD)

                def gelu(i, c):
                    act.wait_ge(a_full, i * TURN + (l * NKEY + c + 1))
                    half, n = divmod(c, HALF)
                    a_(gelus[half][:, bass.ds(i * TURN + n, 1), :].rearrange("p o t -> p (o t)"),
                       bank[4 + c % 2][:, 0:SEQ], ACT.Gelu).then_inc(a_done, 1)

                def take_gates(i, half, s, per):
                    act.wait_ge(g_full, i * per + ((2 * l + half) * 64 + s + 3))
                    nc.scalar.copy(G[half][:, bass.ds(i * (4 * per) + 4 * s, 4), :],
                                   bank[6 + s % 2][:, 0:4 * HALF].rearrange("p (t n) -> p t n", t=4)
                                   ).then_inc(g_free, 1)

                def up(i, c):
                    high_ahead(i, c + HALF * (c // HALF))
                    gelu(i, c)

                def up_gates(c0, half, per, s0=0):
                    def body(i, j):
                        up(i, c0 + j)
                        for q in range(per):
                            take_gates(i, half, s0 + per * j + q, TURN * per)
                    return body

                repeat(act, R1, TURN, up)
                for t in range(NT):
                    A.need(l, "r_sub", t + 1)
                    A.give(l, a_(cs[:, t], cs[:, t], ACT.Exp), "r_exp")
                for c in range(R1, R2):
                    up(0, c)
                A.took(l, "eT")
                A.took(l, "gT")
                repeat(act, HALF - R2, TURN, up_gates(R2, 0, 64 // (HALF - R2)))
                repeat(act, HALF, TURN, lambda i, j: high_ahead(i, HALF + j))
                act.wait_ge(h_ready, l * NKEY + HALF + 2)
                repeat(act, HALF, TURN, up_gates(HALF, 1, 1))
                repeat(act, HALF, TURN, lambda i, j: high_ahead(i, 3 * HALF + j))
                next_split[0] = min(uv + 4 * HALF + AHEAD, DEPTH * NSPLIT)

        @block.vector
        def _(dve):
            V = Side(dve, dve_step)
            v = nc.vector

            def inverse_rms(l, name, ready):
                _, _, n = ROOTS[name]
                ready()
                V.give(l, v.tensor_scalar(stats(name), stats(name), 1.0 / n, EPS, ALU.mult,
                                          ALU.add), "rms_in")
                V.need(l, "rms_rt", RORD[name])
                V.sig(v.reciprocal(stats(name), stats(name)))
                V.settle()

            def norm_rows(l, src, dst, name):
                inverse_rms(l, name, lambda: V.need(l, "sumsq", ROWS[name] + NT))
                for t in range(NT):
                    V.give(l, v.tensor_scalar(dst[:, t, :], src[:, t, :],
                                              stats(name)[:, t:t + 1], None, ALU.mult), "rows")

            def sum_squares(l, name, w):
                for t in range(NT):
                    n = SQO[name] + t
                    V.need(l, "sq", n + 1)
                    g = 512 // w
                    V.give(l, v.tensor_reduce(
                        out=stats(name)[:, t * g:(t + 1) * g],
                        in_=sq[(l * NSQ + n) % 2].rearrange("p (g w) -> p g w", w=w),
                        axis=AX, op=ALU.add), "sq_used")

            def norm_heads(l, name, job, dst, w):
                sum_squares(l, name, w)
                inverse_rms(l, name, V.settle)
                g = 512 // w
                for t in range(NT):
                    r = stats(name)[:, t * g:(t + 1) * g]
                    V.free(v.tensor_tensor(
                        dst[:, t, :].rearrange("p (g w) -> p g w", w=w),
                        pb(f"{job}{t}")[:, :].rearrange("p (g w) -> p g w", w=w),
                        r.unsqueeze(2).broadcast_to([P, g, w]), ALU.mult), f"{job}{t}")

            def x_low(l, name, pre, gain):
                for i in range(4):
                    V.need(l, "xhi", XHI[name] + 2 * i + 2)
                    for c in range(2):
                        k = 2 * i + c
                        o = v.scalar_tensor_tensor(
                            out=xl[:, k, :], in0=pb2(f"{pre}{i}")[:, c, :],
                            scalar=p_(gain, k, k + 1), in1=xh[:, k, :].bitcast(F32),
                            op0=ALU.mult, op1=ALU.subtract)
                        if c:
                            V.free(o, f"{pre}{i}")
                        else:
                            V.sig(o)

            def gain_all(l, job, dst, src, gain, more=None):
                V.full(l, job)
                V.free(v.tensor_scalar(dst, src, p_(gain), more, ALU.mult,
                                       ALU.mult if more is not None else ALU.bypass), job)

            def add_to_x(l, jobs):
                for n, job in enumerate(jobs):
                    t, h = n // 2, n % 2
                    xs = X[:, t, h * 512:(h + 1) * 512]
                    V.full(l, job)
                    V.free(v.tensor_tensor(xs, pb(job)[:, :], xs, ALU.add), job)

            dve.wait_ge(consts, 4)
            v.tensor_copy(iota[:, :, :], iota_f).then_inc(iota_ready, 1)
            dve.wait_ge(strip_mm, 1)
            v.tensor_copy(strip_sb, bank[0][0:NHB, 0:STRIP]).then_inc(strip_sb_ready, 1)
            dve.wait_ge(x_in, 16)
            dve.wait_ge(strip_out, 16)
            for l in range(DEPTH):
                V.l = l
                lam_init = 0.8 - 0.6 * math.exp(-0.3 * l)
                norm_rows(l, X, xn, "x")
                dve.wait_ge(S["params"], 16 * (l + 1))
                x_low(l, "x", "nx", "g_mix")
                for m in range(2):
                    V.sig(v.tensor_tensor(lamt[:, m, :], p_("lam", 2 * m * AD, (2 * m + 1) * AD),
                                          p_("lam", (2 * m + 1) * AD, (2 * m + 2) * AD), ALU.mult))
                V.settle()
                V.give(l, v.tensor_reduce(out=lam[:, 0:2], in_=lamt, axis=AX, op=ALU.add), "lam_s")
                norm_rows(l, ms, ms, "m")
                inverse_rms(l, "ck", lambda: V.need(l, "csq", NT))
                for t in range(NT):
                    job = f"cs{t}"
                    V.sig(v.tensor_scalar(ckn[:, t, :], pb(job)[:, 0:P], stats("ck")[:, t:t + 1],
                                          None, ALU.mult))
                    V.sig(v.tensor_copy(cv[:, t, :], pb(job)[:, P:2 * P]))
                    V.free(v.tensor_copy(iw[:, t, :], pb(job)[:, 2 * P:2 * P + IH]), job)
                norm_heads(l, "cq", "cq", cqn, CD)
                V.need(l, "score0", 3)
                n = 0
                for t in range(NT):
                    k = P * (t + 1)
                    per = 512 // k
                    for i in range(IH // per):
                        V.took(l, f"is{t}{i}")
                        for j in range(per):
                            h = index_head(per, i, j)
                            o = v.scalar_tensor_tensor(
                                out=score[:, t, 0:k], in0=relu[n % 2][:, j * k:(j + 1) * k],
                                scalar=iw[:, t, h:h + 1], in1=score[:, t, 0:k],
                                op0=ALU.mult, op1=ALU.add)
                            if j == per - 1:
                                V.give(l, o, "relu_used")
                            else:
                                V.sig(o)
                            V.settle()
                        n += 1
                norm_heads(l, "mk", "mk", mkn, MD)
                norm_heads(l, "qa", "qa", qan, AD)
                norm_heads(l, "ka", "ka", kan, AD)
                gain_all(l, "ckT", ckT, pb("ckT")[:, 0:SEQ], "ck")
                for i in range(2):
                    gain_all(l, f"cqT{i}", cqT[:, 2 * i:2 * i + 2, :], pb2(f"cqT{i}"), "cq")
                sum_squares(l, "v", P)
                inverse_rms(l, "v", V.settle)
                for t in range(NT):
                    x3 = vg[:, t, :].rearrange("p (g w) -> p g w", w=P)
                    V.give(l, v.tensor_tensor(x3, x3, stats("v")[:, 4 * t:4 * t + 4].unsqueeze(2)
                                              .broadcast_to([P, 4, P]), ALU.mult), "vn")
                for i in range(2):
                    gain_all(l, f"mkT{i}", mkT[:, 2 * i:2 * i + 2, :], pb2(f"mkT{i}"), "mk")
                for i in range(2):
                    gain_all(l, f"qT{i}", qaT[:, 2 * i:2 * i + 2, :], pb2(f"qT{i}"), "aq")
                for i in range(2):
                    gain_all(l, f"kT{i}", kaT[:, 2 * i:2 * i + 2, :], pb2(f"kT{i}"), "ak")
                for t in range(NT):
                    k = P * (t + 1)
                    for r in range(TOPK_C // 8):
                        V.sig(v.max(out=top8[:, :], in_=score[:, t, 0:k]))
                        V.settle()
                        V.sig(v.match_replace(out=score[:, t, 0:k], in_to_replace=top8[:, :],
                                              in_values=score[:, t, 0:k], imm_value=TAKEN))
                        V.settle()
                    V.give(l, v.tensor_scalar(pen[:, t, 0:k], score[:, t, 0:k], TAKEN / 2, MASK,
                                              ALU.is_gt, ALU.mult), "pen")
                dve.wait_ge(S["bias"], 32 * (l + 1))
                V.need(l, "lam_e", 1)
                V.sig(v.tensor_tensor(lam[:, 2:3], lam[:, 1:2], lam[:, 0:1], ALU.subtract))
                V.settle()
                V.sig(v.tensor_scalar(lam[:, 2:3], lam[:, 2:3], -lam_init, None, ALU.add))
                V.settle()

                def a_start(u):
                    h, t = divmod(u, 2)
                    k = P * (t + 1)
                    for m in range(2):
                        job = f"al{h}{m}"
                        V.full(l, job)
                        o = v.scalar_tensor_tensor(
                            out=a_log[u % 2][:, m, 0:k], in0=pb(job)[:, t * P:t * P + k],
                            scalar=AD ** -0.5, in1=bias[t][:, h, :], op0=ALU.mult, op1=ALU.add)
                        if t:
                            V.free(o, job)
                        else:
                            V.sig(o)
                    V.settle()
                    V.sig(v.tensor_reduce(out=a_mx[:, u, :], in_=a_log[u % 2][:, :, 0:k], axis=AX,
                                          op=ALU.max))
                    V.settle()
                    V.give(l, v.tensor_scalar(a_mx[:, u, :], a_mx[:, u, :], -1.0, None, ALU.mult),
                           "a_max")

                def a_end(u):
                    h, t = divmod(u, 2)
                    k = P * (t + 1)
                    V.need(l, "a_exp", u + 1)
                    V.sig(v.reciprocal(a_sum[:, u, :], a_sum[:, u, :]))
                    V.settle()
                    V.sig(v.tensor_tensor(a_sum[:, u, 1:2], a_sum[:, u, 1:2], lam[:, 2:3],
                                          ALU.mult))
                    V.settle()
                    V.sig(v.tensor_scalar(a_log[u % 2][:, 1, 0:k], a_log[u % 2][:, 1, 0:k],
                                          a_sum[:, u, 1:2], None, ALU.mult))
                    V.settle()
                    V.give(l, v.scalar_tensor_tensor(
                        out=a_pd[h][:, t, 0:k], in0=a_log[u % 2][:, 0, 0:k],
                        scalar=a_sum[:, u, 0:1], in1=a_log[u % 2][:, 1, 0:k],
                        op0=ALU.mult, op1=ALU.add), "pd")
                    V.settle()

                a_start(0)
                for u in range(8):
                    if u < 7:
                        a_start(u + 1)
                    a_end(u)
                for i in range(2):
                    V.full(l, f"sv{i}")
                    V.took(l, f"zu{i}")
                    for j in range(2):
                        g = 2 * i + j
                        o = v.scalar_tensor_tensor(
                            out=ybT[:, g, :].rearrange("p (c t) -> p c t", c=2),
                            in0=pb2(f"sv{i}")[:, j, :].rearrange("p (c t) -> p c t", c=2),
                            scalar=p_("bv", g, g + 1),
                            in1=p_("bs", g * P, (g + 1) * P).unsqueeze(1).broadcast_to([P, 2, P]),
                            op0=ALU.mult, op1=ALU.add)
                        if j:
                            V.free(o, f"sv{i}")
                        else:
                            V.sig(o)
                    V.settle()
                    for j in range(2):
                        g = 2 * i + j
                        V.give(l, v.tensor_tensor(ybT[:, g, :], ybT[:, g, :], uT[:, g, :],
                                                  ALU.mult), "yb")
                for t in range(NT):
                    k = P * (t + 1)
                    for n, job in enumerate(["cl0"] if t == 0 else ["cl1", "cl2"]):
                        hs = slice(0, 4) if t == 0 else slice(2 * n, 2 * n + 2)
                        V.full(l, job)
                        V.free(v.scalar_tensor_tensor(
                            out=c_log[t][:, hs, :],
                            in0=pb(job)[:, :].rearrange("p (h k) -> p h k", k=k),
                            scalar=CD ** -0.5, in1=bias[t][:, AH:, :][:, hs, :],
                            op0=ALU.mult, op1=ALU.add), job)
                    V.settle()
                    V.sig(v.tensor_tensor(c_log[t], c_log[t], pen[:, t, 0:k].unsqueeze(1)
                                          .broadcast_to([P, 4, k]), ALU.add))
                    V.settle()
                    V.sig(v.tensor_reduce(out=c_mx[:, t, :], in_=c_log[t], axis=AX, op=ALU.max))
                    V.settle()
                    V.give(l, v.tensor_tensor(c_log[t], c_log[t], c_mx[:, t, :].unsqueeze(2)
                                              .broadcast_to([P, 4, k]), ALU.subtract), "c_max")
                for t in range(NT):
                    k = P * (t + 1)
                    V.need(l, "c_exp", t + 1)
                    V.sig(v.tensor_reduce(out=c_sum[:, t, :], in_=c_log[t], axis=AX, op=ALU.add))
                    V.settle()
                    V.sig(v.reciprocal(c_sum[:, t, :], c_sum[:, t, :]))
                    V.settle()
                    V.give(l, v.tensor_tensor(c_log[t], c_log[t], c_sum[:, t, :].unsqueeze(2)
                                              .broadcast_to([P, 4, k]), ALU.mult), "c_p")
                norm_heads(l, "ya", "ay", ya, P)
                for i in range(2):
                    gain_all(l, f"yT{i}", yaT[:, 2 * i:2 * i + 2, :], pb2(f"yT{i}"), "asub",
                             1.0 - lam_init)
                V.took(l, "gt11")
                for i in range(4):
                    acc = merged[:, 2 * i:2 * i + 2, :]
                    for b, c in enumerate("abc"):
                        job = f"m{c}{i}"
                        V.full(l, job)
                        g = gates[:, b * KC + 2 * i:b * KC + 2 * i + 2, :]
                        V.free(v.tensor_tensor(acc if b == 0 else mtmp, pb2(job), g, ALU.mult), job)
                        V.settle()
                        if b == 1:
                            V.sig(v.tensor_tensor(acc, acc, mtmp, ALU.add))
                            V.settle()
                        if b == 2:
                            V.give(l, v.tensor_tensor(acc, acc, mtmp, ALU.add), "merged")
                add_to_x(l, [f"o{i}" for i in range(4)])
                norm_rows(l, X, xn, "y")
                x_low(l, "y", "ny", "g_mem")
                norm_heads(l, "mq", "mq", mqn, MD)
                for i in range(2):
                    gain_all(l, f"mqT{i}", mqT[:, 2 * i:2 * i + 2, :], pb2(f"mqT{i}"), "mq")
                for t in range(NT):
                    for i in range(2):
                        V.full(l, f"ml{t}{i}")
                        V.sig(v.tensor_reduce(out=m_mx[:, t, 2 * i:2 * i + 2], in_=pb2(f"ml{t}{i}"),
                                              axis=AX, op=ALU.max))
                    V.settle()
                    V.give(l, v.tensor_scalar(m_mx[:, t, :], m_mx[:, t, :], -MD ** -0.5, None,
                                              ALU.mult), "m_max")
                for t in range(NT):
                    V.took(l, f"ml{t}0")
                    V.took(l, f"ml{t}1")
                    V.sig(v.reciprocal(m_sum[:, t, :], m_sum[:, t, :]))
                    V.settle()
                    V.give(l, v.tensor_tensor(m_e[t], m_e[t], m_sum[:, t, :].unsqueeze(2)
                                              .broadcast_to([P, 4, SEQ]), ALU.mult), "m_p")
                add_to_x(l, [f"w{i}" for i in range(4)])
                norm_rows(l, X, xn, "z")
                x_low(l, "z", "nz", "g_peer")
                for t in range(NT):
                    for i in range(4):
                        V.took(l, f"ps{t}{i}")
                for t in range(NT):

                    def sixteen(n, src, vals, idx):
                        for at in (slice(0, 8), slice(8, 16)):
                            for c in range(n):
                                V.sig(v.max(out=vals[:, c, at], in_=src[:, c, :]))
                            V.settle()
                            for c in range(n):
                                V.sig(v.max_index(out=idx[:, c, at], in_max=vals[:, c, at],
                                                  in_values=src[:, c, :]))
                            V.settle()
                            if at.start == 0:
                                for c in range(n):
                                    V.sig(v.match_replace(
                                        out=src[:, c, :], in_to_replace=vals[:, c, at],
                                        in_values=src[:, c, :], imm_value=TAKEN))
                                V.settle()

                    sixteen(16, ps[t], v16[:, t], i16[:, t])
                    V.sig(v.tensor_copy(i16f[:, t], i16[:, t]))
                    vv = v16[:, t].rearrange("p (h two) k -> p h two k", two=2)
                    V.sig(v.tensor_tensor(
                        cand.rearrange("p h (i j) -> p h i j", i=PK),
                        vv[:, :, 0, :].unsqueeze(3).broadcast_to([P, PH, PK, PK]),
                        vv[:, :, 1, :].unsqueeze(2).broadcast_to([P, PH, PK, PK]), ALU.add))
                    V.settle()
                    sixteen(PH, cand, cs[:, t], ci[:, t])
                    V.sig(v.tensor_copy(rstat[:, t, 0, :], cs[:, t, :, 0]))
                    V.settle()
                    V.give(l, v.tensor_tensor(cs[:, t], cs[:, t], rstat[:, t, 0, :].unsqueeze(2)
                                              .broadcast_to([P, PH, PK]), ALU.subtract), "r_sub")
                    ii = i16f[:, t].rearrange("p (h two) k -> p h two k", two=2)
                    cit = ci[:, t].rearrange("p h k -> p (h k)")
                    for part in range(2):
                        if part == 0:
                            V.sig(v.tensor_scalar(half_u[:, t, :], cit, 4, None,
                                                  ALU.logical_shift_right))
                        else:
                            V.sig(v.tensor_scalar(half_u[:, t, :], cit, 15, None, ALU.bitwise_and))
                        V.settle()
                        V.sig(v.tensor_copy(half_f[:, t, :], half_u[:, t, :]))
                        V.settle()
                        V.sig(v.tensor_tensor(
                            eq, half_f[:, t, :].unsqueeze(2).broadcast_to([P, P, PK]),
                            iota16[:, :].unsqueeze(1).broadcast_to([P, P, PK]), ALU.is_equal))
                        V.settle()
                        eq4 = eq.rearrange("p (h k) i -> p h k i", h=PH)
                        V.sig(v.tensor_tensor(eq4, eq4, ii[:, :, part, :].unsqueeze(2)
                                              .broadcast_to([P, PH, PK, PK]), ALU.mult))
                        V.settle()
                        V.sig(v.tensor_reduce(out=etok[:, part, t, :], in_=eq, axis=AX, op=ALU.add))
                        V.settle()
                    V.need(l, "r_exp", t + 1)
                    V.sig(v.tensor_reduce(out=rstat[:, t, 1, :], in_=cs[:, t], axis=AX, op=ALU.add))
                    V.settle()
                    V.sig(v.reciprocal(rstat[:, t, 1, :], rstat[:, t, 1, :]))
                    V.settle()
                    V.give(l, v.tensor_tensor(
                        gate[:, t, :].rearrange("p (h k) -> p h k", h=PH), cs[:, t],
                        rstat[:, t, 1, :].unsqueeze(2).broadcast_to([P, PH, PK]), ALU.mult),
                        "route")
                V.full(l, "eT")
                V.sig(v.tensor_copy(choices[:, 0, :], pb2("eT")[:, 0, :]))
                V.free(v.tensor_copy(choices[:, 1, :], pb2("eT")[:, 1, :]), "eT")
                V.full(l, "gT")
                V.sig(v.tensor_copy(choices[:, 2, :], pb("gT")[:, 0:SEQ]))
                V.settle()
                V.free(v.tensor_tensor(hid[0], pb("gT")[:, 0:SEQ], choices[:, 2, :],
                                       ALU.subtract), "gT")
                V.settle()
                V.sig(v.tensor_copy(choices[:, 3, :], hid[0]))
                V.settle()
                V.sig(v.tensor_tensor(choices[:, 4, :], hid[0], choices[:, 3, :], ALU.subtract))
                V.settle()

                def one_hots(half):
                    per = SOME // SET
                    with dve.Fori(0, SEQ // SOME) as i:
                        v.tensor_copy(some[:, :, :],
                                      choices[:, :, bass.ds(i * SOME, SOME)]).then_inc(toks, 1)
                        dve.wait_ge(toks, i + ((2 * l + half) * (SEQ // SOME) + 1))
                        for s in range(per):
                            at = i * per + ((2 * l + half) * 64 + s + 1)
                            e1, e2 = [some[:, a, s * SET:(s + 1) * SET].unsqueeze(1) for a in (0, 1)]
                            gates_s = some[:, 2:5, s * SET:(s + 1) * SET].unsqueeze(2)
                            dve.wait_ge(g_full, at)
                            v.tensor_tensor(chosen[s % 2], iota[:, half * HALF:(half + 1) * HALF, :],
                                            e2.broadcast_to([P, HALF, SET]),
                                            ALU.is_equal).then_inc(chosen_done, 1)
                            v.tensor_tensor(oh1[s % 2], iota[:, :, :],
                                            e1.broadcast_to([P, NKEY, SET]), ALU.is_equal)
                            dve.wait_ge(chosen_done, at)
                            v.tensor_tensor(
                                oh2[s % 2],
                                chosen[s % 2].unsqueeze(1).broadcast_to([P, 3, HALF, SET]),
                                gates_s.broadcast_to([P, 3, HALF, SET]),
                                ALU.mult).then_inc(oh_ready, 1)
                        dve.wait_ge(oh_ready, i * per + ((2 * l + half) * 64 + per))
                    dve.wait_ge(g_free, (2 * l + half + 1) * 64 + 2)

                def hidden(i, c):
                    half, n = divmod(c, HALF)
                    at = i * TURN + (l * NKEY + c + 1)
                    col = bass.ds(i * TURN + n, 1)
                    dve.wait_ge(a_done, at + 2)
                    v.tensor_tensor(hid[c % 2], gelus[half][:, col, :].rearrange("p o t -> p (o t)"),
                                    G[half][:, :, col].rearrange("p t o -> p (t o)"),
                                    ALU.mult).then_inc(hid_m, 1)
                    dve.wait_ge(hid_m, at)
                    dve.wait_ge(y_full, at)
                    v.tensor_copy(hh[c % 2][:, :], hid[c % 2]).then_inc(hid_h, 1)
                    dve.wait_ge(hid_h, at)
                    v.tensor_tensor(hl[c % 2][:, :], hid[c % 2], hh[c % 2][:, :].bitcast(F32),
                                    ALU.subtract).then_inc(h_ready, 1)

                for half in range(2):
                    one_hots(half)
                    repeat(dve, HALF, TURN, lambda i, j: hidden(i, HALF * half + j))
                dve.wait_ge(y_full, (l + 1) * NKEY + 2)
                for n in range(4):
                    t, h = n // 2, n % 2
                    xs = X[:, t, h * 512:(h + 1) * 512]
                    o = v.tensor_tensor(xs, bank[n][:, :], xs, ALU.add)
                    if n == 3:
                        V.give(l, o, "x_peer")
                    else:
                        V.sig(o)
                V.settle()

        @block.tensor
        def _(pe):
            T = Side(pe, None)
            mm_, tr_ = nc.tensor.matmul, nc.tensor.transpose
            blk = [0]
            owed = []

            def mm(out, lhsT, rhs, start, stop, sem=None):
                o = mm_(out, lhsT, rhs, start=start, stop=stop)
                if sem is not None:
                    o.then_inc(sem, 1)
                elif owed:
                    o.then_inc(owed.pop(0), 1)
                return o

            def mm3(out, w, x, start, stop, sem=None):
                (wH, wL), (xH, xL) = w, x
                mm(out, wH, xH, start, False)
                mm(out, wH, xL, False, False)
                mm(out, wL, xH, False, stop, sem)

            def x_parts(*at):
                return xh[(slice(None),) + at], xl[(slice(None),) + at]

            def begin(l, job):
                n = l * USES[BANK[job]] + USE[job] - 1
                if n:
                    pe.wait_ge(bank_free[BANK[job]], n)

            def fullsem(job):
                return bank_full[BANK[job]]

            def whole_block():
                n = blk[0]
                blk[0] += 1
                assert not BLOCKS[n % NBLK][2]
                pe.wait_ge(landed[n % RAW], 16 * (n // RAW + 1))
                return raw[n % RAW][:, :]

            def split_block():
                n = blk[0]
                blk[0] += 1
                assert BLOCKS[n % NBLK][2]
                s = split_no(n)
                pe.wait_ge(lo_done, s + 1)
                return wh[s % SPLIT][:, :], wl[s % SPLIT][:, :]

            def transposes(l, job, pairs):
                begin(l, job)
                for n, src in enumerate(pairs):
                    o = tr_(pb(job)[:, n * P:(n + 1) * P], src, ident[:, :])
                    if owed and owed[0] is whole_used and n < len(pairs) - 1:
                        o.then_inc(owed.pop(0), 1)
                o.then_inc(fullsem(job), 1)

            def rows_T(l, pre, src):
                for i in range(4):
                    transposes(l, f"{pre}{i}", [src[:, t, c * P:(c + 1) * P]
                                                for c in (2 * i, 2 * i + 1) for t in range(NT)])

            def heads_T(l, pre, src):
                for i in range(2):
                    transposes(l, f"{pre}{i}", [src[:, t, c * P:(c + 1) * P]
                                                for c in (2 * i, 2 * i + 1) for t in range(NT)])

            def token_major(l, job, w=512, srcT=None):
                for t in range(NT):
                    begin(l, f"{job}{t}")
                for b in range(4):
                    ws = [whole_block()] if srcT is not None else split_block()
                    ws = [x.rearrange("p (k n) -> p k n", k=2) for x in ws]
                    for t in range(NT):
                        out = pb(f"{job}{t}")[:, 0:w]
                        for kk in range(2):
                            k = 2 * b + kk
                            end = k == KC - 1
                            signal = fullsem(f"{job}{t}") if end else None
                            rows = slice(t * P, (t + 1) * P)
                            if srcT is not None:
                                mm(out, srcT[:, k, rows], ws[0][:, kk, 0:w], k == 0, end, signal)
                            else:
                                mm3(out, x_parts(k, rows), [x[:, kk, 0:w] for x in ws], k == 0,
                                    end, signal)
                    owed.append(whole_used if srcT is not None else split_used)

            def columns_of(out, ws, signal=None):
                for k in range(KC):
                    mm3(out, [x[:, k * P:(k + 1) * P] for x in ws], x_parts(k, slice(0, SEQ)),
                        k == 0, k == KC - 1, signal if k == KC - 1 else None)

            def transposed(l, job, n=2):
                begin(l, job)
                for c in range(n):
                    columns_of(pb2(job)[:, c, :], split_block(), fullsem(job) if c == n - 1 else None)
                    owed.append(split_used)

            def half_rows(l, jobs, srcT, kc):
                for job in jobs:
                    begin(l, job)
                for k in range(kc):
                    wt = whole_block()
                    for n, job in enumerate(jobs):
                        t, h = n // 2, n % 2
                        end = k == kc - 1
                        mm(pb(job)[:, :], srcT[:, k, t * P:(t + 1) * P],
                           wt[:, h * 512:(h + 1) * 512], k == 0, end, fullsem(job) if end else None)
                    owed.append(whole_used)

            pe.wait_ge(consts, 5)
            pe.wait_ge(strip_in, 32)
            mm_(bank[0][0:NHB, 0:STRIP], relb[:, :], onehot, start=True,
                stop=True).then_inc(strip_mm, 1)
            pe.wait_ge(strip_sb_ready, 1)
            for l in range(DEPTH):
                T.need(l, "rows", ROWS["x"] + NT)
                rows_T(l, "nx", xn)
                for i in range(4):
                    T.took(l, f"nx{i}")
                token_major(l, "cs", 2 * P + IH)
                for i in range(2):
                    transposed(l, f"iq{i}")
                transposed(l, "ik", 1)
                token_major(l, "cq")
                T.need(l, "rows", ROWS["m"] + NT)
                rows_T(l, "mx", ms)
                T.took(l, "iq0")
                T.took(l, "iq1")
                T.took(l, "ik")
                for t in range(NT):
                    k = P * (t + 1)
                    per = 512 // k
                    for i in range(IH // per):
                        job = f"is{t}{i}"
                        begin(l, job)
                        for j in range(per):
                            h = index_head(per, i, j)
                            r = slice(64 * (h % 2), 64 * (h % 2) + 64)
                            mm(pb(job)[:, j * k:(j + 1) * k], iqT[r, h // 2, t * P:(t + 1) * P],
                               ikT[r, 0:k], True, True, fullsem(job) if j == per - 1 else None)
                for i in range(4):
                    T.took(l, f"mx{i}")
                token_major(l, "mk", srcT=msT)
                token_major(l, "mv", srcT=msT)
                token_major(l, "qa")
                token_major(l, "ka")
                T.took(l, "cs0")
                T.took(l, "cs1")
                transposes(l, "ckT", [ckn[:, t, :] for t in range(NT)])
                T.took(l, "cq1")
                T.took(l, "cq0")
                heads_T(l, "cqT", cqn)
                token_major(l, "va")
                token_major(l, "zv")
                T.took(l, "mk0")
                T.took(l, "mk1")
                heads_T(l, "mkT", mkn)
                for t in range(NT):
                    T.took(l, f"qa{t}")
                    T.took(l, f"ka{t}")
                heads_T(l, "qT", qan)
                heads_T(l, "kT", kan)
                for i in range(2):
                    transposed(l, f"zu{i}")
                for i in range(12):
                    transposed(l, f"gt{i}")
                for i in range(2):
                    T.took(l, f"qT{i}")
                    T.took(l, f"kT{i}")
                for h in range(AH):
                    for m in range(2):
                        job = f"al{h}{m}"
                        begin(l, job)
                        r = slice(64 * m, 64 * m + 64)
                        for t in range(NT):
                            k = P * (t + 1)
                            mm(pb(job)[:, t * P:t * P + k], qaT[r, h, t * P:(t + 1) * P],
                               kaT[r, h, 0:k], True, True, fullsem(job) if t else None)
                T.need(l, "vn", NT)
                T.need(l, "wmask", 1)
                for i in range(2):
                    job = f"sv{i}"
                    begin(l, job)
                    for j in range(2):
                        for c in range(NT):
                            g = 2 * i + j
                            mm(pb2(job)[:, j, c * P:(c + 1) * P], vg[:, c, g * P:(g + 1) * P],
                               p_("ws", g * P, (g + 1) * P), True, True,
                               fullsem(job) if j and c else None)
                T.took(l, "ckT")
                T.took(l, "cqT0")
                T.took(l, "cqT1")
                for job, t, hs in (("cl0", 0, range(4)), ("cl1", 1, range(2)),
                                   ("cl2", 1, range(2, 4))):
                    k = P * (t + 1)
                    begin(l, job)
                    for n, h in enumerate(hs):
                        mm(pb(job)[:, n * k:(n + 1) * k], cqT[:, h, t * P:(t + 1) * P],
                           ckT[:, 0:k], True, True, fullsem(job) if h == hs[-1] else None)
                for h in range(AH):
                    T.need(l, "pd", 2 * h + 2)
                    transposes(l, f"pT{h}", [a_pd[h][:, 0, 0:P], a_pd[h][:, 1, 0:P],
                                             a_pd[h][:, 1, P:2 * P]])
                T.took(l, "va0")
                T.took(l, "va1")
                for t in range(NT):
                    begin(l, f"ay{t}")
                for h in range(AH):
                    T.took(l, f"pT{h}")
                    vh = va[:, :, h * P:(h + 1) * P]
                    end = h == AH - 1
                    mm(pb("ay0")[:, h * P:(h + 1) * P], a_pT[h][:, 0, :], vh[:, 0, :], True, True,
                       fullsem("ay0") if end else None)
                    mm(pb("ay1")[:, h * P:(h + 1) * P], a_pT[h][:, 1, :], vh[:, 0, :], True, False)
                    mm(pb("ay1")[:, h * P:(h + 1) * P], a_pT[h][:, 2, :], vh[:, 1, :], False, True,
                       fullsem("ay1") if end else None)
                T.need(l, "c_p", 1)
                transposes(l, "ct0", [c_log[0][:, h, :] for h in range(CH)])
                T.need(l, "c_p", 2)
                for c in range(NT):
                    transposes(l, f"ct{c + 1}", [c_log[1][:, h, c * P:(c + 1) * P]
                                                 for h in range(CH)])
                begin(l, "cy0")
                T.took(l, "ct0")
                mm(pb("cy0")[:, :], cv[:, 0, :], flat(c_pT[0]), True, True, fullsem("cy0"))
                begin(l, "cy1")
                for c in range(NT):
                    T.took(l, f"ct{c + 1}")
                    mm(pb("cy1")[:, :], cv[:, c, :], flat(c_pT[c + 1]), c == 0, c == 1,
                       fullsem("cy1") if c else None)
                T.took(l, "ay0")
                T.took(l, "ay1")
                heads_T(l, "yT", ya)
                T.took(l, "yT0")
                T.took(l, "yT1")
                T.need(l, "yb", 4)
                T.took(l, "cy0")
                T.took(l, "cy1")
                for i in range(4):
                    for b, src in (("a", yaT), ("b", ybT), ("c", ycT)):
                        job = f"m{b}{i}"
                        begin(l, job)
                        wt = whole_block().rearrange("p (c k n) -> p c k n", c=2, k=4)
                        for c in range(2):
                            for k in range(4):
                                mm(pb2(job)[:, c, :], wt[:, c, k, :], src[:, k, :], k == 0, k == 3,
                                   fullsem(job) if c and k == 3 else None)
                        owed.append(whole_used)
                for i in range(4):
                    T.need(l, "merged", i + 1)
                half_rows(l, [f"o{i}" for i in range(4)], merged, KC)
                T.need(l, "rows", ROWS["y"] + NT)
                rows_T(l, "ny", xn)
                for i in range(4):
                    T.took(l, f"ny{i}")
                token_major(l, "mq")
                T.took(l, "mq0")
                T.took(l, "mq1")
                heads_T(l, "mqT", mqn)
                for i in range(2):
                    T.took(l, f"mqT{i}")
                    T.took(l, f"mkT{i}")
                for t in range(NT):
                    for i in range(2):
                        job = f"ml{t}{i}"
                        begin(l, job)
                        for j in range(2):
                            h = 2 * i + j
                            mm(pb2(job)[:, j, :], mqT[:, h, t * P:(t + 1) * P], mkT[:, h, :],
                               True, True, fullsem(job) if j else None)
                for t in range(NT):
                    T.need(l, "m_p", t + 1)
                    for k in range(NT):
                        transposes(l, f"mp{t}{k}", [m_e[t][:, h, k * P:(k + 1) * P]
                                                    for h in range(MH)])
                for t in range(NT):
                    T.took(l, f"mv{t}")
                    for k in range(NT):
                        T.took(l, f"mp{t}{k}")
                for i in range(2):
                    begin(l, f"mo{i}")
                    for j in range(2):
                        h = 2 * i + j
                        for k in range(NT):
                            mm(pb2(f"mo{i}")[:, j, :], mv[:, k, h * P:(h + 1) * P], m_pT[:, k, h, :],
                               k == 0, k == 1, fullsem(f"mo{i}") if j and k else None)
                T.took(l, "mo0")
                T.took(l, "mo1")
                half_rows(l, [f"w{i}" for i in range(4)], moT, 4)
                T.need(l, "rows", ROWS["z"] + NT)
                rows_T(l, "nz", xn)
                for i in range(4):
                    T.took(l, f"nz{i}")
                for i in range(8):
                    transposed(l, f"pq{i}")
                for i in range(8):
                    T.took(l, f"pq{i}")
                for t in range(NT):
                    for i in range(4):
                        job = f"ps{t}{i}"
                        begin(l, job)
                        for j in range(4):
                            c = 4 * i + j
                            mm(pb4(job)[:, j, :], pqT[:, c, t * P:(t + 1) * P],
                               p_("sk", (c % 2) * NKEY, (c % 2 + 1) * NKEY), True, True,
                               fullsem(job) if j == 3 else None)
                for b in range(8):
                    pe.wait_ge(bank_free[b], l * USES[b] + BEFORE_LOOPS[b])
                uv = split_no(l * NBLK + FIRST["uv"])
                assert split_no(blk[0]) == uv and not owed

                def expert_block(i, k):
                    s = uv + k
                    pe.wait_ge(lo_done, i * TURN + (s + 1))
                    return wh[s % SPLIT][:, :], wl[s % SPLIT][:, :]

                def up(i, c):
                    ws = expert_block(i, c + HALF * (c // HALF))
                    pe.wait_ge(a_done, i * TURN + (l * NKEY + c + 1))
                    columns_of(bank[4 + c % 2][:, 0:SEQ], ws, a_full)
                    owed.append(split_used)

                def gate_set(i, half, s, per):
                    at = i * per + ((2 * l + half) * 64 + s + 1)
                    pe.wait_ge(oh_ready, at)
                    pe.wait_ge(g_free, at)
                    for q in range(4):
                        for g in range(3):
                            mm(bank[6 + s % 2][:, q * HALF:(q + 1) * HALF], oh1[s % 2][:, :, q],
                               oh2[s % 2][:, g, :, q], g == 0, g == 2,
                               g_full if q == 3 and g == 2 else None)

                def up_gates(c0, half, per):
                    def body(i, j):
                        up(i, c0 + j)
                        for q in range(per):
                            gate_set(i, half, per * j + q, TURN * per)
                    return body

                def down(i, c, start=False, stop=False):
                    vH, vL = expert_block(i, c + HALF * (c // HALF + 1))
                    pe.wait_ge(h_ready, i * TURN + (l * NKEY + c + 3))
                    for m in range(4):
                        t, h = m // 2, m % 2
                        rows, cols = slice(t * P, (t + 1) * P), slice(h * 512, (h + 1) * 512)
                        mm3(bank[m][:, :], (hh[c % 2][:, rows], hl[c % 2][:, rows]),
                            (vH[:, cols], vL[:, cols]), start, stop, y_full if m == 3 else None)
                    owed.append(split_used)

                def peeled(n, body):
                    body(0, 0)
                    repeat(pe, n - 1, TURN, lambda i, j: body(i, 1 + j))

                peeled(R1, up)
                for c in range(R1, R2):
                    up(0, c)
                T.need(l, "route", NT)
                transposes(l, "eT", [etok[:, part, t, :] for part in range(2) for t in range(NT)])
                transposes(l, "gT", [gate[:, t, :] for t in range(NT)])
                peeled(HALF - R2, up_gates(R2, 0, 64 // (HALF - R2)))
                pe.wait_ge(bank_free[0], (l + 1) * USES[0])
                pe.wait_ge(bank_free[1], (l + 1) * USES[1])
                down(0, 0, start=True)
                repeat(pe, HALF - 1, TURN, lambda i, j: down(i, 1 + j))
                peeled(HALF, up_gates(HALF, 1, 1))
                peeled(HALF - 1, lambda i, j: down(i, HALF + j))
                down(0, NKEY - 1, stop=True)
                blk[0] = (l + 1) * NBLK
        for (l, name), n in made.items():
            assert n == PER_LAYER[name], (l, name, n)


def strip_selector():
    import numpy as np
    n = 255 - np.arange(STRIP)
    exact = BUCKETS // 2
    nf = np.maximum(n, 1).astype(np.float32)
    large = exact + (np.log(nf / exact) / math.log(MAXDIST / exact) * (BUCKETS - exact)).astype(np.int32)
    b = np.where(n < exact, np.maximum(n, 0), np.minimum(large, BUCKETS - 1))
    out = np.zeros((64, STRIP), np.float32)
    out[b, np.arange(STRIP)] = 1.0
    out[BUCKETS, n < 0] = MASK
    return out


def kernel(**inputs):
    import numpy as np
    import concourse.bacc as bacc
    from concourse.bass_utils import run_bass_kernel_spmd

    a = {k: np.asarray(v) for k, v in inputs.items()}

    def token_major(w):
        return w.reshape(4, 2, P, 512).transpose(0, 2, 1, 3).reshape(4, P, 1024)

    def columns(w):
        n = w.shape[1] // P
        return w.reshape(KC, P, n, P).transpose(2, 1, 0, 3).reshape(n, P, 1024)

    def rows(w):
        return w.reshape(-1, P, 1024)

    def branch(w):
        return w.reshape(4, P, 4, 2, P).transpose(2, 1, 3, 0, 4).reshape(4, P, 1024)

    def cols(w):
        return w.reshape(-1, P).T

    blocks = np.empty((DEPTH * NBLK, P, 1024), np.float32)
    par = np.empty((DEPTH, P, NPAR), np.float32)
    widths = [512] * 6 + [CD, CD, IH * ID, ID, IH, 3 * D]
    for l in range(DEPTH):
        qa, ka, va, zu, zv, cq, ck, cv, iq, ik, iw, gts = np.split(
            a["w_in"][l], np.cumsum(widths)[:-1], axis=1)
        u = a["p_u"][l].reshape(NKEY, NKEY, KC, P).transpose(1, 3, 2, 0).reshape(NKEY, P, 1024)
        v = a["p_v"][l].reshape(NKEY, NKEY, D).transpose(1, 0, 2)
        kv = a["m_wkv"][l]
        small = np.concatenate([ck, cv, iw, np.zeros((D, 512 - 2 * CD - IH), np.float32)], 1)
        br = [branch(a[f"w_br_{c}"][l]) for c in "abc"]
        parts = dict(
            cs=token_major(small), iq=columns(iq), ik=columns(np.concatenate([ik, ik], 1)),
            cq=token_major(cq), qa=token_major(qa), ka=token_major(ka), va=token_major(va),
            zv=token_major(zv), zu=columns(zu), gts=columns(gts),
            mk=token_major(kv[:, :512]), mv=token_major(kv[:, 512:]),
            br=np.stack(br, 1).reshape(12, P, 1024), mix_out=rows(a["w_mix_out"][l]),
            mq=token_major(a["m_wq"][l]), mo=rows(a["m_wo"][l]), pq=columns(a["p_wq"][l]))
        at = l * NBLK
        for name, n, _ in STREAM[:-1]:
            assert parts[name].shape[0] == n
            blocks[at:at + n] = parts[name]
            at += n
        for half in range(2):
            for w in (u, v):
                blocks[at:at + HALF] = w[half * HALF:(half + 1) * HALF]
                at += HALF
        everywhere = lambda w: np.broadcast_to(w.reshape(1, -1), (P, w.size))
        small = dict(
            g_mix=cols(a["norm_mix"][l]), g_mem=cols(a["norm_mem"][l]),
            g_src=cols(a["norm_memsrc"][l]), g_peer=cols(a["norm_peer"][l]),
            aq=cols(np.tile(a["a_q_gain"][l], 2)), ak=cols(np.tile(a["a_k_gain"][l], 2)),
            cq=cols(a["c_q_gain"][l]), ck=cols(a["c_k_gain"][l]), mq=cols(a["m_q_gain"][l]),
            mk=cols(a["m_k_gain"][l]), asub=cols(a["a_subln_gain"][l]), bv=cols(a["b_v_gain"][l]),
            ws=a["b_w_s"][l].transpose(2, 0, 1).reshape(P, BG * P),
            bs=everywhere(a["b_b_s"][l]),
            lam=everywhere(np.concatenate([a[k][l] for k in ("a_lq1", "a_lk1", "a_lq2", "a_lk2")])),
            sk=np.concatenate([a["p_subkey1"][l].T, a["p_subkey2"][l].T], 1))
        for name, (lo, hi) in PAR.items():
            par[l, :, lo:hi] = small[name]

    nc = bacc.Bacc("TRN2", target_bir_lowering=False, num_devices=1)
    arrays = dict(x=a["x"].reshape(SEQ, D), mem=a["mem"].reshape(SEQ, D), rel_bias=a["rel_bias"],
                  selector=strip_selector(), par=par, blocks=blocks)
    args = [nc.dram_tensor(n, w.shape, F32, kind="ExternalInput").ap() for n, w in arrays.items()]
    out = nc.dram_tensor("out", (SEQ, D), F32, kind="ExternalOutput").ap()
    strip = nc.dram_tensor("strip", (NHB, P, STRIP), F32).ap()
    build(nc, *args, out, strip)
    r = run_bass_kernel_spmd(nc, [{n: np.ascontiguousarray(w) for n, w in arrays.items()}],
                             core_ids=[0])
    return np.asarray(r.results[0]["out"]).reshape(1, SEQ, D)
```

```python
import math
from contextlib import ExitStack

import concourse.bass as bass
from concourse import mybir

F32 = mybir.dt.float32
F32R = mybir.dt.float32r
U32 = mybir.dt.uint32
BF16 = mybir.dt.bfloat16
ACT = mybir.ActivationFunctionType
ALU = mybir.AluOpType
AX = mybir.AxisListType.X

P = 128
D = 1024
SEQ = 256
NT = SEQ // P
DEPTH = 2
KC = D // P
AH, AD = 4, 64
CH, CD = 4, 128
IH, ID = 8, 64
MH, MD = 4, 128
BG = 4
TOPK_C = 64
PH, PK, NKEY = 8, 16, 128
BUCKETS, MAXDIST = 32, 128
NHB = AH + CH
EPS = 1e-6
MASK = -1e30
TAKEN = -3e38
RAW = 3
SPLIT = 3
AHEAD = 2
TURN = 6
R1, R2, R3 = 34, 38, 40
SET = 4
GATE_STEPS = ((16, 3), (8, 2)), ((64, 1),)
SOME = 64
HALF = NKEY // 2
STRIP = 3 * P

PARTS = [("g_mix", 8), ("g_mem", 8), ("g_src", 8), ("g_peer", 8), ("aq", 1), ("ak", 1), ("cq", 1),
         ("ck", 1), ("mq", 1), ("mk", 1), ("asub", 1), ("bv", 4), ("ws", BG * P), ("bs", BG * P),
         ("lam", 4 * AD), ("sk", 2 * NKEY)]
PAR = {}
NPAR = 0
for _n, _w in PARTS:
    PAR[_n] = (NPAR, NPAR + _w)
    NPAR += _w

STREAM = [("cs", 4, 1), ("iq", 4, 1), ("ik", 1, 1), ("cq", 4, 1),
          ("qa", 4, 1), ("ka", 4, 1), ("va", 4, 1), ("zv", 4, 1), ("zu", 4, 1), ("gts", 24, 1),
          *[(f"br_{b}{i}", 1, b != "c") for i in range(4) for b in "bca"], ("mix_out", 8, 1),
          ("mk", 4, 0), ("mq", 4, 1), ("mv", 4, 0), ("mo", 4, 1), ("pq", 16, 1),
          ("uv", 2 * NKEY, 1)]
BLOCKS = [(_n, _i, _s) for _n, _c, _s in STREAM for _i in range(_c)]
NBLK = len(BLOCKS)
NSPLIT = sum(b[2] for b in BLOCKS)
FIRST = {b[0]: i for i, b in reversed(list(enumerate(BLOCKS)))}


def split_no(n):
    l, k = divmod(n, NBLK)
    return l * NSPLIT + sum(b[2] for b in BLOCKS[:k])


JOBS = (["nx0", "nx1", "nx2", "nx3", "cs0", "cs1", "iq0", "iq1", "ik", "cq0", "cq1",
         "is00", "is01", "is10", "is11", "is12", "is13",
         "qa0", "qa1", "ka0", "ka1", "ckT", "cqT0", "cqT1", "va0", "va1", "zv0", "zv1",
         "qT0", "qT1", "kT0", "kT1", "zu0", "zu1"]
        + [f"al{h}{m}" for h in range(AH) for m in range(2)] + [f"gt{i}" for i in range(7)]
        + [f"pT{i}" for i in range(AH)] + ["gt7", "ay0", "ay1", "sv0", "sv1", "cl0", "cl1", "cl2",
                                           "gt8", "gt9", "gt10", "ct0", "ct1", "ct2", "gt11",
                                           "cy0", "cy1", "yT0", "yT1", "mx0", "mx1", "mx2", "mx3"]
        + [f"m{b}{i}" for i in range(4) for b in "bca"]
        + [f"o{i}" for i in range(4)] + ["mk0", "mk1"] + [f"ny{i}" for i in range(4)]
        + ["mq0", "mq1", "mkT0", "mkT1", "mv0", "mv1", "mqT0", "mqT1", "ml00", "ml01", "ml10",
           "ml11", "mp00", "mp01", "mp10", "mp11", "mo0", "mo1"]
        + [f"w{i}" for i in range(4)] + [f"nz{i}" for i in range(4)]
        + [f"pq{i}" for i in range(8)] + [f"ps{t}{i}" for t in range(NT) for i in range(4)])
BANK = {j: n % 8 for n, j in enumerate(JOBS)}
BEFORE_LOOPS = [sum(1 for j in JOBS if BANK[j] == b) for b in range(8)]
JOBS += ["eT", "gT"]
BANK["eT"], BANK["gT"] = 0, 1
USE = {j: sum(1 for i in JOBS[:n + 1] if BANK[i] == BANK[j]) for n, j in enumerate(JOBS)}
USES = [sum(1 for j in JOBS if BANK[j] == b) for b in range(8)]

ROOTS = dict(x=(0, 2, D), m=(2, 2, D), ck=(4, 2, CD), cq=(6, 8, CD), qa=(14, 16, AD),
             ka=(30, 16, AD), v=(46, 8, P), mk=(54, 8, MD), ya=(62, 8, P), y=(70, 2, D),
             mq=(72, 8, MD), z=(80, 2, D))
SQUARES = ["cq", "qa", "ka", "v", "ya", "mk", "mq"]
NSQ = len(SQUARES) * NT

PER_LAYER = dict(
    params=16, bias=32, mem_in=16, score0=3, xhi=24, sumsq=8, rms_in=len(ROOTS),
    rms_rt=len(ROOTS), rows=8, csq=2, relu_used=6, wmask=1, pen=2, sq=NSQ, sq_used=NSQ, vn=2,
    lam_s=1, lam_e=1, a_max=8, a_exp=8, pd=8, yb=4, c_max=2, c_exp=2, c_p=2, y_hi=4,
    y_lo=4, merged=4, merged_hi=4, merged_lo=4, o_hi=2, m_max=2, m_p=2,
    r_sub=2, r_exp=2, route=2, x_sum=1, x_peer=1, y_tile=1)


def build(nc, x_d, mem_d, relb_d, onehot_d, par_d, w_d, out_d, strip_d):
    ctx = ExitStack()
    with ctx:
        def sb(name, shape, dt=F32):
            return ctx.enter_context(nc.sbuf_tensor(name, shape, dt))

        def sem(name):
            return ctx.enter_context(nc.semaphore(name))

        X = sb("X", [P, NT, D])
        xh, xl = sb("xh", [P, KC, SEQ], F32R), sb("xl", [P, KC, SEQ], F32R)
        raw = [sb(f"raw{i}", [P, 1024]) for i in range(RAW)]
        wh = [sb(f"wh{i}", [P, 1024], F32R) for i in range(SPLIT)]
        wl = [sb(f"wl{i}", [P, 1024], F32R) for i in range(SPLIT)]
        stat = sb("stat", [P, 82])
        ident = sb("ident", [P, P])
        iota = sb("iota", [P, NKEY, SET], BF16)
        credit = sb("credit", [P, 5])
        top8 = sb("top8", [P, 8])
        iota16 = sb("iota16", [P, PK])
        loops = sb("loops", [P, 3 * 1024])
        loop_buf = lambda at, *d: loops[:, at:at + math.prod(d)]
        half_words = lambda at, *d: loops[:, at:at + math.prod(d) // 2].bitcast(BF16)
        oh1 = [half_words(i * 256, NKEY, SET).rearrange("p (n q) -> p n q", q=SET)
               for i in (0, 1)]
        chosen = [half_words(512 + i * 128, HALF, SET).rearrange("p (n q) -> p n q", q=SET)
                  for i in (0, 1)]
        oh2 = [half_words(768 + i * 384, 3, HALF, SET).rearrange(
            "p (g n q) -> p g n q", g=3, q=SET) for i in (0, 1)]
        choices = half_words(1536, 5, SEQ).rearrange("p (a t) -> p a t", a=5)
        hid = [loop_buf(2176 + i * SEQ, SEQ) for i in (0, 1)]
        iota_f = loop_buf(0, NKEY, SET).rearrange("p (n q) -> p n q", q=SET)
        some = sb("some", [P, 5, SOME], BF16)
        hh = [sb(f"hh{i}", [P, SEQ], F32R) for i in (0, 1)]
        hl = [sb(f"hl{i}", [P, SEQ], F32R) for i in (0, 1)]
        arena = sb("arena", [P, 2 * SEQ * HALF])
        part = [arena[:, i * SEQ * HALF:(i + 1) * SEQ * HALF] for i in range(2)]
        G = [a.rearrange("p (t n) -> p t n", n=HALF) for a in part]
        gelus = [part[1 - i].rearrange("p (n t) -> p n t", t=SEQ) for i in range(2)]

        def rooms(whole, at, *shapes):
            out = []
            for shape in shapes:
                n = math.prod(shape)
                assert at + n <= whole.shape[1], (at, n)
                a = whole[:, at:at + n]
                at += n
                names = "abcd"[:len(shape)]
                if len(shape) > 1:
                    a = a.rearrange(f"p ({' '.join(names)}) -> p {' '.join(names)}",
                                    **{c: k for c, k in zip(names, shape)})
                out.append(a)
            return out

        wide = (4, SEQ)
        rows4 = (NT, 512)
        va, vg, c_log1 = rooms(loops, 0, rows4, rows4, (4, SEQ))
        at = 0
        layout = {}

        def put(name, *shapes):
            nonlocal at
            layout[name] = at
            out = rooms(arena, at, *shapes)
            at += sum(math.prod(k) for k in shapes)
            return out

        par, = put("par", (NPAR,))
        bias = put("bias", (NHB, P), (NHB, SEQ))
        xn, = put("xn", (NT, D))
        cqn, qan, kan = put("heads", rows4, rows4, rows4)
        a_pT = rooms(arena, layout["heads"] + 1024, *[(3, P)] * AH)
        merged, mtmp = rooms(arena, layout["heads"], (KC, SEQ), (2, SEQ))
        sq = put("sq", *[(512,)] * 2)
        ckn, cv, iw = put("small", (NT, P), (NT, P), (NT, IH))
        iqT, = put("iqT", wide)
        ybT, = rooms(arena, layout["iqT"], wide)
        ikT, = put("ikT", (SEQ,))
        score, pen = put("score", (NT, SEQ), (NT, SEQ))
        qaT, = put("qaT", wide)
        yaT, = rooms(arena, layout["qaT"], wide)
        kaT, = put("kaT", wide)
        ya, = rooms(arena, layout["kaT"], rows4)
        cqT, ckT = put("cqT", wide, (SEQ,))
        uT, gates = put("gates", wide, (24, SEQ))
        msT, = rooms(arena, layout["bias"], (KC, SEQ))
        mkn, = rooms(arena, layout["gates"], rows4)
        mqn, mqT, _, m_e0, m_e1, m_pT = rooms(
            arena, layout["gates"], rows4, wide, wide, wide, wide, (2, 4, SEQ))
        m_e = [m_e0, m_e1]
        a_log = put("a_log", (2, SEQ), (2, SEQ))
        c_pT = rooms(arena, layout["a_log"], *[(4, P)] * 3)
        put("rest of c_pT", (512,))
        relu = put("relu", (512,), (512,), (1024,))[:2]
        a_pd = rooms(arena, layout["relu"], *[(NT, SEQ)] * AH)
        ycT, = rooms(arena, layout["relu"], wide)
        mkT, = put("mkT", wide)
        c_log = [put("c_log0", (4, P))[0], c_log1]
        mv, = put("mv", rows4)
        lamt, lam = put("lam", (2, AD), (4,))
        a_mx, a_sum = put("a_stats", (8, 2), (8, 2))
        c_mx, c_sum, m_mx, m_sum = put("stats", *[(NT, 4)] * 4)
        ms, = put("ms", (NT, D))
        at = NPAR
        pqT, ps0, ps1 = put("ps", (16, SEQ), (16, P), (16, P))
        cand, eq = rooms(arena, layout["ps"], (PH, 256), (PH * PK, PK))
        ps = [ps0, ps1]
        v16, i16f = put("top", (NT, 16, PK), (NT, 16, PK))
        cs, gate, half_f = put("gate", (NT, PH, PK), (NT, P), (NT, P))
        etok, rstat = put("etok", (2, NT, P), (NT, 3, PH))
        i16, ci, half_u = [x.bitcast(U32) for x in put("int", (NT, 16, PK), (NT, PH, PK), (NT, P))]
        assert at <= SEQ * HALF

        bank = [ctx.enter_context(nc.psum_tensor(f"bank{i}", [P, 512], F32)) for i in range(8)]
        bank_full = [sem(f"bank_full{i}") for i in range(8)]
        bank_free = [sem(f"bank_free{i}") for i in range(8)]
        landed = [sem(f"landed{i}") for i in range(RAW)]
        S = {n: sem(n) for n in PER_LAYER}
        whole_used = sem("whole_used")
        split_used = sem("split_used")
        hi_done, lo_done = sem("hi_done"), sem("lo_done")
        iota_ready = sem("iota_ready")
        x_in = [sem("x_in0"), sem("x_in1")]
        consts, strip_in = sem("consts"), sem("strip_in")
        strip_sb_ready, strip_out, strip_mm = sem("strip_sb"), sem("strip_out"), sem("strip_mm")
        dve_step, act_step, out_done = sem("dve_step"), sem("act_step"), sem("out_done")
        chosen_done = sem("chosen_done")
        oh_ready, g_full, g_free = sem("oh_ready"), sem("g_full"), sem("g_free")
        a_full, a_done, h_ready = sem("a_full"), sem("a_done"), sem("h_ready")
        y_full, toks, hid_m, hid_h = sem("y_full"), sem("toks"), sem("hid_m"), sem("hid_h")

        def p_(name, lo=0, hi=None):
            a, b = PAR[name]
            return par[:, a + lo:(b if hi is None else a + hi)]

        def pb(job):
            return bank[BANK[job]]

        def pb2(job):
            return bank[BANK[job]][:, :].rearrange("p (a b) -> p a b", a=2)

        def pb4(job):
            return bank[BANK[job]][:, :].rearrange("p (a b) -> p a b", a=4)

        def index_head(per, i, j):
            return 2 * per * (i // 2) + i % 2 + 2 * j

        def flat(ap):
            return ap.rearrange("p a b -> p (a b)")

        def repeat(eng, n, turn, body):
            if n // turn:
                with eng.Fori(0, n // turn) as i:
                    for j in range(turn):
                        body(i, j)
            for j in range(n // turn * turn, n):
                body(0, j)

        made = {}

        def whereof(s):
            l, k = divmod(s, NSPLIT)
            return l * NBLK + [i for i, b in enumerate(BLOCKS) if b[2]][k]

        class Side:

            def __init__(self, eng, step):
                self.eng, self.step, self.n, self.last, self.l = eng, step, {}, None, 0

            def sig(self, ins, s=None, by=1):
                s = self.step if s is None else s
                ins.then_inc(s, by)
                self.n[s.name] = self.n.get(s.name, 0) + by
                self.last = s, self.n[s.name]

            def settle(self):
                self.eng.wait_ge(*self.last)

            def give(self, l, ins, name):
                self.sig(ins, S[name])
                made[(l, name)] = made.get((l, name), 0) + 1

            def need(self, l, name, k):
                assert 0 < k <= PER_LAYER[name], (name, k)
                self.eng.wait_ge(S[name], l * PER_LAYER[name] + k)

            def full(self, l, job):
                self.eng.wait_ge(bank_full[BANK[job]], l * USES[BANK[job]] + USE[job])

            def free(self, ins, job):
                b = BANK[job]
                ins.then_inc(bank_free[b], 1)
                self.last = bank_free[b], self.l * USES[b] + USE[job]

            def took(self, l, job):
                self.eng.wait_ge(bank_free[BANK[job]], l * USES[BANK[job]] + USE[job])

        block = ctx.enter_context(nc.Block())
        @block.sync
        def _(sp):
            def load(n):
                old = n - RAW
                if old >= 0 and BLOCKS[old % NBLK][2]:
                    sp.wait_ge(lo_done, split_no(old) + 1)
                elif old >= 0:
                    sp.wait_ge(whole_used, old - split_no(old) + 1)
                sp.dma_start(raw[n % RAW][:, :], w_d[n]).then_inc(landed[n % RAW], 16)

            for t in range(NT):
                sp.dma_start(X[:, t, :], x_d[t * P:(t + 1) * P, :]).then_inc(x_in[t], 16)
            sp.dma_start(par, par_d[0]).then_inc(S["params"], 16)
            for l in range(DEPTH):
                base, loop_from = l * NBLK, l * NBLK + FIRST["uv"] + RAW
                for n in range(base, base + RAW):
                    load(n)
                if l:
                    sp.wait_ge(S["x_peer"], l)
                    sp.dma_start(par, par_d[l]).then_inc(S["params"], 16)
                sp.dma_start(ms, mem_d.rearrange("(t p) d -> p t d", p=P)).then_inc(S["mem_in"], 16)
                for n in range(base + RAW, base + FIRST["cq"]):
                    load(n)
                if l == 0:
                    sp.wait_ge(strip_out, 16)
                for t in range(NT):
                    k = P * (t + 1)
                    src = bass.AP(strip_d.tensor, strip_d.offset + 255 - P * t,
                                  [[STRIP - 1, P], [P * STRIP, NHB], [1, k]])
                    sp.dma_start(bias[t], src).then_inc(S["bias"], 16)
                for n in range(base + FIRST["cq"], loop_from):
                    load(n)

                def load_expert_block(i, j):
                    n = loop_from + j
                    sp.wait_ge(lo_done, i * TURN + (split_no(n - RAW) + 1))
                    src = w_d[bass.ds(i * TURN + n, 1), :, :].rearrange("o p n -> (o p) n")
                    sp.dma_start(raw[n % RAW][:, :], src).then_inc(landed[n % RAW], 16)

                repeat(sp, 2 * NKEY - RAW, TURN, load_expert_block)
            sp.wait_ge(S["x_peer"], DEPTH)
            sp.dma_start(out_d.rearrange("(t p) d -> p t d", p=P), X[:, :, :]).then_inc(out_done, 16)
            sp.wait_ge(out_done, 16)

        relb = sb("relb", [64, NHB])
        onehot = arena[0:64, layout["gates"]:layout["gates"] + STRIP]
        strip_sb = arena[0:NHB, layout["gates"] + STRIP:layout["gates"] + 2 * STRIP]

        @block.gpsimd
        def _(pool):
            nc.gpsimd.memset(relb[:, :], 1.0).then_inc(consts, 1)
            pool.wait_ge(consts, 1)
            pool.dma_start(relb[0:BUCKETS, :], relb_d).then_inc(strip_in, 16)
            pool.dma_start(onehot, onehot_d).then_inc(strip_in, 16)
            nc.gpsimd.memset(ident[:, :], 0.0).then_inc(consts, 1)
            pool.wait_ge(consts, 2)
            nc.gpsimd.affine_select(out=ident[:, :], in_=ident[:, :], compare_op=ALU.not_equal,
                                    fill=1.0, base=0, pattern=[[-1, P]],
                                    channel_multiplier=1).then_inc(consts, 1)
            nc.gpsimd.iota(iota_f, pattern=[[1, NKEY], [0, SET]], base=0, channel_multiplier=0,
                           allow_small_or_imprecise_dtypes=True).then_inc(consts, 1)
            nc.gpsimd.iota(iota16[:, :], pattern=[[1, PK]], base=0, channel_multiplier=0,
                           allow_small_or_imprecise_dtypes=True).then_inc(consts, 1)
            for n, s in enumerate((g_full, g_free, h_ready, a_done, y_full)):
                nc.gpsimd.memset(credit[:, n:n + 1], 0.0).then_inc(s, 2)
            pool.wait_ge(strip_sb_ready, 1)
            pool.dma_start(strip_d, strip_sb.unsqueeze(1).broadcast_to([NHB, P, STRIP])
                           ).then_inc(strip_out, 16)

            def low(i, s):
                n = whereof(s)
                pool.wait_ge(hi_done, i * TURN + (s + 1))
                nc.gpsimd.tensor_tensor(wl[s % SPLIT][:, :], raw[n % RAW][:, :],
                                        wh[s % SPLIT][:, :].bitcast(F32),
                                        ALU.subtract).then_inc(lo_done, 1)

            for l in range(DEPTH):
                if l:
                    pool.wait_ge(S["x_peer"], l)
                nc.gpsimd.memset(score[:, :, :], 0.0).then_inc(S["score0"], 1)
                pool.wait_ge(S["score0"], 3 * l + 1)
                for t in range(NT):
                    k = P * (t + 1)
                    nc.gpsimd.affine_select(out=score[:, t, 0:k], in_=score[:, t, 0:k],
                                            compare_op=ALU.is_ge, fill=MASK, base=P * t,
                                            pattern=[[-1, k]],
                                            channel_multiplier=1).then_inc(S["score0"], 1)
                done = l * NSPLIT
                for s in range(done, done + 4):
                    low(0, s)
                pool.wait_ge(S["params"], 16 * (l + 1))
                ws = p_("ws").rearrange("p (g t) -> p g t", g=BG)
                nc.gpsimd.affine_select(out=ws, in_=ws, compare_op=ALU.is_ge, fill=0.0, base=0,
                                        pattern=[[0, BG], [1, P]],
                                        channel_multiplier=-1).then_inc(S["wmask"], 1)
                first = split_no(l * NBLK + FIRST["uv"])
                for s in range(done + 4, first):
                    low(0, s)
                repeat(pool, 2 * NKEY, TURN, lambda i, j: low(i, first + j))

        def stats(name):
            a, w, _ = ROOTS[name]
            return stat[:, a:a + w]

        RORD = {n: i + 1 for i, n in enumerate(["x", "ck", "cq", "qa", "ka", "m", "v", "ya", "y",
                                                "mk", "mq", "z"])}
        SQO = {n: NT * i for i, n in enumerate(SQUARES)}
        ROWS = {"x": 0, "m": 2, "y": 4, "z": 6}
        XHI = {"x": 0, "y": 8, "z": 16}
        assert sorted(RORD) == sorted(ROOTS)

        @block.scalar
        def _(act):
            A = Side(act, act_step)
            a_ = nc.scalar.activation

            def row_sumsq(l, src, name, ready=None):
                load_sqrt()
                for t in range(NT):
                    if ready:
                        ready(t)
                    A.give(l, a_(xn[:, t, :], src[:, t, :], ACT.Square,
                                 accum_out=stats(name)[:, t:t + 1]), "sumsq")

            def load_sqrt():
                act.wait_ge(g_full, 2)
                A.sig(a_(credit[:, 0:1], credit[:, 0:1], ACT.Sqrt))
                A.settle()

            def root(l, name):
                A.need(l, "rms_in", RORD[name])
                A.give(l, a_(stats(name), stats(name), ACT.Sqrt), "rms_rt")

            def square(l, name, job=None):
                for t in range(NT):
                    n = l * NSQ + SQO[name] + t
                    if n >= 2:
                        act.wait_ge(S["sq_used"], n - 1)
                    if job:
                        A.full(l, f"{job}{t}")
                    A.give(l, a_(sq[n % 2], pb(f"{job}{t}")[:, :] if job else vg[:, t, :],
                                 ACT.Square), "sq")

            def copy_out(l, job, dst, src, func=ACT.Copy):
                A.full(l, job)
                A.free(a_(dst, src, func), job)

            def gain_out(l, job, dst, gain, i):
                A.full(l, job)
                A.sig(a_(dst[:, 2 * i, :], pb2(job)[:, 0, :], ACT.Copy,
                         scale=p_(gain, 2 * i, 2 * i + 1)))
                A.free(a_(dst[:, 2 * i + 1, :], pb2(job)[:, 1, :], ACT.Copy,
                          scale=p_(gain, 2 * i + 1, 2 * i + 2)), job)

            def high(i, s):
                n = whereof(s)
                if s >= SPLIT:
                    act.wait_ge(split_used, i * TURN + (s - SPLIT + 1))
                act.wait_ge(landed[n % RAW], i * (16 * TURN // RAW) + 16 * (n // RAW + 1))
                nc.scalar.copy(wh[s % SPLIT][:, :], raw[n % RAW][:, :]).then_inc(hi_done, 1)

            next_split = [0]

            def split_to(l, name, count, ahead=AHEAD):
                n = l * NBLK + FIRST[name] + count
                while ahead and BLOCKS[n % NBLK][2]:
                    n, ahead = n + 1, ahead - 1
                while next_split[0] < split_no(n):
                    high(0, next_split[0])
                    next_split[0] += 1

            def x_high(l, pre, gain):
                for i in range(4):
                    A.full(l, f"{pre}{i}")
                    for c in range(2):
                        k = 2 * i + c
                        A.give(l, a_(xh[:, k, :], pb2(f"{pre}{i}")[:, c, :], ACT.Copy,
                                     scale=p_(gain, k, k + 1)), "xhi")

            for l in range(DEPTH):
                A.l = l
                row_sumsq(l, X, "x", lambda t: act.wait_ge(*((S["x_peer" if t else "x_sum"], l) if l
                                                            else (x_in[t], 16))))
                root(l, "x")
                split_to(l, "cs", SPLIT - 1, 0)
                act.wait_ge(S["params"], 16 * (l + 1))
                x_high(l, "nx", "g_mix")
                split_to(l, "cs", 4)
                for t in range(NT):
                    A.full(l, f"cs{t}")
                    if l * NSQ + t >= 2:
                        act.wait_ge(S["sq_used"], l * NSQ + t - 1)
                    A.give(l, a_(sq[(l * NSQ + t) % 2][:, 0:P], pb(f"cs{t}")[:, 0:P], ACT.Square,
                                 accum_out=stats("ck")[:, t:t + 1]), "csq")
                root(l, "ck")
                for i in range(2):
                    split_to(l, "iq", 2 * i + 2)
                    copy_out(l, f"iq{i}", iqT[:, 2 * i:2 * i + 2, :], pb2(f"iq{i}"))
                split_to(l, "ik", 1)
                copy_out(l, "ik", ikT, pb("ik")[:, 0:SEQ])
                split_to(l, "cq", 4)
                square(l, "cq", "cq")
                root(l, "cq")
                for n, job in enumerate(["is00", "is01", "is10", "is11", "is12", "is13"]):
                    if l * 6 + n >= 2:
                        act.wait_ge(S["relu_used"], l * 6 + n - 1)
                    copy_out(l, job, relu[n % 2], pb(job)[:, :], ACT.Relu)
                    if n % 2:
                        split_to(l, "qa", 2 + n // 2, 0)
                split_to(l, "qa", 4)
                square(l, "qa", "qa")
                root(l, "qa")
                split_to(l, "ka", 4)
                square(l, "ka", "ka")
                root(l, "ka")
                split_to(l, "va", 2)
                act.wait_ge(S["mem_in"], 16 * (l + 1))
                row_sumsq(l, ms, "m")
                root(l, "m")
                split_to(l, "va", 4)
                for t in range(NT):
                    copy_out(l, f"va{t}", va[:, t, :], pb(f"va{t}")[:, :])
                split_to(l, "zv", 4)
                for t in range(NT):
                    copy_out(l, f"zv{t}", vg[:, t, :], pb(f"zv{t}")[:, :], ACT.Gelu)
                A.settle()
                square(l, "v")
                root(l, "v")
                for i in range(2):
                    split_to(l, "zu", 2 * i + 2)
                    copy_out(l, f"zu{i}", uT[:, 2 * i:2 * i + 2, :], pb2(f"zu{i}"), ACT.Gelu)
                A.need(l, "lam_s", 1)
                A.give(l, a_(lam[:, 0:2], lam[:, 0:2], ACT.Exp), "lam_e")
                for u in range(8):
                    split_to(l, "gts", 2 + 4 * u // 3, 0)
                    k = P * (u % 2 + 1)
                    A.need(l, "a_max", u + 1)
                    for m in range(2):
                        e = a_(a_log[u % 2][:, m, 0:k], a_log[u % 2][:, m, 0:k], ACT.Exp,
                               bias=a_mx[:, u, m:m + 1], accum_out=a_sum[:, u, m:m + 1])
                        if m:
                            A.give(l, e, "a_exp")
                        else:
                            A.sig(e)

                def gates_out(i):
                    split_to(l, "gts", 2 * i + 2)
                    copy_out(l, f"gt{i}", gates[:, 2 * i:2 * i + 2, :], pb2(f"gt{i}"), ACT.Sigmoid)

                for i in range(7):
                    gates_out(i)
                for h in range(AH):
                    copy_out(l, f"pT{h}", a_pT[h],
                             pb(f"pT{h}")[:, 0:3 * P].rearrange("p (a b) -> p a b", a=3))
                gates_out(7)
                square(l, "ya", "ay")
                root(l, "ya")
                for i in (8, 9):
                    gates_out(i)
                for t in range(NT):
                    A.need(l, "c_max", t + 1)
                    A.give(l, a_(c_log[t], c_log[t], ACT.Exp), "c_exp")
                gates_out(10)
                for i in range(3):
                    copy_out(l, f"ct{i}", c_pT[i], pb4(f"ct{i}"))
                gates_out(11)
                split_to(l, "br_b0", 1, 0)

                def y_high(k, src):
                    A.give(l, nc.scalar.copy(xh[:, k:k + 2, :], src[:, k % 4:k % 4 + 2, :]), "y_hi")

                A.need(l, "yb", 4)
                y_high(4, ybT)
                y_high(6, ybT)
                split_to(l, "br_a0", 1, 0)
                for t in range(NT):
                    copy_out(l, f"cy{t}", ycT[:, :, t * P:(t + 1) * P], pb4(f"cy{t}"))
                for i in range(2):
                    A.took(l, f"yT{i}")
                    y_high(2 * i, yaT)
                split_to(l, "br_b1", 1, 0)
                for i in range(4):
                    gain_out(l, f"mx{i}", msT, "g_src", i)
                for i in range(1, 4):
                    split_to(l, f"br_a{i}", 1, 0)
                split_to(l, "mix_out", 1, 0)
                A.full(l, "ma3")
                for i in range(4):
                    if i == 3:
                        split_to(l, "mix_out", 2, 0)
                    A.need(l, "merged", i + 1)
                    A.give(l, nc.scalar.copy(xh[:, 2 * i:2 * i + 2, :],
                                             merged[:, 2 * i:2 * i + 2, :]), "merged_hi")
                split_to(l, "mix_out", 8, 0)
                row_sumsq(l, X, "y", lambda t: A.took(l, f"o{2 * t + 1}"))
                root(l, "y")
                split_to(l, "mq", 2, 0)
                x_high(l, "ny", "g_mem")
                split_to(l, "mq", 3, 0)
                square(l, "mk", "mk")
                root(l, "mk")
                split_to(l, "mq", 4)
                square(l, "mq", "mq")
                root(l, "mq")
                for t in range(NT):
                    A.need(l, "m_max", t + 1)
                    for h in range(MH):
                        job = f"ml{t}{h // 2}"
                        e = a_(m_e[t][:, h, :], pb2(job)[:, h % 2, :], ACT.Exp, scale=MD ** -0.5,
                               bias=m_mx[:, t, h:h + 1], accum_out=m_sum[:, t, h:h + 1])
                        if h % 2:
                            A.free(e, job)
                        else:
                            A.sig(e)
                for t in range(NT):
                    copy_out(l, f"mv{t}", mv[:, t, :], pb(f"mv{t}")[:, :])
                for t in range(NT):
                    for k in range(NT):
                        copy_out(l, f"mp{t}{k}", m_pT[:, k, :, t * P:(t + 1) * P], pb4(f"mp{t}{k}"))
                split_to(l, "mo", 2, 0)
                for i in range(2):
                    A.full(l, f"mo{i}")
                    A.give(l, a_(xh[:, 2 * i:2 * i + 2, :], pb2(f"mo{i}"), ACT.Copy), "o_hi")
                split_to(l, "mo", 4, 0)
                split_to(l, "pq", 1, 0)
                row_sumsq(l, X, "z", lambda t: A.took(l, f"w{2 * t + 1}"))
                root(l, "z")
                x_high(l, "nz", "g_peer")
                split_to(l, "pq", SPLIT, 0)
                for i in range(8):
                    split_to(l, "pq", 2 * i + 2)
                    copy_out(l, f"pq{i}", pqT[:, 2 * i:2 * i + 2, :], pb2(f"pq{i}"))
                for t in range(NT):
                    for i in range(4):
                        copy_out(l, f"ps{t}{i}", ps[t][:, 4 * i:4 * i + 4, :], pb4(f"ps{t}{i}"))

                uv = split_no(l * NBLK + FIRST["uv"])
                assert next_split[0] == uv + AHEAD

                def high_ahead(i, k):
                    if uv + k + AHEAD < DEPTH * NSPLIT:
                        high(i, uv + k + AHEAD)

                def gelu(i, c):
                    act.wait_ge(a_full, i * TURN + (l * NKEY + c + 1))
                    half, n = divmod(c, HALF)
                    a_(gelus[half][:, bass.ds(i * TURN + n, 1), :].rearrange("p o t -> p (o t)"),
                       bank[4 + c % 2][:, 0:SEQ], ACT.Gelu).then_inc(a_done, 1)

                def take_gates(i, half, s, per):
                    act.wait_ge(g_full, i * per + ((2 * l + half) * 64 + s + 3))
                    nc.scalar.copy(G[half][:, bass.ds(i * (4 * per) + 4 * s, 4), :],
                                   bank[6 + s % 2][:, 0:4 * HALF].rearrange("p (t n) -> p t n", t=4)
                                   ).then_inc(g_free, 1)

                def up(i, c):
                    high_ahead(i, c + HALF * (c // HALF))
                    gelu(i, c)

                def up_gates(half):
                    c, s = (R3, 0) if half == 0 else (HALF, 0)
                    for n, per in GATE_STEPS[half]:
                        def body(i, j):
                            k = c + j
                            high_ahead(i, k + HALF * (k // HALF))
                            for q in range(per):
                                take_gates(i, half, s + per * j + q, TURN * per)
                            gelu(i, k)
                        repeat(act, n, TURN, body)
                        c, s = c + n, s + n * per

                repeat(act, R1, TURN, up)
                for t in range(NT):
                    A.need(l, "r_sub", t + 1)
                    A.give(l, a_(cs[:, t], cs[:, t], ACT.Exp), "r_exp")
                for c in range(R1, R3):
                    up(0, c)
                A.took(l, "eT")
                A.took(l, "gT")
                up_gates(0)
                repeat(act, HALF, TURN, lambda i, j: high_ahead(i, HALF + j))
                act.wait_ge(h_ready, l * NKEY + HALF + 2)
                up_gates(1)
                repeat(act, HALF, TURN, lambda i, j: high_ahead(i, 3 * HALF + j))
                next_split[0] = min(uv + 4 * HALF + AHEAD, DEPTH * NSPLIT)

        @block.vector
        def _(dve):
            V = Side(dve, dve_step)
            v = nc.vector

            def inverse_rms(l, name, ready):
                _, _, n = ROOTS[name]
                ready()
                V.give(l, v.tensor_scalar(stats(name), stats(name), 1.0 / n, EPS, ALU.mult,
                                          ALU.add), "rms_in")
                V.need(l, "rms_rt", RORD[name])
                V.sig(v.reciprocal(stats(name), stats(name)))
                V.settle()

            def norm_rows(l, src, dst, name):
                inverse_rms(l, name, lambda: V.need(l, "sumsq", ROWS[name] + NT))
                for t in range(NT):
                    V.give(l, v.tensor_scalar(dst[:, t, :], src[:, t, :],
                                              stats(name)[:, t:t + 1], None, ALU.mult), "rows")

            def sum_squares(l, name, w):
                for t in range(NT):
                    n = SQO[name] + t
                    V.need(l, "sq", n + 1)
                    g = 512 // w
                    V.give(l, v.tensor_reduce(
                        out=stats(name)[:, t * g:(t + 1) * g],
                        in_=sq[(l * NSQ + n) % 2].rearrange("p (g w) -> p g w", w=w),
                        axis=AX, op=ALU.add), "sq_used")

            def norm_heads(l, name, job, dst, w):
                sum_squares(l, name, w)
                inverse_rms(l, name, V.settle)
                g = 512 // w
                for t in range(NT):
                    r = stats(name)[:, t * g:(t + 1) * g]
                    V.free(v.tensor_tensor(
                        dst[:, t, :].rearrange("p (g w) -> p g w", w=w),
                        pb(f"{job}{t}")[:, :].rearrange("p (g w) -> p g w", w=w),
                        r.unsqueeze(2).broadcast_to([P, g, w]), ALU.mult), f"{job}{t}")

            def x_low(l, name, pre, gain):
                for i in range(4):
                    V.need(l, "xhi", XHI[name] + 2 * i + 2)
                    for c in range(2):
                        k = 2 * i + c
                        o = v.scalar_tensor_tensor(
                            out=xl[:, k, :], in0=pb2(f"{pre}{i}")[:, c, :],
                            scalar=p_(gain, k, k + 1), in1=xh[:, k, :].bitcast(F32),
                            op0=ALU.mult, op1=ALU.subtract)
                        if c:
                            V.free(o, f"{pre}{i}")
                        else:
                            V.sig(o)

            def gain_all(l, job, dst, src, gain):
                V.full(l, job)
                V.free(v.tensor_scalar(dst, src, p_(gain), None, ALU.mult), job)

            def add_to_x(l, jobs):
                for n, job in enumerate(jobs):
                    t, h = n // 2, n % 2
                    xs = X[:, t, h * 512:(h + 1) * 512]
                    V.full(l, job)
                    V.free(v.tensor_tensor(xs, pb(job)[:, :], xs, ALU.add), job)

            dve.wait_ge(consts, 4)
            v.tensor_copy(iota[:, :, :], iota_f).then_inc(iota_ready, 1)
            dve.wait_ge(strip_mm, 1)
            v.tensor_copy(strip_sb, bank[0][0:NHB, 0:STRIP]).then_inc(strip_sb_ready, 1)
            for l in range(DEPTH):
                V.l = l
                lam_init = 0.8 - 0.6 * math.exp(-0.3 * l)
                norm_rows(l, X, xn, "x")
                dve.wait_ge(S["params"], 16 * (l + 1))
                x_low(l, "x", "nx", "g_mix")
                for m in range(2):
                    V.sig(v.tensor_tensor(lamt[:, m, :], p_("lam", 2 * m * AD, (2 * m + 1) * AD),
                                          p_("lam", (2 * m + 1) * AD, (2 * m + 2) * AD), ALU.mult))
                V.settle()
                V.give(l, v.tensor_reduce(out=lam[:, 0:2], in_=lamt, axis=AX, op=ALU.add), "lam_s")
                inverse_rms(l, "ck", lambda: V.need(l, "csq", NT))
                for t in range(NT):
                    job = f"cs{t}"
                    V.sig(v.tensor_scalar(ckn[:, t, :], pb(job)[:, 0:P], stats("ck")[:, t:t + 1],
                                          None, ALU.mult))
                    V.sig(v.tensor_copy(cv[:, t, :], pb(job)[:, P:2 * P]))
                    V.free(v.tensor_copy(iw[:, t, :], pb(job)[:, 2 * P:2 * P + IH]), job)
                norm_heads(l, "cq", "cq", cqn, CD)
                V.need(l, "score0", 3)
                n = 0
                for t in range(NT):
                    k = P * (t + 1)
                    per = 512 // k
                    for i in range(IH // per):
                        V.took(l, f"is{t}{i}")
                        for j in range(per):
                            h = index_head(per, i, j)
                            o = v.scalar_tensor_tensor(
                                out=score[:, t, 0:k], in0=relu[n % 2][:, j * k:(j + 1) * k],
                                scalar=iw[:, t, h:h + 1], in1=score[:, t, 0:k],
                                op0=ALU.mult, op1=ALU.add)
                            if j == per - 1:
                                V.give(l, o, "relu_used")
                            else:
                                V.sig(o)
                            V.settle()
                        n += 1
                norm_heads(l, "qa", "qa", qan, AD)
                norm_heads(l, "ka", "ka", kan, AD)
                norm_rows(l, ms, ms, "m")
                gain_all(l, "ckT", ckT, pb("ckT")[:, 0:SEQ], "ck")
                for i in range(2):
                    gain_all(l, f"cqT{i}", cqT[:, 2 * i:2 * i + 2, :], pb2(f"cqT{i}"), "cq")
                sum_squares(l, "v", P)
                inverse_rms(l, "v", V.settle)
                for t in range(NT):
                    x3 = vg[:, t, :].rearrange("p (g w) -> p g w", w=P)
                    V.give(l, v.tensor_tensor(x3, x3, stats("v")[:, 4 * t:4 * t + 4].unsqueeze(2)
                                              .broadcast_to([P, 4, P]), ALU.mult), "vn")
                for i in range(2):
                    gain_all(l, f"qT{i}", qaT[:, 2 * i:2 * i + 2, :], pb2(f"qT{i}"), "aq")
                for i in range(2):
                    gain_all(l, f"kT{i}", kaT[:, 2 * i:2 * i + 2, :], pb2(f"kT{i}"), "ak")
                dve.wait_ge(S["bias"], 32 * (l + 1))
                V.need(l, "lam_e", 1)
                V.sig(v.tensor_tensor(lam[:, 2:3], lam[:, 1:2], lam[:, 0:1], ALU.subtract))
                V.settle()
                V.sig(v.tensor_scalar(lam[:, 2:3], lam[:, 2:3], -lam_init, None, ALU.add))
                V.settle()

                def a_start(u):
                    h, t = divmod(u, 2)
                    k = P * (t + 1)
                    for m in range(2):
                        job = f"al{h}{m}"
                        V.full(l, job)
                        o = v.scalar_tensor_tensor(
                            out=a_log[u % 2][:, m, 0:k], in0=pb(job)[:, t * P:t * P + k],
                            scalar=AD ** -0.5, in1=bias[t][:, h, :], op0=ALU.mult, op1=ALU.add)
                        if t:
                            V.free(o, job)
                        else:
                            V.sig(o)
                    V.settle()
                    V.sig(v.tensor_reduce(out=a_mx[:, u, :], in_=a_log[u % 2][:, :, 0:k], axis=AX,
                                          op=ALU.max))
                    V.settle()
                    V.give(l, v.tensor_scalar(a_mx[:, u, :], a_mx[:, u, :], -1.0, None, ALU.mult),
                           "a_max")

                def a_end(u):
                    h, t = divmod(u, 2)
                    k = P * (t + 1)
                    V.need(l, "a_exp", u + 1)
                    V.sig(v.reciprocal(a_sum[:, u, :], a_sum[:, u, :]))
                    V.settle()
                    V.sig(v.tensor_tensor(a_sum[:, u, 1:2], a_sum[:, u, 1:2], lam[:, 2:3],
                                          ALU.mult))
                    V.settle()
                    V.sig(v.tensor_scalar(a_log[u % 2][:, 1, 0:k], a_log[u % 2][:, 1, 0:k],
                                          a_sum[:, u, 1:2], None, ALU.mult))
                    V.settle()
                    V.give(l, v.scalar_tensor_tensor(
                        out=a_pd[h][:, t, 0:k], in0=a_log[u % 2][:, 0, 0:k],
                        scalar=a_sum[:, u, 0:1], in1=a_log[u % 2][:, 1, 0:k],
                        op0=ALU.mult, op1=ALU.add), "pd")
                    V.settle()

                a_start(0)
                for u in range(8):
                    if u < 7:
                        a_start(u + 1)
                    a_end(u)
                for t in range(NT):
                    k = P * (t + 1)
                    for r in range(TOPK_C // 8):
                        V.sig(v.max(out=top8[:, :], in_=score[:, t, 0:k]))
                        V.settle()
                        V.sig(v.match_replace(out=score[:, t, 0:k], in_to_replace=top8[:, :],
                                              in_values=score[:, t, 0:k], imm_value=TAKEN))
                        V.settle()
                    V.give(l, v.tensor_scalar(pen[:, t, 0:k], score[:, t, 0:k], TAKEN / 2, MASK,
                                              ALU.is_gt, ALU.mult), "pen")
                norm_heads(l, "ya", "ay", ya, P)
                for i in range(2):
                    V.full(l, f"sv{i}")
                    V.took(l, f"zu{i}")
                    for j in range(2):
                        g = 2 * i + j
                        o = v.scalar_tensor_tensor(
                            out=ybT[:, g, :].rearrange("p (c t) -> p c t", c=2),
                            in0=pb2(f"sv{i}")[:, j, :].rearrange("p (c t) -> p c t", c=2),
                            scalar=p_("bv", g, g + 1),
                            in1=p_("bs", g * P, (g + 1) * P).unsqueeze(1).broadcast_to([P, 2, P]),
                            op0=ALU.mult, op1=ALU.add)
                        if j:
                            V.free(o, f"sv{i}")
                        else:
                            V.sig(o)
                    V.settle()
                    for j in range(2):
                        g = 2 * i + j
                        V.give(l, v.tensor_tensor(ybT[:, g, :], ybT[:, g, :], uT[:, g, :],
                                                  ALU.mult), "yb")
                for t in range(NT):
                    k = P * (t + 1)
                    for n, job in enumerate(["cl0"] if t == 0 else ["cl1", "cl2"]):
                        hs = slice(0, 4) if t == 0 else slice(2 * n, 2 * n + 2)
                        V.full(l, job)
                        V.free(v.scalar_tensor_tensor(
                            out=c_log[t][:, hs, :],
                            in0=pb(job)[:, :].rearrange("p (h k) -> p h k", k=k),
                            scalar=CD ** -0.5, in1=bias[t][:, AH:, :][:, hs, :],
                            op0=ALU.mult, op1=ALU.add), job)
                    V.settle()
                    V.sig(v.tensor_tensor(c_log[t], c_log[t], pen[:, t, 0:k].unsqueeze(1)
                                          .broadcast_to([P, 4, k]), ALU.add))
                    V.settle()
                    V.sig(v.tensor_reduce(out=c_mx[:, t, :], in_=c_log[t], axis=AX, op=ALU.max))
                    V.settle()
                    V.give(l, v.tensor_tensor(c_log[t], c_log[t], c_mx[:, t, :].unsqueeze(2)
                                              .broadcast_to([P, 4, k]), ALU.subtract), "c_max")
                for t in range(NT):
                    k = P * (t + 1)
                    V.need(l, "c_exp", t + 1)
                    V.sig(v.tensor_reduce(out=c_sum[:, t, :], in_=c_log[t], axis=AX, op=ALU.add))
                    V.settle()
                    V.sig(v.reciprocal(c_sum[:, t, :], c_sum[:, t, :]))
                    V.settle()
                    V.give(l, v.tensor_tensor(c_log[t], c_log[t], c_sum[:, t, :].unsqueeze(2)
                                              .broadcast_to([P, 4, k]), ALU.mult), "c_p")
                V.took(l, "gt11")

                def y_low(k, src, n):
                    V.need(l, "y_hi", n)
                    V.give(l, v.tensor_tensor(xl[:, k:k + 2, :], src[:, k % 4:k % 4 + 2, :],
                                              xh[:, k:k + 2, :].bitcast(F32), ALU.subtract), "y_lo")

                y_low(4, ybT, 1)
                y_low(6, ybT, 2)
                for i in range(2):
                    V.full(l, f"yT{i}")
                    V.free(v.tensor_scalar(yaT[:, 2 * i:2 * i + 2, :], pb2(f"yT{i}"), p_("asub"),
                                           1.0 - lam_init, ALU.mult, ALU.mult), f"yT{i}")
                for i in range(2):
                    y_low(2 * i, yaT, 3 + i)
                for i in range(4):
                    acc = merged[:, 2 * i:2 * i + 2, :]
                    for b, c in enumerate("bca"):
                        job = f"m{c}{i}"
                        V.full(l, job)
                        first = "abc".index(c) * KC + 2 * i
                        g = gates[:, first:first + 2, :]
                        V.free(v.tensor_tensor(acc if b == 0 else mtmp, pb2(job), g, ALU.mult), job)
                        V.settle()
                        if b == 1:
                            V.sig(v.tensor_tensor(acc, acc, mtmp, ALU.add))
                            V.settle()
                        if b == 2:
                            V.give(l, v.tensor_tensor(acc, acc, mtmp, ALU.add), "merged")
                for i in range(4):
                    V.need(l, "merged_hi", i + 1)
                    pair = slice(2 * i, 2 * i + 2)
                    V.give(l, v.tensor_tensor(xl[:, pair, :], merged[:, pair, :],
                                              xh[:, pair, :].bitcast(F32), ALU.subtract), "merged_lo")
                add_to_x(l, [f"o{i}" for i in range(4)])
                norm_rows(l, X, xn, "y")
                x_low(l, "y", "ny", "g_mem")
                norm_heads(l, "mk", "mk", mkn, MD)
                for i in range(2):
                    gain_all(l, f"mkT{i}", mkT[:, 2 * i:2 * i + 2, :], pb2(f"mkT{i}"), "mk")
                norm_heads(l, "mq", "mq", mqn, MD)
                for i in range(2):
                    gain_all(l, f"mqT{i}", mqT[:, 2 * i:2 * i + 2, :], pb2(f"mqT{i}"), "mq")
                for t in range(NT):
                    for i in range(2):
                        V.full(l, f"ml{t}{i}")
                        V.sig(v.tensor_reduce(out=m_mx[:, t, 2 * i:2 * i + 2], in_=pb2(f"ml{t}{i}"),
                                              axis=AX, op=ALU.max))
                    V.settle()
                    V.give(l, v.tensor_scalar(m_mx[:, t, :], m_mx[:, t, :], -MD ** -0.5, None,
                                              ALU.mult), "m_max")
                for t in range(NT):
                    V.took(l, f"ml{t}0")
                    V.took(l, f"ml{t}1")
                    V.sig(v.reciprocal(m_sum[:, t, :], m_sum[:, t, :]))
                    V.settle()
                    V.give(l, v.tensor_tensor(m_e[t], m_e[t], m_sum[:, t, :].unsqueeze(2)
                                              .broadcast_to([P, 4, SEQ]), ALU.mult), "m_p")
                for i in range(2):
                    V.need(l, "o_hi", i + 1)
                    pair = slice(2 * i, 2 * i + 2)
                    V.free(v.tensor_tensor(xl[:, pair, :], pb2(f"mo{i}"), xh[:, pair, :].bitcast(F32),
                                           ALU.subtract), f"mo{i}")
                add_to_x(l, [f"w{i}" for i in range(4)])
                norm_rows(l, X, xn, "z")
                x_low(l, "z", "nz", "g_peer")
                for t in range(NT):
                    for i in range(4):
                        V.took(l, f"ps{t}{i}")
                for t in range(NT):

                    def sixteen(n, src, vals, idx):
                        for at in (slice(0, 8), slice(8, 16)):
                            for c in range(n):
                                V.sig(v.max(out=vals[:, c, at], in_=src[:, c, :]))
                            V.settle()
                            for c in range(n):
                                V.sig(v.max_index(out=idx[:, c, at], in_max=vals[:, c, at],
                                                  in_values=src[:, c, :]))
                            V.settle()
                            if at.start == 0:
                                for c in range(n):
                                    V.sig(v.match_replace(
                                        out=src[:, c, :], in_to_replace=vals[:, c, at],
                                        in_values=src[:, c, :], imm_value=TAKEN))
                                V.settle()

                    sixteen(16, ps[t], v16[:, t], i16[:, t])
                    V.sig(v.tensor_copy(i16f[:, t], i16[:, t]))
                    vv = v16[:, t].rearrange("p (h two) k -> p h two k", two=2)
                    V.sig(v.tensor_tensor(
                        cand.rearrange("p h (i j) -> p h i j", i=PK),
                        vv[:, :, 0, :].unsqueeze(3).broadcast_to([P, PH, PK, PK]),
                        vv[:, :, 1, :].unsqueeze(2).broadcast_to([P, PH, PK, PK]), ALU.add))
                    V.settle()
                    sixteen(PH, cand, cs[:, t], ci[:, t])
                    V.sig(v.tensor_copy(rstat[:, t, 0, :], cs[:, t, :, 0]))
                    V.settle()
                    V.give(l, v.tensor_tensor(cs[:, t], cs[:, t], rstat[:, t, 0, :].unsqueeze(2)
                                              .broadcast_to([P, PH, PK]), ALU.subtract), "r_sub")
                    ii = i16f[:, t].rearrange("p (h two) k -> p h two k", two=2)
                    cit = ci[:, t].rearrange("p h k -> p (h k)")
                    for part in range(2):
                        if part == 0:
                            V.sig(v.tensor_scalar(half_u[:, t, :], cit, 4, None,
                                                  ALU.logical_shift_right))
                        else:
                            V.sig(v.tensor_scalar(half_u[:, t, :], cit, 15, None, ALU.bitwise_and))
                        V.settle()
                        V.sig(v.tensor_copy(half_f[:, t, :], half_u[:, t, :]))
                        V.settle()
                        V.sig(v.tensor_tensor(
                            eq, half_f[:, t, :].unsqueeze(2).broadcast_to([P, P, PK]),
                            iota16[:, :].unsqueeze(1).broadcast_to([P, P, PK]), ALU.is_equal))
                        V.settle()
                        eq4 = eq.rearrange("p (h k) i -> p h k i", h=PH)
                        V.sig(v.tensor_tensor(eq4, eq4, ii[:, :, part, :].unsqueeze(2)
                                              .broadcast_to([P, PH, PK, PK]), ALU.mult))
                        V.settle()
                        V.sig(v.tensor_reduce(out=etok[:, part, t, :], in_=eq, axis=AX, op=ALU.add))
                        V.settle()
                for t in range(NT):
                    V.need(l, "r_exp", t + 1)
                    V.sig(v.tensor_reduce(out=rstat[:, t, 1, :], in_=cs[:, t], axis=AX, op=ALU.add))
                    V.settle()
                    V.sig(v.reciprocal(rstat[:, t, 1, :], rstat[:, t, 1, :]))
                    V.settle()
                    V.give(l, v.tensor_tensor(
                        gate[:, t, :].rearrange("p (h k) -> p h k", h=PH), cs[:, t],
                        rstat[:, t, 1, :].unsqueeze(2).broadcast_to([P, PH, PK]), ALU.mult),
                        "route")
                V.full(l, "eT")
                V.sig(v.tensor_copy(choices[:, 0, :], pb2("eT")[:, 0, :]))
                V.free(v.tensor_copy(choices[:, 1, :], pb2("eT")[:, 1, :]), "eT")
                V.full(l, "gT")
                V.sig(v.tensor_copy(choices[:, 2, :], pb("gT")[:, 0:SEQ]))
                V.settle()
                V.free(v.tensor_tensor(hid[0], pb("gT")[:, 0:SEQ], choices[:, 2, :],
                                       ALU.subtract), "gT")
                V.settle()
                V.sig(v.tensor_copy(choices[:, 3, :], hid[0]))
                V.settle()
                V.sig(v.tensor_tensor(choices[:, 4, :], hid[0], choices[:, 3, :], ALU.subtract))
                V.settle()

                def one_hots(half):
                    per = SOME // SET
                    with dve.Fori(0, SEQ // SOME) as i:
                        v.tensor_copy(some[:, :, :],
                                      choices[:, :, bass.ds(i * SOME, SOME)]).then_inc(toks, 1)
                        dve.wait_ge(toks, i + ((2 * l + half) * (SEQ // SOME) + 1))
                        for s in range(per):
                            at = i * per + ((2 * l + half) * 64 + s + 1)
                            e1, e2 = [some[:, a, s * SET:(s + 1) * SET].unsqueeze(1) for a in (0, 1)]
                            gates_s = some[:, 2:5, s * SET:(s + 1) * SET].unsqueeze(2)
                            dve.wait_ge(g_full, at)
                            v.tensor_tensor(chosen[s % 2], iota[:, half * HALF:(half + 1) * HALF, :],
                                            e2.broadcast_to([P, HALF, SET]),
                                            ALU.is_equal).then_inc(chosen_done, 1)
                            v.tensor_tensor(oh1[s % 2], iota[:, :, :],
                                            e1.broadcast_to([P, NKEY, SET]), ALU.is_equal)
                            dve.wait_ge(chosen_done, at)
                            v.tensor_tensor(
                                oh2[s % 2],
                                chosen[s % 2].unsqueeze(1).broadcast_to([P, 3, HALF, SET]),
                                gates_s.broadcast_to([P, 3, HALF, SET]),
                                ALU.mult).then_inc(oh_ready, 1)
                        dve.wait_ge(oh_ready, i * per + ((2 * l + half) * 64 + per))
                    dve.wait_ge(g_free, (2 * l + half + 1) * 64 + 2)

                def hidden(i, c):
                    half, n = divmod(c, HALF)
                    at = i * TURN + (l * NKEY + c + 1)
                    col = bass.ds(i * TURN + n, 1)
                    dve.wait_ge(a_done, at + 2)
                    v.tensor_tensor(hid[c % 2], gelus[half][:, col, :].rearrange("p o t -> p (o t)"),
                                    G[half][:, :, col].rearrange("p t o -> p (t o)"),
                                    ALU.mult).then_inc(hid_m, 1)
                    dve.wait_ge(hid_m, at)
                    dve.wait_ge(y_full, at)
                    v.tensor_copy(hh[c % 2][:, :], hid[c % 2]).then_inc(hid_h, 1)
                    dve.wait_ge(hid_h, at)
                    v.tensor_tensor(hl[c % 2][:, :], hid[c % 2], hh[c % 2][:, :].bitcast(F32),
                                    ALU.subtract).then_inc(h_ready, 1)

                for half in range(2):
                    one_hots(half)
                    repeat(dve, HALF, TURN, lambda i, j: hidden(i, HALF * half + j))
                V.need(l, "y_tile", 1)
                for n in range(4):
                    if n == 2:
                        dve.wait_ge(y_full, (l + 1) * NKEY + 2)
                    t, h = n // 2, n % 2
                    xs = X[:, t, h * 512:(h + 1) * 512]
                    o = v.tensor_tensor(xs, bank[n][:, :], xs, ALU.add)
                    if n == 3:
                        V.give(l, o, "x_peer")
                    elif n == 1:
                        V.give(l, o, "x_sum")
                    else:
                        V.sig(o)
                V.settle()

        @block.tensor
        def _(pe):
            T = Side(pe, None)
            mm_, tr_ = nc.tensor.matmul, nc.tensor.transpose
            blk = [0]
            owed = []

            def mm(out, lhsT, rhs, start, stop, sem=None):
                o = mm_(out, lhsT, rhs, start=start, stop=stop)
                if sem is not None:
                    o.then_inc(sem, 1)
                elif owed:
                    o.then_inc(owed.pop(0), 1)
                return o

            def mm3(out, w, x, start, stop, sem=None):
                (wH, wL), (xH, xL) = w, x
                mm(out, wH, xH, start, False)
                mm(out, wH, xL, False, False)
                mm(out, wL, xH, False, stop, sem)

            def x_parts(*at):
                return xh[(slice(None),) + at], xl[(slice(None),) + at]

            def begin(l, job):
                n = l * USES[BANK[job]] + USE[job] - 1
                if n:
                    pe.wait_ge(bank_free[BANK[job]], n)

            def fullsem(job):
                return bank_full[BANK[job]]

            def whole_block():
                n = blk[0]
                blk[0] += 1
                assert not BLOCKS[n % NBLK][2]
                pe.wait_ge(landed[n % RAW], 16 * (n // RAW + 1))
                return raw[n % RAW][:, :]

            def split_block():
                n = blk[0]
                blk[0] += 1
                assert BLOCKS[n % NBLK][2]
                s = split_no(n)
                pe.wait_ge(lo_done, s + 1)
                return wh[s % SPLIT][:, :], wl[s % SPLIT][:, :]

            def transposes(l, job, pairs):
                begin(l, job)
                for n, src in enumerate(pairs):
                    o = tr_(pb(job)[:, n * P:(n + 1) * P], src, ident[:, :])
                o.then_inc(fullsem(job), 1)

            def rows_T(l, pre, src, name):
                for i in range(4):
                    begin(l, f"{pre}{i}")
                for t in range(NT):
                    T.need(l, "rows", ROWS[name] + t + 1)
                    for i in range(4):
                        for c in range(2):
                            k = 2 * i + c
                            o = tr_(pb2(f"{pre}{i}")[:, c, t * P:(t + 1) * P],
                                    src[:, t, k * P:(k + 1) * P], ident[:, :])
                            if t == NT - 1 and c:
                                o.then_inc(fullsem(f"{pre}{i}"), 1)
                            elif owed and owed[0] is whole_used:
                                o.then_inc(owed.pop(0), 1)

            def heads_T(l, pre, src):
                for i in range(2):
                    transposes(l, f"{pre}{i}", [src[:, t, c * P:(c + 1) * P]
                                                for c in (2 * i, 2 * i + 1) for t in range(NT)])

            def token_major(l, job, w=512, srcT=None, blocks=range(4), x_from=None):
                if blocks[0] == 0:
                    for t in range(NT):
                        begin(l, f"{job}{t}")
                for b in blocks:
                    if x_from:
                        T.took(l, f"{x_from}{b}")
                    ws = [whole_block()] if srcT is not None else split_block()
                    ws = [x.rearrange("p (k n) -> p k n", k=2) for x in ws]
                    for t in range(NT):
                        out = pb(f"{job}{t}")[:, 0:w]
                        for kk in range(2):
                            k = 2 * b + kk
                            end = k == KC - 1
                            signal = fullsem(f"{job}{t}") if end else None
                            rows = slice(t * P, (t + 1) * P)
                            if srcT is not None:
                                mm(out, srcT[:, k, rows], ws[0][:, kk, 0:w], k == 0, end, signal)
                            else:
                                mm3(out, x_parts(k, rows), [x[:, kk, 0:w] for x in ws], k == 0,
                                    end, signal)
                    owed.append(whole_used if srcT is not None else split_used)

            def columns_of(out, ws, signal=None, between={}):
                for k in range(KC):
                    if k in between:
                        between[k]()
                    mm3(out, [x[:, k * P:(k + 1) * P] for x in ws], x_parts(k, slice(0, SEQ)),
                        k == 0, k == KC - 1, signal if k == KC - 1 else None)

            def transposed(l, job, n=2, x_from=None):
                begin(l, job)
                made_x = {2 * i: lambda i=i: T.took(l, f"{x_from}{i}") for i in range(4) if x_from}
                for c in range(n):
                    columns_of(pb2(job)[:, c, :], split_block(), fullsem(job) if c == n - 1 else None,
                               {} if c else made_x)
                    owed.append(split_used)

            def half_rows(l, jobs, kc, ready):
                for job in jobs:
                    begin(l, job)
                for k in range(kc):
                    ready(k)
                    ws = split_block()
                    for n, job in enumerate(jobs):
                        t, h = n // 2, n % 2
                        end = k == kc - 1
                        mm3(pb(job)[:, :], x_parts(k, slice(t * P, (t + 1) * P)),
                            [x[:, h * 512:(h + 1) * 512] for x in ws], k == 0, end,
                            fullsem(job) if end else None)
                    owed.append(split_used)

            pe.wait_ge(consts, 5)
            pe.wait_ge(strip_in, 32)
            mm_(bank[0][0:NHB, 0:STRIP], relb[:, :], onehot, start=True,
                stop=True).then_inc(strip_mm, 1)
            pe.wait_ge(strip_sb_ready, 1)
            for l in range(DEPTH):
                rows_T(l, "nx", xn, "x")
                token_major(l, "cs", 2 * P + IH, x_from="nx")
                for i in range(2):
                    transposed(l, f"iq{i}")
                transposed(l, "ik", 1)
                token_major(l, "cq")
                T.took(l, "iq0")
                T.took(l, "iq1")
                T.took(l, "ik")
                for t in range(NT):
                    k = P * (t + 1)
                    per = 512 // k
                    for i in range(IH // per):
                        job = f"is{t}{i}"
                        begin(l, job)
                        for j in range(per):
                            h = index_head(per, i, j)
                            r = slice(64 * (h % 2), 64 * (h % 2) + 64)
                            mm(pb(job)[:, j * k:(j + 1) * k], iqT[r, h // 2, t * P:(t + 1) * P],
                               ikT[r, 0:k], True, True, fullsem(job) if j == per - 1 else None)
                token_major(l, "qa")
                token_major(l, "ka")
                T.took(l, "cs0")
                T.took(l, "cs1")
                transposes(l, "ckT", [ckn[:, t, :] for t in range(NT)])
                T.took(l, "cq1")
                T.took(l, "cq0")
                heads_T(l, "cqT", cqn)
                token_major(l, "va")
                token_major(l, "zv")
                for t in range(NT):
                    T.took(l, f"qa{t}")
                    T.took(l, f"ka{t}")
                heads_T(l, "qT", qan)
                heads_T(l, "kT", kan)
                for i in range(2):
                    transposed(l, f"zu{i}")
                for i in range(2):
                    T.took(l, f"qT{i}")
                    T.took(l, f"kT{i}")
                for h in range(AH):
                    for m in range(2):
                        job = f"al{h}{m}"
                        begin(l, job)
                        r = slice(64 * m, 64 * m + 64)
                        for t in range(NT):
                            k = P * (t + 1)
                            mm(pb(job)[:, t * P:t * P + k], qaT[r, h, t * P:(t + 1) * P],
                               kaT[r, h, 0:k], True, True, fullsem(job) if t else None)
                for i in range(7):
                    transposed(l, f"gt{i}")
                for h in range(AH):
                    T.need(l, "pd", 2 * h + 2)
                    transposes(l, f"pT{h}", [a_pd[h][:, 0, 0:P], a_pd[h][:, 1, 0:P],
                                             a_pd[h][:, 1, P:2 * P]])
                transposed(l, "gt7")
                T.took(l, "va0")
                T.took(l, "va1")
                for t in range(NT):
                    begin(l, f"ay{t}")
                for h in range(AH):
                    T.took(l, f"pT{h}")
                    vh = va[:, :, h * P:(h + 1) * P]
                    end = h == AH - 1
                    mm(pb("ay0")[:, h * P:(h + 1) * P], a_pT[h][:, 0, :], vh[:, 0, :], True, True,
                       fullsem("ay0") if end else None)
                    mm(pb("ay1")[:, h * P:(h + 1) * P], a_pT[h][:, 1, :], vh[:, 0, :], True, False)
                    mm(pb("ay1")[:, h * P:(h + 1) * P], a_pT[h][:, 2, :], vh[:, 1, :], False, True,
                       fullsem("ay1") if end else None)
                T.need(l, "vn", NT)
                T.need(l, "wmask", 1)
                for i in range(2):
                    job = f"sv{i}"
                    begin(l, job)
                    for j in range(2):
                        for c in range(NT):
                            g = 2 * i + j
                            mm(pb2(job)[:, j, c * P:(c + 1) * P], vg[:, c, g * P:(g + 1) * P],
                               p_("ws", g * P, (g + 1) * P), True, True,
                               fullsem(job) if j and c else None)
                T.took(l, "ckT")
                T.took(l, "cqT0")
                T.took(l, "cqT1")
                for job, t, hs in (("cl0", 0, range(4)), ("cl1", 1, range(2)),
                                   ("cl2", 1, range(2, 4))):
                    k = P * (t + 1)
                    begin(l, job)
                    for n, h in enumerate(hs):
                        mm(pb(job)[:, n * k:(n + 1) * k], cqT[:, h, t * P:(t + 1) * P],
                           ckT[:, 0:k], True, True, fullsem(job) if h == hs[-1] else None)
                for i in (8, 9, 10):
                    transposed(l, f"gt{i}")
                T.need(l, "c_p", 1)
                transposes(l, "ct0", [c_log[0][:, h, :] for h in range(CH)])
                T.need(l, "c_p", 2)
                for c in range(NT):
                    transposes(l, f"ct{c + 1}", [c_log[1][:, h, c * P:(c + 1) * P]
                                                 for h in range(CH)])
                transposed(l, "gt11")
                begin(l, "cy0")
                T.took(l, "ct0")
                mm(pb("cy0")[:, :], cv[:, 0, :], flat(c_pT[0]), True, True, fullsem("cy0"))
                begin(l, "cy1")
                for c in range(NT):
                    T.took(l, f"ct{c + 1}")
                    mm(pb("cy1")[:, :], cv[:, c, :], flat(c_pT[c + 1]), c == 0, c == 1,
                       fullsem("cy1") if c else None)
                T.took(l, "ay0")
                T.took(l, "ay1")
                heads_T(l, "yT", ya)
                T.need(l, "c_p", NT)
                rows_T(l, "mx", ms, "m")
                for i in range(4):
                    for b in "bca":
                        job = f"m{b}{i}"
                        begin(l, job)
                        whole = b == "c"
                        ws = [whole_block()] if whole else split_block()
                        ws = [x.rearrange("p (c k n) -> p c k n", c=2, k=4) for x in ws]
                        if i == 0:
                            if whole:
                                T.took(l, "cy0")
                                T.took(l, "cy1")
                            else:
                                T.need(l, "y_lo", 4 if b == "a" else 2)
                        for c in range(2):
                            for k in range(4):
                                signal = fullsem(job) if c and k == 3 else None
                                if whole:
                                    mm(pb2(job)[:, c, :], ws[0][:, c, k, :], ycT[:, k, :], k == 0,
                                       k == 3, signal)
                                else:
                                    mm3(pb2(job)[:, c, :], [x[:, c, k, :] for x in ws],
                                        x_parts(k + 4 * (b == "b"), slice(0, SEQ)), k == 0, k == 3,
                                        signal)
                        owed.append(whole_used if whole else split_used)
                half_rows(l, [f"o{i}" for i in range(4)], KC,
                          lambda k: T.need(l, "merged_lo", k // 2 + 1))
                for i in range(4):
                    T.took(l, f"mx{i}")
                token_major(l, "mk", srcT=msT)
                rows_T(l, "ny", xn, "y")
                token_major(l, "mq", x_from="ny")
                T.took(l, "mk0")
                T.took(l, "mk1")
                heads_T(l, "mkT", mkn)
                token_major(l, "mv", srcT=msT, blocks=(0, 1))
                T.took(l, "mq0")
                T.took(l, "mq1")
                heads_T(l, "mqT", mqn)
                for i in range(2):
                    T.took(l, f"mqT{i}")
                    T.took(l, f"mkT{i}")
                for t in range(NT):
                    for i in range(2):
                        job = f"ml{t}{i}"
                        begin(l, job)
                        for j in range(2):
                            h = 2 * i + j
                            mm(pb2(job)[:, j, :], mqT[:, h, t * P:(t + 1) * P], mkT[:, h, :],
                               True, True, fullsem(job) if j else None)
                token_major(l, "mv", srcT=msT, blocks=(2, 3))
                for t in range(NT):
                    T.need(l, "m_p", t + 1)
                    for k in range(NT):
                        transposes(l, f"mp{t}{k}", [m_e[t][:, h, k * P:(k + 1) * P]
                                                    for h in range(MH)])
                for t in range(NT):
                    T.took(l, f"mv{t}")
                    for k in range(NT):
                        T.took(l, f"mp{t}{k}")
                for i in range(2):
                    begin(l, f"mo{i}")
                    for j in range(2):
                        h = 2 * i + j
                        for k in range(NT):
                            mm(pb2(f"mo{i}")[:, j, :], mv[:, k, h * P:(h + 1) * P], m_pT[:, k, h, :],
                               k == 0, k == 1, fullsem(f"mo{i}") if j and k else None)
                half_rows(l, [f"w{i}" for i in range(4)], 4, lambda k: T.took(l, f"mo{k // 2}"))
                rows_T(l, "nz", xn, "z")
                for i in range(8):
                    transposed(l, f"pq{i}", x_from=None if i else "nz")
                for i in range(8):
                    T.took(l, f"pq{i}")
                for t in range(NT):
                    for i in range(4):
                        job = f"ps{t}{i}"
                        begin(l, job)
                        for j in range(4):
                            c = 4 * i + j
                            mm(pb4(job)[:, j, :], pqT[:, c, t * P:(t + 1) * P],
                               p_("sk", (c % 2) * NKEY, (c % 2 + 1) * NKEY), True, True,
                               fullsem(job) if j == 3 else None)
                for b in range(8):
                    pe.wait_ge(bank_free[b], l * USES[b] + BEFORE_LOOPS[b])
                uv = split_no(l * NBLK + FIRST["uv"])
                assert split_no(blk[0]) == uv and not owed

                def expert_block(i, k):
                    s = uv + k
                    pe.wait_ge(lo_done, i * TURN + (s + 1))
                    return wh[s % SPLIT][:, :], wl[s % SPLIT][:, :]

                def up(i, c, between={}):
                    ws = expert_block(i, c + HALF * (c // HALF))
                    pe.wait_ge(a_done, i * TURN + (l * NKEY + c + 1))
                    columns_of(bank[4 + c % 2][:, 0:SEQ], ws, a_full, between)
                    owed.append(split_used)

                def gate_set(i, half, s, per):
                    at = i * per + ((2 * l + half) * 64 + s + 1)
                    pe.wait_ge(oh_ready, at)
                    pe.wait_ge(g_free, at)
                    for q in range(4):
                        for g in range(3):
                            mm(bank[6 + s % 2][:, q * HALF:(q + 1) * HALF], oh1[s % 2][:, :, q],
                               oh2[s % 2][:, g, :, q], g == 0, g == 2,
                               g_full if q == 3 and g == 2 else None)

                def up_gates(half):
                    c, s = (R3, 0) if half == 0 else (HALF, 0)
                    for n, per in GATE_STEPS[half]:
                        repeat(pe, n, TURN, lambda i, j: up(i, c + j, {
                            KC * (q + 1) // (per + 1): lambda q=q: gate_set(
                                i, half, s + per * j + q, TURN * per) for q in range(per)}))
                        c, s = c + n, s + n * per

                def down(i, c, start=False, stop=False, tile_done=None):
                    vH, vL = expert_block(i, c + HALF * (c // HALF + 1))
                    pe.wait_ge(h_ready, i * TURN + (l * NKEY + c + 3))
                    for m in range(4):
                        t, h = m // 2, m % 2
                        rows, cols = slice(t * P, (t + 1) * P), slice(h * 512, (h + 1) * 512)
                        mm3(bank[m][:, :], (hh[c % 2][:, rows], hl[c % 2][:, rows]),
                            (vH[:, cols], vL[:, cols]), start, stop,
                            y_full if m == 3 else tile_done if m == 1 else None)
                    owed.append(split_used)

                up(0, 0)
                repeat(pe, R1 - 1, TURN, lambda i, j: up(i, 1 + j))
                for c in range(R1, R2):
                    up(0, c)
                T.need(l, "route", NT)
                transposes(l, "eT", [etok[:, part, t, :] for part in range(2) for t in range(NT)])
                transposes(l, "gT", [gate[:, t, :] for t in range(NT)])
                for c in range(R2, R3):
                    up(0, c)
                up_gates(0)
                pe.wait_ge(bank_free[0], (l + 1) * USES[0])
                pe.wait_ge(bank_free[1], (l + 1) * USES[1])
                down(0, 0, start=True)
                repeat(pe, HALF - 1, TURN, lambda i, j: down(i, 1 + j))
                up_gates(1)
                repeat(pe, HALF - 1, TURN, lambda i, j: down(i, HALF + j))
                down(0, NKEY - 1, stop=True, tile_done=S["y_tile"])
                blk[0] = (l + 1) * NBLK
        for (l, name), n in made.items():
            assert n == PER_LAYER[name], (l, name, n)


def strip_selector():
    import numpy as np
    n = 255 - np.arange(STRIP)
    exact = BUCKETS // 2
    nf = np.maximum(n, 1).astype(np.float32)
    large = exact + (np.log(nf / exact) / math.log(MAXDIST / exact)
                     * (BUCKETS - exact)).astype(np.int32)
    b = np.where(n < exact, np.maximum(n, 0), np.minimum(large, BUCKETS - 1))
    out = np.zeros((64, STRIP), np.float32)
    out[b, np.arange(STRIP)] = 1.0
    out[BUCKETS, n < 0] = MASK
    return out


def kernel(**inputs):
    import numpy as np
    import concourse.bacc as bacc
    from concourse.bass_utils import run_bass_kernel_spmd

    a = {k: np.asarray(v) for k, v in inputs.items()}

    def token_major(w):
        return w.reshape(4, 2, P, 512).transpose(0, 2, 1, 3).reshape(4, P, 1024)

    def columns(w):
        n = w.shape[1] // P
        return w.reshape(KC, P, n, P).transpose(2, 1, 0, 3).reshape(n, P, 1024)

    def rows(w):
        return w.reshape(-1, P, 1024)

    def branch(w):
        return w.reshape(4, P, 4, 2, P).transpose(2, 1, 3, 0, 4).reshape(4, P, 1024)

    def cols(w):
        return w.reshape(-1, P).T

    blocks = np.empty((DEPTH * NBLK, P, 1024), np.float32)
    par = np.empty((DEPTH, P, NPAR), np.float32)
    widths = [512] * 6 + [CD, CD, IH * ID, ID, IH, 3 * D]
    for l in range(DEPTH):
        qa, ka, va, zu, zv, cq, ck, cv, iq, ik, iw, gts = np.split(
            a["w_in"][l], np.cumsum(widths)[:-1], axis=1)
        u = a["p_u"][l].reshape(NKEY, NKEY, KC, P).transpose(1, 3, 2, 0).reshape(NKEY, P, 1024)
        v = a["p_v"][l].reshape(NKEY, NKEY, D).transpose(1, 0, 2)
        kv = a["m_wkv"][l]
        small = np.concatenate([ck, cv, iw, np.zeros((D, 512 - 2 * CD - IH), np.float32)], 1)
        br = [branch(a[f"w_br_{c}"][l]) for c in "abc"]
        parts = dict(
            cs=token_major(small), iq=columns(iq), ik=columns(np.concatenate([ik, ik], 1)),
            cq=token_major(cq), qa=token_major(qa), ka=token_major(ka), va=token_major(va),
            zv=token_major(zv), zu=columns(zu), gts=columns(gts),
            mk=token_major(kv[:, :512]), mv=token_major(kv[:, 512:]),
            **{f"br_{b}{i}": w[i:i + 1] for b, w in zip("abc", br) for i in range(4)},
            mix_out=rows(a["w_mix_out"][l]),
            mq=token_major(a["m_wq"][l]), mo=rows(a["m_wo"][l]), pq=columns(a["p_wq"][l]))
        at = l * NBLK
        for name, n, _ in STREAM[:-1]:
            assert parts[name].shape[0] == n
            blocks[at:at + n] = parts[name]
            at += n
        for half in range(2):
            for w in (u, v):
                blocks[at:at + HALF] = w[half * HALF:(half + 1) * HALF]
                at += HALF
        everywhere = lambda w: np.broadcast_to(w.reshape(1, -1), (P, w.size))
        small = dict(
            g_mix=cols(a["norm_mix"][l]), g_mem=cols(a["norm_mem"][l]),
            g_src=cols(a["norm_memsrc"][l]), g_peer=cols(a["norm_peer"][l]),
            aq=cols(np.tile(a["a_q_gain"][l], 2)), ak=cols(np.tile(a["a_k_gain"][l], 2)),
            cq=cols(a["c_q_gain"][l]), ck=cols(a["c_k_gain"][l]), mq=cols(a["m_q_gain"][l]),
            mk=cols(a["m_k_gain"][l]), asub=cols(a["a_subln_gain"][l]), bv=cols(a["b_v_gain"][l]),
            ws=a["b_w_s"][l].transpose(2, 0, 1).reshape(P, BG * P),
            bs=everywhere(a["b_b_s"][l]),
            lam=everywhere(np.concatenate([a[k][l] for k in ("a_lq1", "a_lk1", "a_lq2", "a_lk2")])),
            sk=np.concatenate([a["p_subkey1"][l].T, a["p_subkey2"][l].T], 1))
        for name, (lo, hi) in PAR.items():
            par[l, :, lo:hi] = small[name]

    nc = bacc.Bacc("TRN2", target_bir_lowering=False, num_devices=1)
    arrays = dict(x=a["x"].reshape(SEQ, D), mem=a["mem"].reshape(SEQ, D), rel_bias=a["rel_bias"],
                  selector=strip_selector(), par=par, blocks=blocks)
    args = [nc.dram_tensor(n, w.shape, F32, kind="ExternalInput").ap() for n, w in arrays.items()]
    out = nc.dram_tensor("out", (SEQ, D), F32, kind="ExternalOutput").ap()
    strip = nc.dram_tensor("strip", (NHB, P, STRIP), F32).ap()
    build(nc, *args, out, strip)
    r = run_bass_kernel_spmd(nc, [{n: np.ascontiguousarray(w) for n, w in arrays.items()}],
                             core_ids=[0])
    return np.asarray(r.results[0]["out"]).reshape(1, SEQ, D)
```
